# Optimizing a Trainium2 kernel written in Bass

```python
import jax, jax.numpy as jnp
from jax import lax
import numpy as np

D_MODEL = 1024
BATCH = 1
SEQ = 512
DEPTH = 1

MLA_HEADS = 8
MLA_NOPE = 64
MLA_ROPE = 32
MLA_QK = MLA_NOPE + MLA_ROPE
MLA_V = 64
Q_LORA = 256
KV_LORA = 128
ROPE_THETA = 10000.0
Q_BLOCK = 128
RWKV_HEADS = 8
RWKV_HEAD = 64
RWKV_WIDTH = RWKV_HEADS * RWKV_HEAD
DECAY_LORA = 64
AAA_LORA = 64
GATE_LORA = 128
RWKV_SLAB = 3 * RWKV_WIDTH + DECAY_LORA + AAA_LORA + GATE_LORA
GN_EPS = 64e-5
IN_SIZES = (Q_LORA, KV_LORA, MLA_ROPE, RWKV_SLAB, D_MODEL, D_MODEL)
D_IN = sum(IN_SIZES)
N_EXPERTS = 32
TOP_K = 4
D_FF = D_MODEL
SWIGLU_LIMIT = 7.0
SWIGLU_ALPHA = 1.702
EXPERT_BLOCK = 128
NORM_EPS = 1e-6

kernel_name = 'hybrid_mla_rwkv7_moe_adaln'

def _split(x, sizes):
    return jnp.split(x, np.cumsum(sizes)[:-1].tolist(), axis=-1)

def rms_norm(x, w):
    xf = x.astype(jnp.float32)
    y = xf * lax.rsqrt(jnp.mean(xf * xf, axis=-1, keepdims=True) + NORM_EPS)
    return (y * w.astype(jnp.float32)).astype(x.dtype)

def modulate(x, norm_w, shift, scale):
    return rms_norm(x, norm_w) * (1.0 + scale[:, None, :]) + shift[:, None, :]

def apply_rope(x, positions):
    half = x.shape[-1] // 2
    inv_freq = ROPE_THETA ** (-jnp.arange(half, dtype=jnp.float32) / half)
    ang = positions.astype(jnp.float32)[:, :, None] * inv_freq
    cos = jnp.cos(ang)[:, :, None, :]
    sin = jnp.sin(ang)[:, :, None, :]
    xf = x.astype(jnp.float32)
    x1, x2 = xf[..., :half], xf[..., half:]
    return jnp.concatenate([x1 * cos - x2 * sin, x2 * cos + x1 * sin], axis=-1).astype(x.dtype)

def causal_attention(q, k, v):
    B, S, H, Dq = q.shape
    scale = Dq ** -0.5
    outs = []
    for i in range(S // Q_BLOCK):
        lo, hi = i * Q_BLOCK, (i + 1) * Q_BLOCK
        s = jnp.einsum('bqhd,bkhd->bhqk', q[:, lo:hi], k[:, :hi],
                       preferred_element_type=jnp.float32) * scale
        q_pos = lo + jnp.arange(Q_BLOCK)
        k_pos = jnp.arange(hi)
        s = jnp.where(k_pos[None, :] <= q_pos[:, None], s, -jnp.inf)
        p = jax.nn.softmax(s, axis=-1).astype(v.dtype)
        outs.append(jnp.einsum('bhqk,bkhd->bqhd', p, v[:, :hi]))
    return jnp.concatenate(outs, axis=1)

def mla_branch(c_q, c_kv, k_rope, positions, q_a_norm_w, w_q_up, kv_a_norm_w, w_kv_up,
               q_norm_w, k_norm_w, w_o_mla):
    B, S, _ = c_q.shape
    q = (rms_norm(c_q, q_a_norm_w) @ w_q_up).reshape(B, S, MLA_HEADS, MLA_QK)
    kv = (rms_norm(c_kv, kv_a_norm_w) @ w_kv_up).reshape(B, S, MLA_HEADS, MLA_NOPE + MLA_V)
    k_nope, v = kv[..., :MLA_NOPE], kv[..., MLA_NOPE:]
    k_rope = jnp.broadcast_to(k_rope[:, :, None, :], (B, S, MLA_HEADS, MLA_ROPE)).astype(k_nope.dtype)
    k = jnp.concatenate([k_nope, k_rope], axis=-1)
    q = rms_norm(q, q_norm_w)
    k = rms_norm(k, k_norm_w)
    q = jnp.concatenate([q[..., :MLA_NOPE], apply_rope(q[..., MLA_NOPE:], positions)], axis=-1)
    k = jnp.concatenate([k[..., :MLA_NOPE], apply_rope(k[..., MLA_NOPE:], positions)], axis=-1)
    o = causal_attention(q, k, v)
    return o.reshape(B, S, MLA_HEADS * MLA_V) @ w_o_mla

def wkv7_scan(r, decay, k, v, a_vec, b_vec):
    B, S, H, N = r.shape

    def step(state, inp):
        r_t, w_t, k_t, v_t, a_t, b_t = inp
        sa = jnp.einsum('bhvk,bhk->bhv', state, a_t)
        state = (state * w_t[:, :, None, :] + sa[..., None] * b_t[:, :, None, :]
                 + v_t[..., None] * k_t[:, :, None, :])
        y = jnp.einsum('bhvk,bhk->bhv', state, r_t)
        return state, y

    xs = tuple(jnp.moveaxis(t.astype(jnp.float32), 1, 0) for t in (r, decay, k, v, a_vec, b_vec))
    s0 = jnp.zeros((B, H, N, N), jnp.float32)
    _, ys = lax.scan(step, s0, xs)
    return jnp.moveaxis(ys, 0, 1)

def rwkv7_branch(slab, rwkv_mu, w0, w2, a0, a2, g2, k_k, k_a, r_k, ln_w, ln_b, w_o):
    B, S, _ = slab.shape
    p = slab.astype(jnp.float32)
    prev = jnp.pad(p[:, :-1], ((0, 0), (1, 0), (0, 0)))
    p = p + (prev - p) * rwkv_mu
    r, k, v, w_lo, a_lo, g_lo = _split(
        p, (RWKV_WIDTH, RWKV_WIDTH, RWKV_WIDTH, DECAY_LORA, AAA_LORA, GATE_LORA))
    log_w = -jax.nn.softplus(-(w0 + jnp.tanh(w_lo) @ w2)) - 0.5
    decay = jnp.exp(-jnp.exp(log_w.astype(jnp.float32)))
    a = jax.nn.sigmoid(a0 + a_lo @ a2)
    g = jax.nn.sigmoid(g_lo) @ g2

    def heads(t):
        return t.reshape(B, S, RWKV_HEADS, RWKV_HEAD).astype(jnp.float32)

    kk = heads(k * k_k)
    kk = kk / jnp.maximum(jnp.sqrt(jnp.sum(kk * kk, axis=-1, keepdims=True)), 1e-12)
    k = k * (1.0 + (a - 1.0) * k_a)
    rh, kh, vh, ah = heads(r), heads(k), heads(v), heads(a)
    y = wkv7_scan(rh, heads(decay), kh, vh, -kk, kk * ah)
    mu = jnp.mean(y, axis=-1, keepdims=True)
    var = jnp.mean(jnp.square(y - mu), axis=-1, keepdims=True)
    y = ((y - mu) * lax.rsqrt(var + GN_EPS)).reshape(B, S, RWKV_WIDTH) * ln_w + ln_b
    bonus = jnp.sum(rh * kh * r_k, axis=-1, keepdims=True) * vh
    y = (y + bonus.reshape(B, S, RWKV_WIDTH)) * g
    return y @ w_o

def hybrid_mixer(h, positions, w_in, q_a_norm_w, w_q_up, kv_a_norm_w, w_kv_up, q_norm_w, k_norm_w,
                 w_o_mla, rwkv_mu, rwkv_w0, rwkv_w2, rwkv_a0, rwkv_a2, rwkv_g2, rwkv_k_k, rwkv_k_a,
                 rwkv_r_k, rwkv_ln_w, rwkv_ln_b, rwkv_w_o, w_out):
    c_q, c_kv, k_rope, slab, gate_a, gate_b = _split(h @ w_in, IN_SIZES)
    o_a = mla_branch(c_q, c_kv, k_rope, positions, q_a_norm_w, w_q_up, kv_a_norm_w, w_kv_up,
                     q_norm_w, k_norm_w, w_o_mla)
    o_b = rwkv7_branch(slab, rwkv_mu, rwkv_w0, rwkv_w2, rwkv_a0, rwkv_a2, rwkv_g2, rwkv_k_k,
                       rwkv_k_a, rwkv_r_k, rwkv_ln_w, rwkv_ln_b, rwkv_w_o)
    merged = (jax.nn.sigmoid(gate_a.astype(jnp.float32)) * o_a.astype(jnp.float32)
              + jax.nn.sigmoid(gate_b.astype(jnp.float32)) * o_b.astype(jnp.float32))
    return merged.astype(h.dtype) @ w_out

def moe_ffn(h, w_router, b_router, w_gate_up, b_gate_up, w_down, b_down):
    B, S, D = h.shape
    T = B * S
    n_assign = T * TOP_K
    hf = h.reshape(T, D)
    logits = jnp.dot(hf, w_router, preferred_element_type=jnp.float32) + b_router.astype(jnp.float32)
    top_v, top_e = lax.top_k(logits, TOP_K)
    top_w = jax.nn.softmax(top_v, axis=-1)
    flat_e = top_e.reshape(-1)
    flat_tok = jnp.arange(n_assign, dtype=jnp.int32) // TOP_K
    order = jnp.argsort(flat_e)
    sorted_e = flat_e[order]
    counts = jnp.bincount(flat_e, length=N_EXPERTS)
    padded = (counts + EXPERT_BLOCK - 1) // EXPERT_BLOCK * EXPERT_BLOCK
    pad_end = jnp.cumsum(padded)
    pad_start = pad_end - padded
    start = jnp.cumsum(counts) - counts
    dest = pad_start[sorted_e] + jnp.arange(n_assign) - start[sorted_e]
    n_rows = n_assign + N_EXPERTS * EXPERT_BLOCK
    n_blocks = n_rows // EXPERT_BLOCK
    row_tok = jnp.zeros((n_rows,), jnp.int32).at[dest].set(flat_tok[order])
    row_w = jnp.zeros((n_rows,), jnp.float32).at[dest].set(top_w.reshape(-1)[order])
    blk_e = jnp.minimum(jnp.searchsorted(pad_end, jnp.arange(n_blocks) * EXPERT_BLOCK, side='right'),
                        N_EXPERTS - 1)
    xs = hf[row_tok].reshape(n_blocks, EXPERT_BLOCK, D)

    def expert_block(args):
        xb, e = args
        gu = xb @ w_gate_up[e] + b_gate_up[e]
        gate = jnp.minimum(gu[:, 0::2], SWIGLU_LIMIT)
        up = jnp.clip(gu[:, 1::2], -SWIGLU_LIMIT, SWIGLU_LIMIT)
        act = (up + 1.0) * gate * jax.nn.sigmoid(SWIGLU_ALPHA * gate)
        return act @ w_down[e] + b_down[e]

    ys = lax.map(expert_block, (xs, blk_e)).reshape(n_rows, D)
    out = jnp.zeros((T, D), jnp.float32).at[row_tok].add(ys.astype(jnp.float32) * row_w[:, None])
    return out.reshape(B, S, D).astype(h.dtype)

def setup_inputs(seed: int = 0) -> dict:
    key = jax.random.key(seed)
    ks = iter(jax.random.split(key, 40))
    L, D = DEPTH, D_MODEL

    def nrm(shape, scale):
        return jax.random.normal(next(ks), shape, jnp.float32) * scale

    def gain(shape):
        return 1.0 + nrm(shape, 0.05)

    x = nrm((BATCH, SEQ, D), 1.0)
    c = nrm((BATCH, D), 1.0)
    offsets = jax.random.randint(next(ks), (BATCH, 1), 0, 1024, dtype=jnp.int32)
    positions = offsets + jnp.arange(SEQ, dtype=jnp.int32)[None, :]
    return dict(
        x=x, c=c, positions=positions,
        ada_w=nrm((L, D, 6 * D), 0.5 * D ** -0.5), ada_b=nrm((L, 6 * D), 0.1),
        norm_mix_w=gain((L, D)), norm_ffn_w=gain((L, D)),
        w_in=nrm((L, D, D_IN), D ** -0.5),
        q_a_norm_w=gain((L, Q_LORA)),
        w_q_up=nrm((L, Q_LORA, MLA_HEADS * MLA_QK), Q_LORA ** -0.5),
        kv_a_norm_w=gain((L, KV_LORA)),
        w_kv_up=nrm((L, KV_LORA, MLA_HEADS * (MLA_NOPE + MLA_V)), KV_LORA ** -0.5),
        q_norm_w=gain((L, MLA_QK)), k_norm_w=gain((L, MLA_QK)),
        w_o_mla=nrm((L, MLA_HEADS * MLA_V, D), (MLA_HEADS * MLA_V) ** -0.5),
        rwkv_mu=jax.random.uniform(next(ks), (L, RWKV_SLAB), jnp.float32, 0.0, 1.0),
        rwkv_w0=jax.random.uniform(next(ks), (L, RWKV_WIDTH), jnp.float32, -6.0, 1.0),
        rwkv_w2=nrm((L, DECAY_LORA, RWKV_WIDTH), 0.5 * DECAY_LORA ** -0.5),
        rwkv_a0=nrm((L, RWKV_WIDTH), 0.5),
        rwkv_a2=nrm((L, AAA_LORA, RWKV_WIDTH), 0.5 * AAA_LORA ** -0.5),
        rwkv_g2=nrm((L, GATE_LORA, RWKV_WIDTH), GATE_LORA ** -0.5),
        rwkv_k_k=0.85 + nrm((L, RWKV_WIDTH), 0.05),
        rwkv_k_a=1.0 + nrm((L, RWKV_WIDTH), 0.05),
        rwkv_r_k=nrm((L, RWKV_HEADS, RWKV_HEAD), 0.1),
        rwkv_ln_w=gain((L, RWKV_WIDTH)), rwkv_ln_b=nrm((L, RWKV_WIDTH), 0.02),
        rwkv_w_o=nrm((L, RWKV_WIDTH, D), RWKV_WIDTH ** -0.5),
        w_out=nrm((L, D, D), D ** -0.5),
        w_router=nrm((L, D, N_EXPERTS), D ** -0.5), b_router=nrm((L, N_EXPERTS), 0.01),
        w_gate_up=nrm((L, N_EXPERTS, D, 2 * D_FF), D ** -0.5),
        b_gate_up=nrm((L, N_EXPERTS, 2 * D_FF), 0.01),
        w_down=nrm((L, N_EXPERTS, D_FF, D), D_FF ** -0.5),
        b_down=nrm((L, N_EXPERTS, D), 0.01),
    )

def reference(x, c, positions, ada_w, ada_b, norm_mix_w, norm_ffn_w, w_in, q_a_norm_w, w_q_up,
              kv_a_norm_w, w_kv_up, q_norm_w, k_norm_w, w_o_mla, rwkv_mu, rwkv_w0, rwkv_w2,
              rwkv_a0, rwkv_a2, rwkv_g2, rwkv_k_k, rwkv_k_a, rwkv_r_k, rwkv_ln_w, rwkv_ln_b,
              rwkv_w_o, w_out, w_router, b_router, w_gate_up, b_gate_up, w_down, b_down):
    cond = jax.nn.silu(c)
    for l in range(DEPTH):
        mod = cond @ ada_w[l] + ada_b[l]
        shift1, scale1, gate1, shift2, scale2, gate2 = jnp.split(mod, 6, axis=-1)
        h = modulate(x, norm_mix_w[l], shift1, scale1)
        mix = hybrid_mixer(h, positions, w_in[l], q_a_norm_w[l], w_q_up[l], kv_a_norm_w[l],
                           w_kv_up[l], q_norm_w[l], k_norm_w[l], w_o_mla[l], rwkv_mu[l],
                           rwkv_w0[l], rwkv_w2[l], rwkv_a0[l], rwkv_a2[l], rwkv_g2[l], rwkv_k_k[l],
                           rwkv_k_a[l], rwkv_r_k[l], rwkv_ln_w[l], rwkv_ln_b[l], rwkv_w_o[l], w_out[l])
        x = x + (gate1[:, None, :] * mix).astype(x.dtype)
        h = modulate(x, norm_ffn_w[l], shift2, scale2)
        ffn = moe_ffn(h, w_router[l], b_router[l], w_gate_up[l], b_gate_up[l], w_down[l], b_down[l])
        x = x + (gate2[:, None, :] * ffn).astype(x.dtype)
    return x


_drawn_inputs = setup_inputs


def setup_inputs(seed=0):
    import zlib

    import numpy as np

    out = dict(_drawn_inputs(seed))
    spreads = {}
    factors = {'norm_mix_w': 3.733,
     'q_a_norm_w': 8.0,
     'kv_a_norm_w': 8.0,
     'q_norm_w': 8.0,
     'k_norm_w': 8.0,
     'rwkv_w2': 6.205,
     'rwkv_k_k': 34.92,
     'rwkv_k_a': 4.432,
     'rwkv_ln_w': 45.52,
     'rwkv_ln_b': 64.0,
     'b_router': 36.584,
     'b_gate_up': 64.0,
     'b_down': 200.0,
     'norm_ffn_w': 8.0}
    for name, (base, spread) in spreads.items():
        noise = np.random.default_rng([zlib.crc32(name.encode()), seed]).standard_normal(out[name].shape)
        drawn = base * np.exp(spread * noise) if base else spread * noise
        out[name] = __import__('jax').numpy.asarray(drawn.astype(out[name].dtype))
    for name, factor in factors.items():
        out[name] = (out[name] * factor).astype(out[name].dtype)
    return out
```

```python
from contextlib import ExitStack

import concourse.bass as bass
from concourse import mybir

F32 = mybir.dt.float32
F32R = mybir.dt.float32r
I32 = mybir.dt.int32
U32 = mybir.dt.uint32
ALU = mybir.AluOpType
ACT = mybir.ActivationFunctionType
AX_X = mybir.AxisListType.X

P = 128
SEQ, D = 512, 1024
NT, KD = SEQ // P, D // P
HEADS, NOPE, ROPE, DV = 8, 64, 32, 64
QK = NOPE + ROPE
HALF = ROPE // 2
Q_LORA, KV_LORA = 256, 128
WIDTH = 512
FT = WIDTH // P
MLA_IN = Q_LORA + KV_LORA + ROPE
SLAB = 3 * WIDTH + 256
GATES = MLA_IN + SLAB
NMU = SLAB // P
CH = 64
NCH = SEQ // CH
N_EXP, TOP_K, D_FF = 32, 4, 1024
NORM_EPS, GN_EPS = 1e-6, 64e-5
DECAY = -0.6065306597126334
LIMIT, ALPHA = 7.0, 1.702
TWO_PI, PI_BELOW, ROUND = 6.283185307179586, 3.1415925, 12582912.0
TURN_PARTS = (6.28125, 0.0019340515136718750, 6.283185307179586 - 6.28125 - 0.0019340515136718750)
JOBS = 64
RING = 3

ROWS = {}
_n = 0
for _name, _k in (("c", 8), ("norm_mix_w", 8), ("q_a_norm_w", 2), ("kv_a_norm_w", 1), ("mu", NMU), ("w0", 4),
                  ("a0", 4), ("k_k", 4), ("k_a", 4), ("r_k", 4), ("ln_w", 4), ("ln_b", 4)):
    ROWS[_name] = (_n, _k)
    _n += _k
N_ROWS = _n


class Steps:

    def __init__(self, sem, names):
        self.sem, self.value, self.count = sem, {n: i + 1 for i, n in enumerate(names)}, 0
        assert len(self.value) == len(names)

    def __call__(self, name):
        self.count += 1
        assert self.value[name] == self.count, (name, self.value[name], self.count)
        return self.sem, 1

    def at(self, name):
        return self.sem, self.value[name]


def names(fmt, n):
    return [fmt.format(i) for i in range(n)]


class Space:

    def __init__(self, nc, ctx, a):
        self.nc, self.ctx, self.a = nc, ctx, a

    def sb(self, ctx, **shapes):
        return [ctx.enter_context(self.nc.sbuf_tensor(f"sb_{name}", shape, dt)) for name, (shape, dt) in shapes.items()]

    def sem(self, ctx, name):
        return ctx.enter_context(self.nc.semaphore(name))

    def steps(self, ctx, name, order):
        return Steps(self.sem(ctx, name), order)

    def col(self, name, i=0):
        return self.cols[:, ROWS[name][0] + i:ROWS[name][0] + i + 1]


def ring_chunks(a):
    def rows(w, lo, hi):
        return w[0, :, lo:hi].rearrange("(k p) n -> p k n", p=P)

    slab = MLA_IN
    chunks = [rows(a["ada_w"], 512 * j, 512 * j + 512) for j in range(12)]
    chunks += [rows(a["w_in"], slab + 3 * WIDTH, slab + SLAB)]
    chunks += [rows(a["w_in"], slab + 512 * j, slab + 512 * j + 512) for j in range(3)]
    chunks += [rows(a["w_in"], 0, MLA_IN)]
    chunks += [rows(a["w_in"], GATES + 512 * j, GATES + 512 * j + 512) for j in range(2)]
    chunks += [rows(a["w_o_mla"], 0, D)]
    chunks += [rows(a["w_in"], GATES + D + 512 * j, GATES + D + 512 * j + 512) for j in range(2)]
    chunks += [rows(a["rwkv_w_o"], 0, D)]
    chunks += [rows(a["w_out"], 512 * j, 512 * j + 512) for j in range(2)]
    return chunks


ADA0, LO, RKV, MLA, GA, OA, GB, OB, WOUT, N_CHUNKS = 0, 12, 13, 16, 17, 19, 20, 22, 23, 25


def slot(g, i):
    k, n = g.chunks[i].shape[1:]
    return g.ring[:, i % RING, 0:k * n].rearrange("p (k n) -> p k n", k=k)


def load_chunk(g, eng, i):
    eng.dma_start(slot(g, i), g.chunks[i]).then_inc(g.ring_in[i % RING], 16)


def chunk_loaded(g, i):
    return g.ring_in[i % RING], 16 * (i // RING + 1)


def phase_adaln(nc, g):
    a = g.a
    with ExitStack() as ctx:
        (g.stage, g.cond, g.sig, g.condrep, g.ada_b_row, g.mod1, g.ffn_w_row, g.xn, g.junk, g.ss, g.rstd, g.mod1_cols, g.gain) = g.sb(ctx, stage=([N_ROWS, P], F32), cond=([P, KD], F32), sig=([P, KD], F32),
             condrep=([P, KD, P], F32), ada_b_row=([1, 6 * D], F32), mod1=([P, 4, 512], F32), ffn_w_row=([P, D], F32),
             xn=([P, NT, D], F32), junk=([P, D], F32), ss=([P, NT], F32), rstd=([P, NT], F32), mod1_cols=([P, 2 * KD], F32),
             gain=([P, KD], F32))
        rows_in, row_in, x_in = (g.sem(ctx, n) for n in ("rows_in", "ada_row_in", "x_in"))
        pool_s = g.steps(ctx, "a_consts", names("c{}", N_CONSTS))
        vec = g.steps(ctx, "a_vec", ["cols", "cond"] + names("rep{}", KD) + ["rstd"] + names("xn{}", NT) + names("mcol{}", 4)
                      + ["gain"] + names("h{}", KD) + ["g2"])
        act = g.steps(ctx, "a_act", ["sig"] + names("mod{}", 4) + names("sq{}", NT) + ["std"] + names("mod{}", 12)[4:])
        pe = g.steps(ctx, "a_pe", ["rows"] + names("ada{}", 4) + names("mcol{}", 4) + ["ada4"] + names("h{}", KD) + names("ada{}", 12)[5:])
        ps = g.ps
        block = ctx.enter_context(nc.Block())
        n_rows = 0

        @block.sync
        def _(sp):
            flat = {"c": a["c"], "mu": a["rwkv_mu"], "r_k": a["rwkv_r_k"][0].rearrange("h n -> (h n)").unsqueeze(0)}
            for name, (at, k) in ROWS.items():
                src = flat.get(name)
                if src is None:
                    src = a[name if name in a else "rwkv_" + name]
                sp.dma_start(g.stage[at:at + k, :], src.rearrange("a (k p) -> (a k) p", p=P)).then_inc(rows_in, 16)
            load_chunk(g, sp, 0)
            sp.dma_start(g.ada_b_row[:, :], a["ada_b"]).then_inc(row_in, 16)
            load_chunk(g, sp, 1)
            sp.dma_start(g.x[:, :, :], a["x"][0].rearrange("(t p) d -> p t d", p=P)).then_inc(x_in, 16)
            load_chunk(g, sp, 2)
            for i in range(RING, 12 + RING):
                sp.wait_ge(*pe.at(f"ada{i - RING}"))
                load_chunk(g, sp, i)

            sp.wait_ge(*vec.at("g2"))
            sp.dma_start(g.mod_rows, g.mod[0:1, :, :]).then_inc(g.mod_out, 16)
            sp.wait_ge(g.mod_out, 16)

        @block.gpsimd
        def _(pool):
            make_constants(nc, g, pool, pool_s)

        @block.scalar
        def _(sc):
            def small(dst, src):
                sc.dma_start(dst, src).then_inc(g.small_in, 16)
                g.n_small += 16

            g.n_small = 0
            small(g.ffn_w_row[:, :], a["norm_ffn_w"].partition_broadcast(P).rearrange("p a n -> p (a n)"))
            for i, n in enumerate(("q_norm_w", "k_norm_w")):
                small(g.qk_w[:, i, :], a[n].partition_broadcast(P).rearrange("p a n -> p (a n)"))
            small(g.b_router[:, :], a["b_router"].partition_broadcast(P).rearrange("p a n -> p (a n)"))
            small(g.freq[:, :], a["inv_freq"].partition_broadcast(P).rearrange("p a n -> p (a n)"))
            sc.dma_start(g.pos[:, :], a["positions"][0].rearrange("(t p) -> p t", p=P), allow_slow_non_contiguous=True).then_inc(g.small_in, 16)
            small(g.w_lo[0:64, :], a["rwkv_w2"][0])
            small(g.w_lo[64:128, :], a["rwkv_a2"][0])
            small(g.w_g[:, :], a["rwkv_g2"][0])
            small(g.w_router[:, :, :], a["w_router"][0].rearrange("(k p) n -> p k n", p=P))
            sc.wait_ge(*vec.at("cols"))
            sc.activation(g.sig[:, :], g.cols[:, 0:KD], ACT.Sigmoid).then_inc(*act("sig"))

            def evacuate(j):
                sc.wait_ge(*pe.at(f"ada{j}"))
                dst = g.mod1[:, j, :] if j < 4 else g.mod[:, (j - 4) // 2, (j % 2) * 512:(j % 2) * 512 + 512]
                sc.copy(dst, ps[1 + j % 3][:, :]).then_inc(*act(f"mod{j}"))

            for j in range(4):
                evacuate(j)
            sc.wait_ge(x_in, 16)
            for t in range(NT):
                if t:
                    sc.wait_ge(*act.at(f"sq{t - 1}"))
                sc.activation(g.junk[:, :], g.x[:, t, :], ACT.Square, accum_out=g.ss[:, t:t + 1]).then_inc(*act(f"sq{t}"))
            sc.wait_ge(*act.at(f"sq{NT - 1}"))
            sc.wait_ge(g.eps_ready, 1)
            sc.activation(g.rstd[:, :], g.ss[:, :], ACT.Sqrt, bias=g.eps[:, 0:1], scale=1.0 / D).then_inc(*act("std"))
            for j in range(4, 12):
                evacuate(j)

        @block.vector
        def _(ve):
            ve.memset(g.eps[:, 0:1], NORM_EPS)
            ve.memset(g.eps[:, 1:2], GN_EPS).then_inc(g.eps_ready, 1)
            ve.wait_ge(*pe.at("rows"))
            ve.tensor_copy(g.cols[:, :], ps[0][:, 0:N_ROWS]).then_inc(*vec("cols"))
            ve.wait_ge(*act.at("sig"))
            ve.wait_ge(*vec.at("cols"))
            ve.tensor_tensor(g.cond[:, :], g.cols[:, 0:KD], g.sig[:, :], ALU.mult).then_inc(*vec("cond"))
            ve.wait_ge(*pool_s.at("c2"))
            ve.wait_ge(*vec.at("cond"))
            for k in range(KD):
                ve.tensor_scalar(g.condrep[:, k, :], g.ones[:, :], g.cond[:, k:k + 1], None, ALU.mult).then_inc(*vec(f"rep{k}"))
            ve.wait_ge(*act.at("std"))
            ve.reciprocal(g.rstd[:, :], g.rstd[:, :]).then_inc(*vec("rstd"))
            ve.wait_ge(*vec.at("rstd"))
            for t in range(NT):
                ve.tensor_scalar(g.xn[:, t, :], g.x[:, t, :], g.rstd[:, t:t + 1], None, ALU.mult).then_inc(*vec(f"xn{t}"))
            for q in range(4):
                ve.wait_ge(*pe.at(f"mcol{q}"))
                src = ps[4 + q][:, :].rearrange("p (b n) -> p b n", b=4)[:, :, 0]
                ve.tensor_copy(g.mod1_cols[:, 4 * q:4 * q + 4], src).then_inc(*vec(f"mcol{q}"))
            ve.wait_ge(*vec.at("mcol3"))
            at = ROWS["norm_mix_w"][0]
            ve.scalar_tensor_tensor(g.gain[:, :], g.mod1_cols[:, KD:2 * KD], 1.0, g.cols[:, at:at + KD], ALU.add, ALU.mult).then_inc(*vec("gain"))
            ve.wait_ge(*vec.at("gain"))
            for k in range(KD):
                ve.wait_ge(*pe.at(f"h{k}"))
                ve.tensor_scalar(g.hT[:, k, :], ps[4 + k % 4][:, :], g.gain[:, k:k + 1], g.mod1_cols[:, k:k + 1],
                                 ALU.mult, ALU.add).then_inc(*vec(f"h{k}"))
            ve.wait_ge(g.small_in, 16 * 10)
            ve.wait_ge(*act.at("mod11"))
            ve.scalar_tensor_tensor(g.mod[:, 2, :], g.mod[:, 2, :], 1.0, g.ffn_w_row[:, :], ALU.add, ALU.mult).then_inc(*vec("g2"))

        @block.tensor
        def _(te):
            te.wait_ge(rows_in, 16 * len(ROWS))
            te.wait_ge(*pool_s.at("c2"))
            te.transpose(ps[0][:, 0:N_ROWS], g.stage[:, :], g.ident[0:N_ROWS, 0:N_ROWS]).then_inc(*pe("rows"))
            te.wait_ge(row_in, 16)
            te.wait_ge(*vec.at(f"rep{KD - 1}"))

            def ada(j):
                te.wait_ge(*chunk_loaded(g, j))
                if j >= 3:
                    te.wait_ge(*act.at(f"mod{j - 3}"))
                out = ps[1 + j % 3][:, :]
                te.matmul(out, g.ones[0:1, :], g.ada_b_row[:, 512 * j:512 * j + 512], start=True, stop=False)
                for k in range(KD):
                    mm = te.matmul(out, g.condrep[:, k, :], slot(g, j)[:, k, :], start=False, stop=(k == KD - 1))
                mm.then_inc(*pe(f"ada{j}"))

            for j in range(4):
                ada(j)
            for q in range(4):
                te.wait_ge(*act.at(f"mod{q}"))
                for b in range(4):
                    mm = te.transpose(ps[4 + q][:, 128 * b:128 * b + 128], g.mod1[:, q, 128 * b:128 * b + 128], g.ident[:, :])
                mm.then_inc(*pe(f"mcol{q}"))
            ada(4)
            te.wait_ge(*vec.at(f"xn{NT - 1}"))
            for k in range(KD):
                te.wait_ge(*vec.at(f"h{k - 4}" if k >= 4 else f"mcol{k}"))
                for t in range(NT):
                    mm = te.transpose(ps[4 + k % 4][:, P * t:P * t + P], g.xn[:, t, P * k:P * k + P], g.ident[:, :])
                mm.then_inc(*pe(f"h{k}"))
            for j in range(5, 12):
                ada(j)


N_CONSTS = 57


def make_constants(nc, g, pool, s):
    def step(ins):
        ins.then_inc(*s(f"c{s.count}"))
        pool.wait_ge(s.sem, s.count)

    def select(dst, pattern, op, fill, base, cm):
        step(pool.affine_select(out=dst, in_=dst, pattern=pattern, compare_op=op, fill=fill, base=base, channel_multiplier=cm))

    def fill(dst, value):
        step(pool.memset(dst, value))

    fill(g.ones[:, :], 1.0)
    fill(g.ident[:, :], 0.0)
    select(g.ident[:, :], [[-1, P]], ALU.not_equal, 1.0, 0, 1)
    fill(g.eye64[:, :], 0.0)
    for base in (0, -64):
        select(g.eye64[:, :], [[-1, 64]], ALU.not_equal, 1.0, base, 1)
    fill(g.gram_mask[:, :, :], 1.0)
    select(g.gram_mask[:, 0, :], [[1, P]], ALU.is_gt, 0.0, 0, -1)
    select(g.gram_mask[:, 1, :], [[1, P]], ALU.is_ge, 0.0, 0, -1)
    fill(g.gram_mask[0:64, :, 64:P], 0.0)
    fill(g.causal[:, :], 0.0)
    select(g.causal[:, :], [[-1, P]], ALU.is_ge, -1e30, 0, 1)
    fill(g.chunk_mask[:, :], 1.0)
    fill(g.chunk_mask[:, :].rearrange("p (c n) -> p c n", n=CH)[:, :, 0], 0.0)
    for l in range(6):
        b = 1 << l
        half = g.level_mask[:, l, :].rearrange("p (j h b) -> p j h b", h=2, b=b)
        fill(g.level_mask[:, l, :], 0.0)
        fill(half[:, :, 1, :], 1.0)
        select(half[:, :, 1, :], [[-2 * b, P // (2 * b)], [0, b]], ALU.is_ge, 0.0, 0, 1)
        select(half[:, :, 1, :], [[2 * b, P // (2 * b)], [0, b]], ALU.is_ge, 0.0, b - 1, -1)
    fill(g.head_ones[:, :], 0.0)
    fill(g.head_ones[0:64, 0:64], 1.0)
    fill(g.head_ones[64:P, 64:P], 1.0)
    fill(g.later[:, :], 1.0)
    select(g.later[:, :], [[1, P]], ALU.is_gt, 0.0, 0, -1)
    for dst, n, cm in ((g.iota_row, P, 0), (g.iota_part, 1, 1)):
        step(pool.iota(dst[:, :], [[1, n]], base=0, channel_multiplier=cm, allow_small_or_imprecise_dtypes=True))
    fill(g.vec1[:, :], 1.0)
    assert s.count <= N_CONSTS, s.count


def phase_project(nc, g):
    with ExitStack() as ctx:
        tile = ([P, SEQ], F32)
        (g.raw, g.lerp, g.wa, g.sg, g.not_mu, g.ka, g.rn) = g.sb(ctx, raw=([P, 4, SEQ + 1], F32), lerp=([P, 2, SEQ], F32), wa=tile, sg=tile, not_mu=([P, NMU], F32), ka=tile, rn=tile)
        quarter = lambda buf, i: buf[:, 2 * i:2 * i + 2, :].rearrange("p a (b n) -> p (a b) n", n=SEQ)
        sw, al, rk = quarter(g.x, 0), quarter(g.x, 1), quarter(g.mod, 0)
        csum, ew = quarter(g.mod, 1)[:, 0:2, :], quarter(g.mod, 1)[:, 2:4, :]
        flat = g.AR[:, :, :, :, :].rearrange("p i t x n -> p i (t x n)")
        squares, norms = flat[:, :, 0:SEQ], flat[:, :, SEQ:2 * SEQ]
        f4 = range(FT)
        outs = ["l0", "l1"] + [f"r{i}" for i in f4] + [f"k{i}" for i in f4] + [f"{x}{i}" for i in f4 for x in ("zw", "za")]
        outs += [f"{x}{i}" for x in ("g", "ss", "v", "m", "bo") for i in f4]
        pe = g.steps(ctx, "b_pe", outs)
        exps = [[f"{x}{i}" for x in ("ew", "ep", "ei")] for i in f4]
        act = g.steps(ctx, "b_act", outs[:6] + ["tanh", "sigg"] + outs[6:18] + names("sq{}", 4) + outs[18:26] + exps[0] + exps[1]
                      + ["v0", "v1"] + exps[2] + ["v2", "v3"] + exps[3] + names("m{}", 4))
        lerps = outs[:10] + names("v{}", 4)

        def forms(i):
            return [f"{x}{i}" for x in ("ld", "L", "Lp", "nm", "rn", "kk", "ka", "k2", "rk", "R", "A", "kb", "B", "K", "wc")]

        vec = g.steps(ctx, "b_vec", ["not_mu", "zero"] + [x for n in lerps[:10] for x in (f"t_{n}", n)] + names("kk0{}", 4)
                      + [x for i in f4 for x in forms(i) + ({1: ["t_v0", "v0", "t_v1", "v1"], 2: ["t_v2", "v2", "t_v3", "v3"]}.get(i, []))]
                      + names("bv{}", 4))
        block = ctx.enter_context(nc.Block())
        bank = {n: g.ps[j % 8] for j, n in enumerate(outs)}

        @block.sync
        def _(sp):
            for i, last in ((LO, "l1"), (LO + 1, "r3"), (LO + 2, "k3"), (LO + 3, "v3"), (MLA, "m3")):
                if i + RING <= MLA:
                    sp.wait_ge(*pe.at(last))
                    load_chunk(g, sp, i + RING)

        @block.tensor
        def _(te):
            def product(name, pairs, cols=SEQ):
                j = outs.index(name)
                if j >= 8:
                    te.wait_ge(*act.at(outs[j - 8]))
                for n, (lhsT, rhs) in enumerate(pairs):
                    mm = te.matmul(bank[name][:, 0:cols], lhsT, rhs, start=(n == 0), stop=(n == len(pairs) - 1))
                mm.then_inc(*pe(name))

            def feature(name, chunk, i):
                te.wait_ge(*chunk_loaded(g, chunk))
                w = slot(g, chunk)
                product(name, [(w[:, k, P * i:P * i + P], g.hT[:, k, :]) for k in range(KD)])

            for i in range(2):
                feature(f"l{i}", LO, i)
            for i in f4:
                feature(f"r{i}", RKV, i)
            for i in f4:
                feature(f"k{i}", RKV + 1, i)
            te.wait_ge(*act.at("tanh"))
            for i in f4:
                at = slice(P * i, P * i + P)
                product(f"zw{i}", [(g.w_lo[0:64, at], g.wa[0:64, :])])
                product(f"za{i}", [(g.w_lo[64:P, at], g.wa[64:P, :])])
            te.wait_ge(*act.at("sigg"))
            for i in f4:
                product(f"g{i}", [(g.w_g[:, P * i:P * i + P], g.sg[:, :])])
            for i in f4:
                te.wait_ge(*act.at(f"sq{i}"))
                product(f"ss{i}", [(g.head_ones[:, :], squares[:, i, :])])
            for i in f4:
                feature(f"v{i}", RKV + 2, i)
            te.wait_ge(*chunk_loaded(g, MLA))
            for t in range(NT):
                product(f"m{t}", [(g.hT[:, k, P * t:P * t + P], slot(g, MLA)[:, k, :]) for k in range(KD)], MLA_IN)
            for i in f4:
                te.wait_ge(*vec.at(f"rk{i}"))
                product(f"bo{i}", [(g.head_ones[:, :], rk[:, i, :])])

        @block.scalar
        def _(sc):
            def raw(name):
                m = lerps.index(name)
                sc.wait_ge(*pe.at(name))
                sc.wait_ge(*(vec.at(lerps[m - 4]) if m >= 4 else vec.at("zero")))
                sc.copy(g.raw[:, m % 4, 1:SEQ + 1], bank[name][:, :]).then_inc(*act(name))

            for n in lerps[:6]:
                raw(n)
            sc.wait_ge(*vec.at("l0"))
            sc.activation(g.wa[0:64, :], g.wa[0:64, :], ACT.Tanh).then_inc(*act("tanh"))
            sc.wait_ge(*vec.at("l1"))
            sc.activation(g.sg[:, :], g.sg[:, :], ACT.Sigmoid).then_inc(*act("sigg"))
            for n in lerps[6:10]:
                raw(n)
            for i in f4:
                sc.wait_ge(*pe.at(f"zw{i}"))
                sc.activation(sw[:, i, :], bank[f"zw{i}"][:, :], ACT.Sigmoid, bias=g.col("w0", i)).then_inc(*act(f"zw{i}"))
                sc.wait_ge(*pe.at(f"za{i}"))
                sc.activation(al[:, i, :], bank[f"za{i}"][:, :], ACT.Sigmoid, bias=g.col("a0", i)).then_inc(*act(f"za{i}"))
            for i in f4:
                sc.wait_ge(*vec.at(f"kk0{i}"))
                sc.activation(squares[:, i, :], g.Bt[:, i, :], ACT.Square).then_inc(*act(f"sq{i}"))
            for i in f4:
                sc.wait_ge(*pe.at(f"g{i}"))
                sc.copy(g.gate[:, i, :], bank[f"g{i}"][:, :]).then_inc(*act(f"g{i}"))
            for i in f4:
                sc.wait_ge(*pe.at(f"ss{i}"))
                sc.activation(norms[:, i, :], bank[f"ss{i}"][:, :], ACT.Sqrt).then_inc(*act(f"ss{i}"))

            def exponentials(i):
                j = i % 2
                sc.wait_ge(*vec.at(f"L{i}"))
                sc.activation(ew[:, j, :], csum[:, j, :], ACT.Exp).then_inc(*act(f"ew{i}"))
                sc.wait_ge(*vec.at(f"Lp{i}"))
                sc.activation(sw[:, i, :], sw[:, i, :], ACT.Exp).then_inc(*act(f"ep{i}"))
                sc.activation(csum[:, j, :], csum[:, j, :], ACT.Exp, scale=-1.0).then_inc(*act(f"ei{i}"))

            exponentials(0)
            exponentials(1)
            raw("v0")
            raw("v1")
            exponentials(2)
            raw("v2")
            raw("v3")
            exponentials(3)
            for t in range(NT):
                sc.wait_ge(*pe.at(f"m{t}"))
                sc.copy(g.mla_in[:, t, :], bank[f"m{t}"][:, 0:MLA_IN]).then_inc(*act(f"m{t}"))

        @block.vector
        def _(ve):
            at = ROWS["mu"][0]
            ve.tensor_scalar(g.not_mu[:, :], g.cols[:, at:at + NMU], -1.0, 1.0, ALU.mult, ALU.add).then_inc(*vec("not_mu"))
            ve.memset(g.raw[:, :, 0:1], 0.0).then_inc(*vec("zero"))
            ve.wait_ge(*vec.at("zero"))

            def shift(name, dst, mu):
                m = lerps.index(name)
                ve.wait_ge(*act.at(name))
                ve.tensor_scalar(g.lerp[:, m % 2, :], g.raw[:, m % 4, 0:SEQ], g.col("mu", mu), None, ALU.mult).then_inc(*vec(f"t_{name}"))
                ve.wait_ge(*vec.at(f"t_{name}"))
                ve.scalar_tensor_tensor(dst, g.raw[:, m % 4, 1:SEQ + 1], g.not_mu[:, mu:mu + 1], g.lerp[:, m % 2, :],
                                        ALU.mult, ALU.add).then_inc(*vec(name))

            shift("l0", g.wa[:, :], 12)
            shift("l1", g.sg[:, :], 13)
            for i in f4:
                shift(f"r{i}", g.bv[:, i, :], i)
            for i in f4:
                shift(f"k{i}", g.Kt[:, i, :], 4 + i)
            for i in f4:
                ve.wait_ge(*vec.at(f"k{i}"))
                ve.tensor_scalar(g.Bt[:, i, :], g.Kt[:, i, :], g.col("k_k", i), None, ALU.mult).then_inc(*vec(f"kk0{i}"))
            for i in f4:
                if i >= 2:
                    for n in (2 * i - 4, 2 * i - 3):
                        shift(f"v{n}", g.v[:, n, :], 8 + n)
                j = i % 2
                k, r, b = g.Kt[:, i, :], g.bv[:, i, :], g.Bt[:, i, :]
                ve.wait_ge(*act.at(f"zw{i}"))
                ve.tensor_scalar(sw[:, i, :], sw[:, i, :], DECAY, None, ALU.mult).then_inc(*vec(f"ld{i}"))
                ve.wait_ge(*vec.at(f"ld{i}"))
                ve.tensor_tensor_scan(csum[:, j, :], g.chunk_mask[:, :], sw[:, i, :], 0.0, ALU.mult, ALU.add).then_inc(*vec(f"L{i}"))
                ve.wait_ge(*vec.at(f"L{i}"))
                ve.tensor_tensor(sw[:, i, :], csum[:, j, :], sw[:, i, :], ALU.subtract).then_inc(*vec(f"Lp{i}"))
                ve.wait_ge(*act.at(f"ss{i}"))
                ve.tensor_scalar(g.rn[:, :], norms[:, i, :], 1e-12, None, ALU.max).then_inc(*vec(f"nm{i}"))
                ve.wait_ge(*vec.at(f"nm{i}"))
                ve.reciprocal(g.rn[:, :], g.rn[:, :]).then_inc(*vec(f"rn{i}"))
                ve.wait_ge(*vec.at(f"rn{i}"))
                ve.tensor_tensor(b, b, g.rn[:, :], ALU.mult).then_inc(*vec(f"kk{i}"))
                ve.wait_ge(*act.at(f"za{i}"))
                ve.tensor_scalar(g.ka[:, :], al[:, i, :], -1.0, g.col("k_a", i), ALU.add, ALU.mult).then_inc(*vec(f"ka{i}"))
                ve.wait_ge(*vec.at(f"ka{i}"))
                ve.scalar_tensor_tensor(k, g.ka[:, :], 1.0, k, ALU.add, ALU.mult).then_inc(*vec(f"k2{i}"))
                ve.wait_ge(*vec.at(f"k2{i}"))
                ve.scalar_tensor_tensor(rk[:, i, :], r, g.col("r_k", i), k, ALU.mult, ALU.mult).then_inc(*vec(f"rk{i}"))
                split = lambda x: x.rearrange("p (t n) -> p t n", t=NT)
                ve.wait_ge(*act.at(f"ew{i}"))
                ve.tensor_tensor(g.AR[:, i, :, 1, :], split(r), split(ew[:, j, :]), ALU.mult).then_inc(*vec(f"R{i}"))
                ve.wait_ge(*act.at(f"ep{i}"))
                ve.scalar_tensor_tensor(g.AR[:, i, :, 0, :], split(b), -1.0, split(sw[:, i, :]), ALU.mult, ALU.mult).then_inc(*vec(f"A{i}"))
                ve.wait_ge(*vec.at(f"A{i}"))
                ve.tensor_tensor(b, b, al[:, i, :], ALU.mult).then_inc(*vec(f"kb{i}"))
                ve.wait_ge(*vec.at(f"kb{i}"))
                ve.wait_ge(*act.at(f"ei{i}"))
                ve.tensor_tensor(b, b, csum[:, j, :], ALU.mult).then_inc(*vec(f"B{i}"))
                ve.tensor_tensor(k, k, csum[:, j, :], ALU.mult).then_inc(*vec(f"K{i}"))
                ve.tensor_copy(g.w_end[:, i, :], ew[:, j, :].rearrange("p (c n) -> p c n", n=CH)[:, :, CH - 1]).then_inc(*vec(f"wc{i}"))
            for i in f4:
                ve.wait_ge(*pe.at(f"bo{i}"))
                ve.tensor_tensor(g.bv[:, i, :], bank[f"bo{i}"][:, :], g.v[:, i, :], ALU.mult).then_inc(*vec(f"bv{i}"))


def phase_rwkv(nc, g):
    with ExitStack() as ctx:
        ring = g.ring[:, :, :]
        gm_buf = [ring[:, j, :].rearrange("p (u n) -> p u n", u=8) for j in range(2)]
        scratch = [ring[:, 2, :], g.x[:, :, :].rearrange("p a b -> p (a b)"), g.mod[:, :, :].rearrange("p a b -> p (a b)")]
        take = [0]

        def quad():
            i = take[0]
            take[0] += 1
            return scratch[i // 8][:, 512 * (i % 8):512 * (i % 8) + 512].rearrange("p (u n) -> p u n", u=4)

        X = [quad() for _ in range(2)]
        T = [quad() for _ in range(2)]
        TT = [quad() for _ in range(2)]
        off = [[quad() for _ in range(2)] for _ in range(2)]
        X0 = [quad() for _ in range(2)]
        Y1 = [quad() for _ in range(2)]
        (g.tok, g.square) = g.sb(ctx, tok=([P, 2, NT, 4, P], F32), square=([P, 2, SEQ], F32))
        ysq = g.square
        fts, halves = range(FT), range(2)
        fh = [(f, h) for f in fts for h in halves]

        def pre_names(f):
            return [f"tm{f}{t}" for t in range(NT)] + [f"gm{f}{u}" for u in range(8)]

        def level_names(f, l):
            out = [f"xx{f}{l}{h}" for h in halves]
            for h in halves:
                out += [f"tt{f}{l}{h}"] + ([f"t{f}{l}{h}"] if l < 5 else [])
            return out

        def post_names(f):
            return [f"{x}{f}{h}" for x in ("x0", "y1", "ry", "eg") for h in halves]

        order = pre_names(0)
        for f in fts:
            order += [f"tr{f}{h}" for h in halves]
            nxt = pre_names(f + 1) if f + 1 < FT else []
            for l in range(1, 6):
                order += level_names(f, l)
                order += nxt[3 * (l - 1):3 * l]
            order += post_names(f)
        chain = []
        for c in range(NCH):
            chain += [f"y{c}"] + ([f"s{c}"] if c < NCH - 1 else [])
        tail = [f"{x}{f}" for x in ("mean", "var") for f in fts]
        pe = g.steps(ctx, "c_pe", order + chain + tail)
        pool_names = []
        for f in fts:
            pool_names += [f"off{f}0{h}" for h in halves] + [f"i{f}{h}" for h in halves] + [f"off{f}{l}{h}" for l in range(1, 6) for h in halves]
        pool = g.steps(ctx, "c_pool", pool_names)
        act_names, vec_names = [], []
        for n in order:
            if n[0:2] in ("tm", "tr", "x0", "y1"):
                act_names.append(n)
            elif n[0:2] in ("gm", "tt"):
                vec_names.append(n)
            elif n[0] == "x":
                act_names.append(n)
            elif n[0:2] == "ry":
                vec_names.append("r" + n[2:])
                act_names.append("y0_" + n[2:])
            elif n[0:2] == "eg":
                vec_names += [f"{x}{n[2:]}{c}" for c in range(2) for x in "eg"]
            else:
                vec_names.append(n)
        vec_names += ["s_first"]
        for c in range(NCH - 1):
            vec_names += [f"s{c}_{f}" for f in fts]
        vec_names += [f"y{f}" for f in fts] + [f"mean{f}" for f in fts]
        vec_names += [f"{x}{f}" for f in fts for x in ("rs", "yn", "ya", "yb", "yT")]
        act_names += [f"ysq{f}" for f in fts] + [f"std{f}" for f in fts]
        act = g.steps(ctx, "c_act", act_names)
        vec = g.steps(ctx, "c_vec", vec_names)
        block = ctx.enter_context(nc.Block())
        ps = g.ps
        pre_bank = {}
        for f in fts:
            for j, n in enumerate(pre_names(f)):
                pre_bank[n] = ps[j % 4]

        def gm(f, u):
            return gm_buf[f % 2][:, u, :]

        def rows(hh):
            return slice(64 * hh, 64 * hh + 64)

        def unit(u):
            return u // 4, u % 4, u // 2, u % 2

        def as_units(ap):
            return ap.rearrange("p (u n) -> p u n", u=4)

        def yc_of(f):
            return g.Bt[:, f, :]

        def yv_of(f):
            return g.Kt[:, f, :]

        @block.tensor
        def _(te):
            def group(out, pairs):
                for n, (lhsT, rhs) in enumerate(pairs):
                    mm = te.matmul(out, lhsT, rhs, start=(n == 0), stop=(n == len(pairs) - 1))
                return mm

            def pre(f, n):
                names_ = pre_names(f)
                j = names_.index(n)
                prev = names_[j - 4] if j >= 4 else (pre_names(f - 1)[j + 8] if f else None)
                if prev:
                    te.wait_ge(*(act.at(prev) if prev.startswith("tm") else vec.at(prev)))
                if j in (2, 3) and f >= 2:
                    te.wait_ge(*vec.at(f"g{f - 2}{j - 2}1"))
                bank = pre_bank[n]
                if j < NT:
                    cols = slice(P * j, P * j + P)
                    for i, src in enumerate((g.v[:, f, cols], g.Bt[:, f, cols], g.Kt[:, f, cols], g.AR[:, f, j, 0, :])):
                        mm = te.transpose(bank[:, P * i:P * i + P], src, g.ident[:, :])
                else:
                    _, _, t, hh = unit(j - NT)
                    for i, src in enumerate((g.Bt, g.Kt)):
                        mm = te.matmul(bank[:, 256 * i:256 * i + 256], src[rows(hh), f, P * t:P * t + P],
                                       g.AR[rows(hh), f, t, :, :].rearrange("p a n -> p (a n)"), start=True, stop=True)
                mm.then_inc(*pe(n))

            for n in pre_names(0):
                pre(0, n)
            for f in fts:
                tok = g.tok[:, f % 2, :, :, :]
                for h in halves:
                    te.wait_ge(*pool.at(f"i{f}{h}"))
                    if f:
                        te.wait_ge(*act.at(f"y0_{f - 1}{h}"))
                        te.wait_ge(*vec.at(f"r{f - 1}{h}"))
                    for u in range(4):
                        mm = te.transpose(ps[4 + 2 * h][:, P * u:P * u + P], TT[h][:, u, :], g.ident[:, :])
                    mm.then_inc(*pe(f"tr{f}{h}"))
                nxt = pre_names(f + 1) if f + 1 < FT else []
                for l in range(1, 6):
                    for h in halves:
                        te.wait_ge(*pool.at(f"off{f}{l}{h}"))
                        te.wait_ge(*(act.at(f"tr{f}{h}") if l == 1 else vec.at(f"t{f}{l - 1}{h}")))
                        for u in range(4):
                            mm = te.matmul(ps[4 + 2 * h][:, P * u:P * u + P], off[l % 2][h][:, u, :], T[h][:, u, :], start=True, stop=True)
                        mm.then_inc(*pe(f"xx{f}{l}{h}"))
                    for h in halves:
                        te.wait_ge(*act.at(f"xx{f}{l}{h}"))
                        if l > 1:
                            te.wait_ge(*vec.at(f"tt{f}{l - 1}{h}"))
                        elif f:
                            te.wait_ge(*vec.at(f"g{f - 1}{h}1"))
                        for u in range(4):
                            mm = te.matmul(ps[5 + 2 * h][:, P * u:P * u + P], X[h][:, u, :], TT[h][:, u, :], start=True, stop=True)
                        mm.then_inc(*pe(f"tt{f}{l}{h}"))
                        if l < 5:
                            for u in range(4):
                                mm = te.matmul(ps[4 + 2 * h][:, P * u:P * u + P], TT[h][:, u, :], X[h][:, u, :], start=True, stop=True)
                            mm.then_inc(*pe(f"t{f}{l}{h}"))
                    for n in nxt[3 * (l - 1):3 * l]:
                        pre(f + 1, n)
                for h in halves:
                    te.wait_ge(*act.at(f"xx{f}5{h}"))
                    te.wait_ge(*act.at(f"tm{f}{2 * h + 1}"))
                    for u in range(4):
                        _, _, t, hh = unit(4 * h + u)
                        mm = te.matmul(ps[4 + 2 * h][:, 64 * u:64 * u + 64], gm(f, 4 * h + u)[:, 256:384], tok[:, t, 0, 64 * hh:64 * hh + 64],
                                       start=True, stop=True)
                    mm.then_inc(*pe(f"x0{f}{h}"))
                for h in halves:
                    te.wait_ge(*act.at(f"x0{f}{h}"))
                    te.wait_ge(*vec.at(f"tt{f}5{h}"))
                    for u in range(4):
                        _, _, t, hh = unit(4 * h + u)
                        for at, rhs in ((0, tok[:, t, 3, 64 * hh:64 * hh + 64]), (64, X0[h][:, u, 0:64])):
                            mm = te.matmul(ps[5 + 2 * h][:, P * u + at:P * u + at + 64], TT[h][:, u, :], rhs, start=True, stop=True)
                    mm.then_inc(*pe(f"y1{f}{h}"))
                for h in halves:
                    te.wait_ge(*act.at(f"y1{f}{h}"))
                    for u in range(4):
                        _, _, t, hh = unit(4 * h + u)
                        m, at = gm(f, 4 * h + u), 256 * (u // 2)
                        te.matmul(ps[4 + 2 * h][rows(hh), at:at + P], Y1[h][:, u, 0:64], m[:, 128:256], start=True, stop=True)
                        mm = group(ps[4 + 2 * h][rows(hh), at + P:at + 2 * P],
                                   [(Y1[h][:, u, 64:P], m[:, 128:256]), (tok[:, t, 0, 64 * hh:64 * hh + 64], m[:, 384:512])])
                    mm.then_inc(*pe(f"ry{f}{h}"))
                for h in halves:
                    te.wait_ge(*vec.at(f"gm{min(f + 1, FT - 1)}{6 + h}"))
                    te.wait_ge(*act.at(f"y1{f}{h}"))
                    for u in range(4):
                        _, _, t, hh = unit(4 * h + u)
                        cols = slice(64 * hh, 64 * hh + 64)
                        for c in range(2):
                            bank, at = (ps[5 + 2 * h], ps[2 + h])[c], P * (u // 2)
                            te.matmul(bank[rows(hh), at:at + 64], Y1[h][rows(c), u, 0:64], tok[rows(c), t, 1, cols], start=True, stop=True)
                            mm = group(bank[rows(hh), at + 64:at + P],
                                       [(tok[rows(c), t, 1, cols], Y1[h][rows(c), u, 64:P]), (tok[rows(c), t, 2, cols], tok[rows(c), t, 0, cols])])
                    mm.then_inc(*pe(f"eg{f}{h}"))
            te.wait_ge(*vec.at("s_first"))
            te.wait_ge(*act.at("y0_31"))
            for c in range(NCH):
                if c:
                    te.wait_ge(*vec.at(f"s{c - 1}_3"))
                for f in fts:
                    for hh in range(2):
                        state = g.AR[rows(hh), f, c // 2, 0, 64 * (c % 2):64 * (c % 2) + 64]
                        mm = te.matmul(ps[4 + f][rows(hh), 64 * c:64 * c + 64], state,
                                       g.AR[rows(hh), f, c // 2, 1, 64 * (c % 2):64 * (c % 2) + 64], start=True, stop=True)
                mm.then_inc(*pe(f"y{c}"))
                if c == NCH - 1:
                    continue
                for f in fts:
                    for hh in range(2):
                        state = g.AR[rows(hh), f, c // 2, 0, 64 * (c % 2):64 * (c % 2) + 64]
                        mm = te.matmul(ps[c % 2][rows(hh), 64 * f:64 * f + 64], g.Bt[rows(hh), f, 64 * c:64 * c + 64], state, start=True, stop=True)
                mm.then_inc(*pe(f"s{c}"))
            for f in fts:
                te.wait_ge(*vec.at(f"y{f}"))
                te.matmul(ps[f][:, :], g.head_ones[:, :], g.v[:, f, :], start=True, stop=True).then_inc(*pe(f"mean{f}"))
            for f in fts:
                te.wait_ge(*act.at(f"ysq{f}"))
                te.matmul(ps[4 + f][:, :], g.head_ones[:, :], ysq[:, f % 2, :], start=True, stop=True).then_inc(*pe(f"var{f}"))

        @block.gpsimd
        def _(po):
            for f in fts:
                def masked(l, h):
                    src = gm_buf[f % 2][:, 4 * h:4 * h + 4, 0:P]
                    mask = g.level_mask[:, l:l + 1, :].broadcast_to([P, 4, P])
                    po.tensor_tensor(off[l % 2][h], src, mask, ALU.mult).then_inc(*pool(f"off{f}{l}{h}"))

                for h in halves:
                    po.wait_ge(*vec.at(f"gm{f}{4 * h + 3}"))
                    if f:
                        po.wait_ge(*pe.at(f"y1{f - 1}{h}"))
                    masked(0, h)
                for h in halves:
                    po.wait_ge(*pool.at(f"off{f}0{h}"))
                    eye = g.ident[:, :].unsqueeze(1).broadcast_to([P, 4, P])
                    po.tensor_tensor(TT[h], off[0][h], eye, ALU.add).then_inc(*pool(f"i{f}{h}"))
                for l in range(1, 6):
                    for h in halves:
                        if l >= 2:
                            po.wait_ge(*(pool.at(f"i{f}{h}") if l == 2 else pe.at(f"xx{f}{l - 2}{h}")))
                        masked(l, h)

        @block.scalar
        def _(sc):
            for n in order:
                k = n[0:2]
                if k == "tm":
                    f, t = int(n[2]), int(n[3])
                    if f >= 2:
                        sc.wait_ge(*pe.at(f"eg{f - 2}1"))
                    sc.wait_ge(*pe.at(n))
                    sc.copy(g.tok[:, f % 2, t, :, :].rearrange("p a n -> p (a n)"), pre_bank[n][:, :]).then_inc(*act(n))
                elif k in ("tr", "x0", "y1"):
                    f, h = int(n[2]), int(n[3])
                    sc.wait_ge(*pe.at(n))
                    dst = {"tr": T, "x0": X0, "y1": Y1}[k][h]
                    n_cols = 64 if k == "x0" else P
                    src = ps[(5 if k == "y1" else 4) + 2 * h][:, 0:4 * n_cols]
                    sc.copy(dst[:, :, 0:n_cols], as_units(src)).then_inc(*act(n))
                elif n[0] == "x":
                    h = int(n[4])
                    sc.wait_ge(*pe.at(n))
                    sc.copy(X[h], as_units(ps[4 + 2 * h][:, :])).then_inc(*act(n))
                elif k == "ry":
                    f, h = int(n[2]), int(n[3])
                    sc.wait_ge(*vec.at(f"r{f}{h}"))
                    src = ps[4 + 2 * h][:, :].rearrange("p (t x n) -> p t x n", t=2, x=2)[:, :, 1, :]
                    sc.copy(g.v[:, f, 256 * h:256 * h + 256].rearrange("p (t n) -> p t n", t=2), src).then_inc(*act(f"y0_{f}{h}"))
            for f in fts:
                sc.wait_ge(*vec.at(f"mean{f}"))
                if f >= 2:
                    sc.wait_ge(*pe.at(f"var{f - 2}"))
                sc.activation(ysq[:, f % 2, :], yc_of(f), ACT.Square).then_inc(*act(f"ysq{f}"))
            for f in fts:
                sc.wait_ge(*pe.at(f"var{f}"))
                sc.activation(yv_of(f), ps[4 + f][:, :], ACT.Sqrt, bias=g.eps[:, 1:2], scale=1.0 / DV).then_inc(*act(f"std{f}"))

        @block.vector
        def _(ve):
            for n in order:
                if n[0:2] == "gm":
                    f, u = int(n[2]), int(n[3])
                    ve.wait_ge(*pe.at(n))
                    if f >= 2:
                        ve.wait_ge(*pe.at(f"ry{f - 2}1"))
                    mask = g.gram_mask[:, :, :].rearrange("p a n -> p (a n)").unsqueeze(1).broadcast_to([P, 2, 256])
                    ve.tensor_tensor(gm(f, u).rearrange("p (x n) -> p x n", x=2), pre_bank[n][:, :].rearrange("p (x n) -> p x n", x=2),
                                     mask, ALU.mult).then_inc(*vec(n))
                elif n[0:2] == "tt" or (n[0] == "t" and n[1].isdigit()):
                    h = int(n[-1])
                    ve.wait_ge(*pe.at(n))
                    dst, b = (TT, 5) if n[0:2] == "tt" else (T, 4)
                    if n[0:2] == "tt" and f"t{n[2:]}" in pe.value:
                        ve.wait_ge(*pe.at(f"t{n[2:]}"))
                    ve.tensor_tensor(dst[h], as_units(ps[b + 2 * h][:, :]), dst[h], ALU.add).then_inc(*vec(n))
                elif n[0:2] == "ry":
                    f, h = int(n[2]), int(n[3])
                    ve.wait_ge(*pe.at(n))
                    src = ps[4 + 2 * h][:, :].rearrange("p (t x n) -> p t x n", t=2, x=2)[:, :, 0, :]
                    dst = g.AR[:, f, 2 * h:2 * h + 2, 1, :]
                    ve.tensor_tensor(dst, src, dst, ALU.add).then_inc(*vec(f"r{f}{h}"))
                elif n[0:2] == "eg":
                    f, h = int(n[2]), int(n[3])
                    ve.wait_ge(*pe.at(n))
                    for c in range(2):
                        src = (ps[5 + 2 * h], ps[2 + h])[c][:, 0:2 * P].rearrange("p (t x n) -> p t x n", t=2, x=2)
                        part = lambda buf: buf[:, f, 256 * h:256 * h + 256].rearrange("p (t c n) -> p t c n", t=2, c=2)[:, :, c, :]
                        eye = g.eye64[:, :].unsqueeze(1).broadcast_to([P, 2, 64])
                        w = g.w_end[:, f, 4 * h:4 * h + 4].rearrange("p (t c) -> p t c", t=2)[:, :, c:c + 1].broadcast_to([P, 2, 64])
                        ve.tensor_tensor(part(g.Bt), src[:, :, 0, :], eye, ALU.add).then_inc(*vec(f"e{f}{h}{c}"))
                        ve.tensor_tensor(part(g.Kt), src[:, :, 1, :], w, ALU.mult).then_inc(*vec(f"g{f}{h}{c}"))
            ve.wait_ge(*pe.at("eg31"))
            ve.memset(g.AR[:, :, 0, 0, 0:64], 0.0).then_inc(*vec("s_first"))
            for c in range(NCH - 1):
                ve.wait_ge(*pe.at(f"s{c}"))
                for f in fts:
                    at = c + 1
                    dst = g.AR[:, f, at // 2, 0, 64 * (at % 2):64 * (at % 2) + 64]
                    ve.scalar_tensor_tensor(dst, ps[c % 2][:, 64 * f:64 * f + 64], g.w_end[:, f, c:c + 1], g.Kt[:, f, 64 * c:64 * c + 64],
                                            ALU.mult, ALU.add).then_inc(*vec(f"s{c}_{f}"))
            for f in fts:
                ve.wait_ge(*pe.at(f"y{NCH - 1}"))
                ve.wait_ge(*act.at(f"y0_{f}1"))
                ve.tensor_tensor(g.v[:, f, :], ps[4 + f][:, :], g.v[:, f, :], ALU.add).then_inc(*vec(f"y{f}"))
            for f in fts:
                ve.wait_ge(*pe.at(f"mean{f}"))
                ve.wait_ge(*vec.at(f"y{f}"))
                ve.scalar_tensor_tensor(yc_of(f), ps[f][:, :], -1.0 / DV, g.v[:, f, :], ALU.mult, ALU.add).then_inc(*vec(f"mean{f}"))
            for f in fts:
                ve.wait_ge(*act.at(f"std{f}"))
                ve.reciprocal(yv_of(f), yv_of(f)).then_inc(*vec(f"rs{f}"))
                ve.wait_ge(*vec.at(f"rs{f}"))
                ve.tensor_tensor(yc_of(f), yc_of(f), yv_of(f), ALU.mult).then_inc(*vec(f"yn{f}"))
                ve.wait_ge(*vec.at(f"yn{f}"))
                ve.tensor_scalar(yc_of(f), yc_of(f), g.col("ln_w", f), g.col("ln_b", f), ALU.mult, ALU.add).then_inc(*vec(f"ya{f}"))
                ve.wait_ge(*vec.at(f"ya{f}"))
                ve.tensor_tensor(yc_of(f), yc_of(f), g.bv[:, f, :], ALU.add).then_inc(*vec(f"yb{f}"))
                ve.wait_ge(*vec.at(f"yb{f}"))
                ve.tensor_tensor(g.yT[:, f, :], yc_of(f), g.gate[:, f, :], ALU.mult).then_inc(*vec(f"yT{f}"))


def phase_mla(nc, g):
    with ExitStack() as ctx:
        (g.w_q, g.w_kv, g.cn, g.cT, g.qk, g.sqk, g.rope, g.v_tok, g.probT, g.o_tok, g.ss2, g.ssn, g.stat, g.trig, g.ang, g.turns,
         g.posf, g.junk2) = g.sb(ctx, w_q=([P, 2, HEADS * QK], F32), w_kv=([P, HEADS * (NOPE + DV)], F32), cn=([P, NT, Q_LORA + KV_LORA], F32),
             cT=([P, 3, SEQ], F32), qk=([P, 2, 2 * HEADS, QK], F32), sqk=([P, 2 * HEADS, QK], F32), rope=([P, 2, 4, 2 * HEADS, HALF], F32),
             v_tok=([P, NT, HEADS * DV], F32), probT=([P, 2, SEQ], F32), o_tok=([P, NT, HEADS * DV], F32),
             ss2=([P, NT, 2], F32), ssn=([P, NT, 2 * HEADS], F32), stat=([P, 4, NT * HEADS], F32), trig=([P, 2, NT, HALF], F32),
             ang=([P, NT, HALF], F32), turns=([P, 2, NT, HALF], F32), posf=([P, NT], F32), junk2=([P, Q_LORA], F32))
        qkT = [buf[0:QK, :, :].rearrange("p a (b n) -> p (a b) n", n=SEQ) for buf in (g.x, g.mod)]
        prob = g.qk[:, 0, :, :].rearrange("p h n -> p (h n)").rearrange("p (a n) -> p a n", n=SEQ)
        w_in = g.sem(ctx, "mla_weights_in")
        ts, units = range(NT), range(NT * HEADS)
        SCALE = float(QK) ** -0.5
        maxs, negs, sums, rsums = (g.stat[:, i, :] for i in range(4))
        act = g.steps(ctx, "d_act", [f"{x}{t}" for t in ts for x in ("sqq", "sqk")] + ["stq", "stk"] + names("ct{}", 3) + ["sin"]
                      + [n for t in ts for n in [f"{x}{t}" for x in ("q0_", "q1_", "kn0_", "vv0_", "kn1_", "vv1_", "kr", "sq", "sn")]
                         + ([f"tq{t - 1}{j}" for j in range(4)] if t else [])] + names("tq3{}", 4) + [x for u in units for x in [f"ex{u}"] + ([f"pc{u - 1}"] if u else [])]
                      + [f"pc{len(units) - 1}"] + names("ot{}", 4))
        vec = g.steps(ctx, "d_vec", ["rc"] + [f"{x}{t}" for t in ts for x in ("cq", "ck")] + ["posf"] + names("ang{}", NT)
                      + ["n0", "n1", "n2", "n3"] + [f"r{j}{i}" for j in range(2) for i in range(3)] + ["shift", "cl0", "cl1"]
                      + [f"{x}{t}" for t in ts for x in ("red", "rn", "nq", "c1_", "s2_", "c2_", "s1_", "o1_", "o2_")]
                      + [x for u in units for x in ([f"ov{u - 3}"] if u >= 3 else []) + [f"mx{u}", f"ng{u}"] + ([f"rs{u - 1}"] if u else [])] + [f"rs{len(units) - 1}", f"ov{len(units) - 3}", f"ov{len(units) - 2}", f"ov{len(units) - 1}"])
        pool = g.steps(ctx, "d_pool", names("nw{}", NT))
        outs = [f"{x}{t}" for t in ts for x in ("q0_", "q1_", "kv0_", "kv1_")]
        tqs = [f"tq{t}{j}" for t in ts for j in range(4)]
        pe_names = names("ct{}", 3) + outs[0:4]
        for t in ts:
            pe_names += outs[4 * (t + 1):4 * (t + 2)] + tqs[4 * t:4 * t + 4]
        pe_names += ["s0", "s1"]
        for u in units:
            pe_names += ([f"s{u + 2}"] if u + 2 < len(units) else []) + [f"pt{u}"] + ([f"o{u - 1}"] if u else [])
        pe_names += [f"o{len(units) - 1}"] + names("ot{}", 4)
        pe = g.steps(ctx, "d_pe", pe_names)
        block = ctx.enter_context(nc.Block())
        ps = g.ps
        last = len(units) - 1

        @block.sync
        def _(sp):
            sp.dma_start(g.w_q[:, :, :], g.a["w_q_up"][0].rearrange("(k p) n -> p k n", p=P)).then_inc(w_in, 16)
            sp.dma_start(g.w_kv[:, :], g.a["w_kv_up"][0]).then_inc(w_in, 16)
            for i in range(GA, GA + RING):
                load_chunk(g, sp, i)

        @block.tensor
        def _(te):
            for j in range(3):
                te.wait_ge(*vec.at("ck3" if j == 2 else "cq3"))
                for t in ts:
                    mm = te.transpose(ps[j][:, P * t:P * t + P], g.cn[:, t, P * j:P * j + P], g.ident[:, :])
                mm.then_inc(*pe(f"ct{j}"))

            def up(t):
                at = slice(P * t, P * t + P)
                for i in range(2):
                    if t:
                        te.wait_ge(*act.at(f"q{i}_{t - 1}"))
                    else:
                        te.wait_ge(*act.at("ct2"))
                    for k in range(2):
                        mm = te.matmul(ps[i][:, 0:384], g.cT[:, k, at], g.w_q[:, k, 384 * i:384 * i + 384], start=(k == 0), stop=(k == 1))
                    mm.then_inc(*pe(f"q{i}_{t}"))
                for i in range(2):
                    if t:
                        te.wait_ge(*act.at(f"vv{i}_{t - 1}"))
                    te.matmul(ps[2 + i][:, :], g.cT[:, 2, at], g.w_kv[:, 512 * i:512 * i + 512], start=True, stop=True).then_inc(*pe(f"kv{i}_{t}"))

            te.wait_ge(w_in, 32)
            up(0)
            for t in ts:
                if t + 1 < NT:
                    up(t + 1)
                te.wait_ge(*vec.at(f"o2_{t}"))
                for j in range(4):
                    if t:
                        te.wait_ge(*act.at(f"tq{t - 1}{j}"))
                    for h in range(4):
                        mm = te.transpose(ps[4 + j][0:QK, P * h:P * h + P], g.qk[:, t % 2, 4 * j + h, :], g.ident[:, :])
                    mm.then_inc(*pe(f"tq{t}{j}"))

            def scores(u):
                qt, h = u // HEADS, u % HEADS
                if u >= 3:
                    te.wait_ge(*act.at(f"ex{u - 3}"))
                bank, n = ps[u % 3], P * (qt + 1)
                te.matmul(bank[:, 0:n], qkT[0][:, h, P * qt:n], qkT[1][:, h, 0:n], start=True, stop=False)
                te.matmul(bank[:, n - P:n], g.ident[:, :], g.causal[:, :], start=False, stop=True).then_inc(*pe(f"s{u}"))

            def turn(u):
                qt = u // HEADS
                te.wait_ge(*act.at(f"ex{u}"))
                if u >= 2:
                    te.wait_ge(*act.at(f"pc{u - 2}"))
                for kt in range(qt + 1):
                    mm = te.transpose(ps[3 + u % 2][:, P * kt:P * kt + P], prob[:, u % 3, P * kt:P * kt + P], g.ident[:, :])
                mm.then_inc(*pe(f"pt{u}"))

            def values(u):
                qt, h = u // HEADS, u % HEADS
                te.wait_ge(*act.at(f"pc{u}"))
                if u >= 2:
                    te.wait_ge(*vec.at(f"ov{u - 2}"))
                for kt in range(qt + 1):
                    mm = te.matmul(ps[5 + u % 2][:, 0:DV], g.probT[:, u % 2, P * kt:P * kt + P], g.v_tok[:, kt, DV * h:DV * h + DV],
                                   start=(kt == 0), stop=(kt == qt))
                mm.then_inc(*pe(f"o{u}"))

            te.wait_ge(*act.at("tq33"))
            scores(0)
            scores(1)
            for u in units:
                if u + 2 <= last:
                    scores(u + 2)
                turn(u)
                if u:
                    values(u - 1)
            values(last)
            te.wait_ge(*vec.at(f"ov{last}"))
            for j in range(4):
                for t in ts:
                    mm = te.transpose(ps[j][:, P * t:P * t + P], g.o_tok[:, t, P * j:P * j + P], g.ident[:, :])
                mm.then_inc(*pe(f"ot{j}"))

        @block.gpsimd
        def _(po):
            for t in ts:
                po.wait_ge(*vec.at(f"nq{t}"))
                x = g.qk[:, t % 2, :, :].rearrange("p (a h) n -> p a h n", a=2)
                for i in range(1):
                    w = g.qk_w[:, :, :].unsqueeze(2).broadcast_to([P, 2, HEADS, QK])
                    po.tensor_tensor(x, x, w, ALU.mult).then_inc(*pool(f"nw{t}"))

        @block.scalar
        def _(sc):
            for t in ts:
                for n, lo, hi, i in (("sqq", 0, Q_LORA, 0), ("sqk", Q_LORA, Q_LORA + KV_LORA, 1)):
                    if t or i:
                        sc.wait_ge(*act.at(f"sqq{t}" if i else f"sqk{t - 1}"))
                    sc.activation(g.junk2[:, 0:hi - lo], g.mla_in[:, t, lo:hi], ACT.Square, accum_out=g.ss2[:, t, i:i + 1]).then_inc(*act(f"{n}{t}"))
            sc.wait_ge(*act.at("sqk3"))
            for i, n, k in ((0, "stq", Q_LORA), (1, "stk", KV_LORA)):
                sc.activation(g.ss2[:, :, i], g.ss2[:, :, i], ACT.Sqrt, bias=g.eps[:, 0:1], scale=1.0 / k).then_inc(*act(n))
            for j in range(3):
                sc.wait_ge(*pe.at(f"ct{j}"))
                w = g.col("q_a_norm_w", j) if j < 2 else g.col("kv_a_norm_w")
                sc.activation(g.cT[:, j, :], ps[j][:, :], ACT.Copy, scale=w).then_inc(*act(f"ct{j}"))
            sc.wait_ge(*vec.at("cl1"))
            sc.activation(g.trig[:, :, :, :], g.turns[:, :, :, :], ACT.Sin).then_inc(*act("sin"))

            def turned(t):
                for j in range(4):
                    sc.wait_ge(*pe.at(f"tq{t}{j}"))
                    dst = qkT[j // 2][:, 4 * (j % 2):4 * (j % 2) + 4, P * t:P * t + P]
                    sc.copy(dst, ps[4 + j][0:QK, :].rearrange("p (h n) -> p h n", h=4)).then_inc(*act(f"tq{t}{j}"))

            for t in ts:
                x = g.qk[:, t % 2, :, :]
                if t >= 2:
                    sc.wait_ge(*pe.at(f"tq{t - 2}3"))
                for i in range(2):
                    sc.wait_ge(*pe.at(f"q{i}_{t}"))
                    sc.copy(x[:, 4 * i:4 * i + 4, :], ps[i][:, 0:384].rearrange("p (h n) -> p h n", h=4)).then_inc(*act(f"q{i}_{t}"))
                for i in range(2):
                    kv = ps[2 + i][:, :].rearrange("p (h n) -> p h n", h=4)
                    sc.wait_ge(*pe.at(f"kv{i}_{t}"))
                    sc.copy(x[:, 8 + 4 * i:12 + 4 * i, 0:NOPE], kv[:, :, 0:NOPE]).then_inc(*act(f"kn{i}_{t}"))
                    sc.copy(g.v_tok[:, t, 256 * i:256 * i + 256].rearrange("p (h n) -> p h n", h=4), kv[:, :, NOPE:]).then_inc(*act(f"vv{i}_{t}"))
                kr = g.mla_in[:, t:t + 1, Q_LORA + KV_LORA:].broadcast_to([P, HEADS, ROPE])
                sc.copy(x[:, 8:16, NOPE:QK], kr).then_inc(*act(f"kr{t}"))
                sc.wait_ge(*act.at(f"kr{t}"))
                if t:
                    sc.wait_ge(*vec.at(f"red{t - 1}"))
                sc.activation(g.sqk[:, :, :], x, ACT.Square).then_inc(*act(f"sq{t}"))
                sc.wait_ge(*vec.at(f"red{t}"))
                sc.activation(g.ssn[:, t, :], g.ssn[:, t, :], ACT.Sqrt, bias=g.eps[:, 0:1], scale=1.0 / QK).then_inc(*act(f"sn{t}"))
                if t:
                    turned(t - 1)
            turned(NT - 1)

            def probs_copy(u):
                n = P * (u // HEADS + 1)
                sc.wait_ge(*pe.at(f"pt{u}"))
                if u >= 2:
                    sc.wait_ge(*pe.at(f"o{u - 2}"))
                sc.copy(g.probT[:, u % 2, 0:n], ps[3 + u % 2][:, 0:n]).then_inc(*act(f"pc{u}"))

            for u in units:
                n = P * (u // HEADS + 1)
                sc.wait_ge(*vec.at(f"ng{u}"))
                sc.activation(prob[:, u % 3, 0:n], ps[u % 3][:, 0:n], ACT.Exp, bias=negs[:, u:u + 1], scale=SCALE,
                              accum_out=sums[:, u:u + 1]).then_inc(*act(f"ex{u}"))
                if u:
                    probs_copy(u - 1)
            probs_copy(last)
            for j in range(4):
                sc.wait_ge(*pe.at(f"ot{j}"))
                sc.copy(g.oT[:, j, :], ps[j][:, :]).then_inc(*act(f"ot{j}"))

        @block.vector
        def _(ve):
            ve.wait_ge(*act.at("stk"))
            ve.reciprocal(g.ss2[:, :, :], g.ss2[:, :, :]).then_inc(*vec("rc"))
            ve.wait_ge(*vec.at("rc"))
            for t in ts:
                for n, lo, hi, i in (("cq", 0, Q_LORA, 0), ("ck", Q_LORA, Q_LORA + KV_LORA, 1)):
                    ve.tensor_scalar(g.cn[:, t, lo:hi], g.mla_in[:, t, lo:hi], g.ss2[:, t, i:i + 1], None, ALU.mult).then_inc(*vec(f"{n}{t}"))
            ve.tensor_copy(g.posf[:, :], g.pos[:, :]).then_inc(*vec("posf"))
            ve.wait_ge(*vec.at("posf"))
            for t in ts:
                ve.tensor_scalar(g.ang[:, t, :], g.freq[:, :], g.posf[:, t:t + 1], None, ALU.mult).then_inc(*vec(f"ang{t}"))
            ve.wait_ge(*vec.at("ang3"))
            ve.tensor_scalar(g.turns[:, 0, :, :], g.ang[:, :, :], 1.0 / TWO_PI, 0.25, ALU.mult, ALU.add).then_inc(*vec("n0"))
            ve.tensor_scalar(g.turns[:, 1, :, :], g.ang[:, :, :], 1.0 / TWO_PI, None, ALU.mult).then_inc(*vec("n1"))
            ve.wait_ge(*vec.at("n1"))
            ve.tensor_scalar(g.turns[:, :, :, :], g.turns[:, :, :, :], ROUND, None, ALU.add).then_inc(*vec("n2"))
            ve.wait_ge(*vec.at("n2"))
            ve.tensor_scalar(g.turns[:, :, :, :], g.turns[:, :, :, :], -ROUND, None, ALU.add).then_inc(*vec("n3"))
            ve.wait_ge(*vec.at("n3"))
            for j in range(2):
                rest = g.ang[:, :, :]
                for i, part in enumerate(TURN_PARTS):
                    dst = g.trig[:, j, :, :]
                    ve.scalar_tensor_tensor(dst, g.turns[:, j, :, :], -part, rest, ALU.mult, ALU.add).then_inc(*vec(f"r{j}{i}"))
                    ve.wait_ge(*vec.at(f"r{j}{i}"))
                    rest = dst
            ve.tensor_scalar(g.trig[:, 0, :, :], g.trig[:, 0, :, :], TWO_PI / 4, None, ALU.add).then_inc(*vec("shift"))
            ve.wait_ge(*vec.at("shift"))
            ve.tensor_scalar(g.turns[:, :, :, :], g.trig[:, :, :, :], PI_BELOW, None, ALU.min).then_inc(*vec("cl0"))
            ve.wait_ge(*vec.at("cl0"))
            ve.tensor_scalar(g.turns[:, :, :, :], g.turns[:, :, :, :], -PI_BELOW, None, ALU.max).then_inc(*vec("cl1"))
            for t in ts:
                x = g.qk[:, t % 2, :, :]
                ve.wait_ge(*act.at(f"sq{t}"))
                ve.tensor_reduce(g.ssn[:, t, :], g.sqk[:, :, :], AX_X, ALU.add).then_inc(*vec(f"red{t}"))
                ve.wait_ge(*act.at(f"sn{t}"))
                ve.reciprocal(g.ssn[:, t, :], g.ssn[:, t, :]).then_inc(*vec(f"rn{t}"))
                ve.wait_ge(*vec.at(f"rn{t}"))
                ve.tensor_tensor(x, x, g.ssn[:, t, :].unsqueeze(2).broadcast_to([P, 2 * HEADS, QK]), ALU.mult).then_inc(*vec(f"nq{t}"))
                ve.wait_ge(*pool.at(f"nw{t}"))
                ve.wait_ge(*act.at("sin"))
                x1, x2 = x[:, :, NOPE:NOPE + HALF], x[:, :, NOPE + HALF:QK]
                cos, sin = (g.trig[:, i, t:t + 1, :].broadcast_to([P, 2 * HEADS, HALF]) for i in range(2))
                tmp = [g.rope[:, t % 2, i, :, :] for i in range(4)]
                for i, (n, xx, f) in enumerate((("c1_", x1, cos), ("s2_", x2, sin), ("c2_", x2, cos), ("s1_", x1, sin))):
                    ve.tensor_tensor(tmp[i], xx, f, ALU.mult).then_inc(*vec(f"{n}{t}"))
                ve.wait_ge(*vec.at(f"s1_{t}"))
                ve.tensor_tensor(x1, tmp[0], tmp[1], ALU.subtract).then_inc(*vec(f"o1_{t}"))
                ve.tensor_tensor(x2, tmp[2], tmp[3], ALU.add).then_inc(*vec(f"o2_{t}"))

            def output(u):
                qt, h = u // HEADS, u % HEADS
                ve.wait_ge(*pe.at(f"o{u}"))
                ve.wait_ge(*vec.at(f"rs{u}"))
                ve.tensor_scalar(g.o_tok[:, qt, DV * h:DV * h + DV], ps[5 + u % 2][:, 0:DV], rsums[:, u:u + 1], None, ALU.mult).then_inc(*vec(f"ov{u}"))

            def inverse(u):
                ve.wait_ge(*act.at(f"ex{u}"))
                ve.reciprocal(rsums[:, u:u + 1], sums[:, u:u + 1]).then_inc(*vec(f"rs{u}"))

            for u in units:
                if u >= 3:
                    output(u - 3)
                ve.wait_ge(*pe.at(f"s{u}"))
                ve.tensor_reduce(maxs[:, u:u + 1], ps[u % 3][:, 0:P * (u // HEADS + 1)], AX_X, ALU.max).then_inc(*vec(f"mx{u}"))
                ve.wait_ge(*vec.at(f"mx{u}"))
                ve.tensor_scalar(negs[:, u:u + 1], maxs[:, u:u + 1], -SCALE, None, ALU.mult).then_inc(*vec(f"ng{u}"))
                if u:
                    inverse(u - 1)
            inverse(last)
            output(last - 2)
            output(last - 1)
            output(last)


def phase_output(nc, g):
    with ExitStack() as ctx:
        (g.merged, g.sig_b, g.gated) = g.sb(ctx, merged=([P, KD, SEQ], F32), sig_b=([P, KD, SEQ], F32), gated=([P, 2, 512], F32))
        ks, ts = range(KD), range(NT)
        rows_in = g.sem(ctx, "rows_back")
        tiles = [f"{x}{i}" for x in ("ga", "oa", "gb", "ob") for i in ks] + [f"w{t}{n}" for n in range(2) for t in ts]
        pe = g.steps(ctx, "e_pe", tiles)
        act = g.steps(ctx, "e_act", tiles[0:8] + tiles[16:24])
        vec = g.steps(ctx, "e_vec", tiles[8:16] + [x for i in ks for x in (f"ob{i}", f"m{i}")] + [x for n in tiles[32:] for x in (n, f"x_{n}")])
        block = ctx.enter_context(nc.Block())
        bank = {n: g.ps[j % 8] for j, n in enumerate(tiles)}
        reader = {n: (act if n[0] == "g" else vec) for n in tiles}

        @block.sync
        def _(sp):
            sp.dma_start(g.x[:, :, :], g.a["x"][0].rearrange("(t p) d -> p t d", p=P)).then_inc(rows_in, 16)
            sp.dma_start(g.mod[:, :, :], g.mod_rows.partition_broadcast(P).rearrange("p a r n -> p (a r) n")).then_inc(rows_in, 16)
            for i, last in ((GA, "ga3"), (GA + 1, "ga7"), (OA, "oa7"), (GB, "gb3"), (GB + 1, "gb7")):
                sp.wait_ge(*pe.at(last))
                load_chunk(g, sp, i + RING)

        @block.tensor
        def _(te):
            def product(name, pairs):
                j = tiles.index(name)
                if j >= 8:
                    te.wait_ge(*reader[tiles[j - 8]].at(tiles[j - 8]))
                for n, (lhsT, rhs) in enumerate(pairs):
                    mm = te.matmul(bank[name][:, :], lhsT, rhs, start=(n == 0), stop=(n == len(pairs) - 1))
                mm.then_inc(*pe(name))

            for x, gate, o, src in (("a", GA, OA, g.oT), ("b", GB, OB, g.yT)):
                for i in ks:
                    te.wait_ge(*chunk_loaded(g, gate + i // 4))
                    w = slot(g, gate + i // 4)
                    product(f"g{x}{i}", [(w[:, k, P * (i % 4):P * (i % 4) + P], g.hT[:, k, :]) for k in ks])
                te.wait_ge(*chunk_loaded(g, o))
                for i in ks:
                    product(f"o{x}{i}", [(slot(g, o)[:, k, P * i:P * i + P], src[:, k, :]) for k in range(FT)])
            te.wait_ge(*vec.at("m7"))
            for n in range(2):
                te.wait_ge(*chunk_loaded(g, WOUT + n))
                for t in ts:
                    product(f"w{t}{n}", [(g.merged[:, k, P * t:P * t + P], slot(g, WOUT + n)[:, k, :]) for k in ks])

        @block.scalar
        def _(sc):
            for x, dst in (("ga", g.merged), ("gb", g.sig_b)):
                for i in ks:
                    sc.wait_ge(*pe.at(f"{x}{i}"))
                    sc.activation(dst[:, i, :], bank[f"{x}{i}"][:, :], ACT.Sigmoid).then_inc(*act(f"{x}{i}"))

        @block.vector
        def _(ve):
            for i in ks:
                ve.wait_ge(*pe.at(f"oa{i}"))
                ve.wait_ge(*act.at(f"ga{i}"))
                ve.tensor_tensor(g.merged[:, i, :], bank[f"oa{i}"][:, :], g.merged[:, i, :], ALU.mult).then_inc(*vec(f"oa{i}"))
            for i in ks:
                ve.wait_ge(*pe.at(f"ob{i}"))
                ve.wait_ge(*act.at(f"gb{i}"))
                ve.tensor_tensor(g.sig_b[:, i, :], bank[f"ob{i}"][:, :], g.sig_b[:, i, :], ALU.mult).then_inc(*vec(f"ob{i}"))
                ve.wait_ge(*vec.at(f"ob{i}"))
                ve.tensor_tensor(g.merged[:, i, :], g.merged[:, i, :], g.sig_b[:, i, :], ALU.add).then_inc(*vec(f"m{i}"))
            ve.wait_ge(rows_in, 32)
            for j, name in enumerate(tiles[32:]):
                t, at = int(name[1]), slice(512 * int(name[2]), 512 * int(name[2]) + 512)
                ve.wait_ge(*pe.at(name))
                if j >= 2:
                    ve.wait_ge(*vec.at(f"x_{tiles[32 + j - 2]}"))
                ve.tensor_tensor(g.gated[:, j % 2, :], bank[name][:, :], g.mod[:, 0, at], ALU.mult).then_inc(*vec(name))
                ve.wait_ge(*vec.at(name))
                ve.tensor_tensor(g.x[:, t, at], g.x[:, t, at], g.gated[:, j % 2, :], ALU.add).then_inc(*vec(f"x_{name}"))


class Turns:

    def __init__(self, sem, order):
        self.sem, self.place, self.n, self.done = sem, {s: i + 1 for i, s in enumerate(order)}, len(order), 0
        assert len(self.place) == self.n

    def __call__(self, name):
        self.done += 1
        assert self.place[name] == self.done, (name, self.place[name], self.done)
        return self.sem, 1

    def credit(self):
        return self.sem, self.n

    def at(self, name, turn):
        return self.sem, self.n * turn + (self.n + self.place[name])

    def before(self, name, turn):
        return self.sem, self.n * turn + self.place[name]


FAR = 100000.0


def phase_route(nc, g):
    with ExitStack() as ctx:
        area = g.w_raw[:, :, :].rearrange("p a n -> p (a n)")
        h2 = area[:, 0:NT * D].rearrange("p (t d) -> p t d", t=NT)
        h2T = area[:, NT * D:2 * NT * D].rearrange("p (k n) -> p k n", k=KD)
        rows = g.acc[:, :, :].rearrange("p a n -> p (a n)")
        rank, maskT, wT = (rows[0:N_EXP, 512 * i:512 * i + 512] for i in range(3))
        block_sum, job_end, oh_lt, twice = (rows[0:64, 1536 + 64 * i:1600 + 64 * i] for i in range(4))
        counts = rows[0:64, 1792:1856]
        choice = rows[:, 2048:2560].rearrange("p (t k e) -> p t k e", t=NT, k=TOP_K)
        chosen = rows[:, 2560:3072].rearrange("p (t k e) -> p t k e", t=NT, k=TOP_K)
        mask = rows[:, 3072:3328].rearrange("p (t a e) -> p t a e", t=NT, a=2)
        weight = rows[:, 3328:3456].rearrange("p (t e) -> p t e", t=NT)
        logits = rows[:, 3456:3584].rearrange("p (t e) -> p t e", t=NT)
        ss, rstd = rows[:, 3584:3588], rows[:, 3588:3592]
        top = rows[:, 3592:3624].rearrange("p (t k) -> p t k", t=NT)
        idx = rows[:, 3624:3640].rearrange("p (t k) -> p t k", t=NT)
        neg, total, inv = rows[:, 3640:3644], rows[:, 3644:3648], rows[:, 3648:3652]
        ex = rows[:, 3652:3668].rearrange("p (t k) -> p t k", t=NT)
        prob = rows[:, 3668:3684].rearrange("p (t k) -> p t k", t=NT)
        square = g.mod[:, 0, :]
        (g.top_i, g.bias_raw) = g.sb(ctx, top_i=([P, NT, 8], U32), bias_raw=([2 * N_EXP, 2 * D_FF + D], F32))
        ts, ks = range(NT), range(KD)
        pe = g.steps(ctx, "f_pe", names("h{}", KD) + ["lg", "rank", "count", "maskT", "wT", "js", "table", "total"]
                     + names("slot{}", NT) + names("weight{}", NT))
        act = g.steps(ctx, "f_act", names("sq{}", NT) + ["std"] + [f"hi{t}" for t in ts] + names("h{}", KD)[0::2] + names("ex{}", NT))
        vec = g.steps(ctx, "f_vec", ["rstd"] + [x for t in ts for x in (f"g{t}", f"s{t}")] + names("h{}", KD)[1::2] + ["lg"]
                      + names("max{}", NT) + names("mi{}", NT) + ["idx", "neg", "inv", "prob", "choice", "chosen", "mask", "mask2", "weight"]
                      + ["later2a", "later2b", "counts", "b0", "b1", "b2", "b3", "maskT", "wT", "js", "rank", "jg", "je", "lt", "table",
                         "rm", "rf", "tab", "nb"] + names("slot{}", NT) + names("weight{}", NT) + ["zero", "bias_hi", "bias_lo"])
        pool = g.steps(ctx, "f_pool", names("lo{}", NT))
        bias_in = g.sem(ctx, "bias_in")
        block = ctx.enter_context(nc.Block())
        ps = g.ps

        @block.sync
        def _(sp):
            for i in range(2):
                at = slice(N_EXP * i, N_EXP * i + N_EXP)
                sp.dma_start(g.bias_raw[at, 0:2 * D_FF], g.a["b_gate_up"][0]).then_inc(bias_in, 16)
                sp.dma_start(g.bias_raw[at, 2 * D_FF:], g.a["b_down"][0]).then_inc(bias_in, 16)

        @block.gpsimd
        def _(po):
            for t in ts:
                po.wait_ge(*act.at(f"hi{t}"))
                po.tensor_tensor(g.h2_lo[:, t, :], h2[:, t, :], g.h2_hi[:, t, :].bitcast(F32), ALU.subtract).then_inc(*pool(f"lo{t}"))

        @block.scalar
        def _(sc):
            for t in ts:
                if t:
                    sc.wait_ge(*act.at(f"sq{t - 1}"))
                sc.activation(square, g.x[:, t, :], ACT.Square, accum_out=ss[:, t:t + 1]).then_inc(*act(f"sq{t}"))
            sc.wait_ge(*act.at("sq3"))
            sc.activation(rstd, ss, ACT.Sqrt, bias=g.eps[:, 0:1], scale=1.0 / D).then_inc(*act("std"))
            for t in ts:
                sc.wait_ge(*vec.at(f"s{t}"))
                sc.copy(g.h2_hi[:, t, :], h2[:, t, :]).then_inc(*act(f"hi{t}"))
            for k in ks[0::2]:
                sc.wait_ge(*pe.at(f"h{k}"))
                sc.copy(h2T[:, k, :], ps[k][:, :]).then_inc(*act(f"h{k}"))
            sc.wait_ge(*vec.at("neg"))
            for t in ts:
                sc.activation(ex[:, t, :], top[:, t, 0:TOP_K], ACT.Exp, bias=neg[:, t:t + 1], accum_out=total[:, t:t + 1]).then_inc(*act(f"ex{t}"))

        @block.tensor
        def _(te):
            te.wait_ge(*vec.at("s3"))
            for k in ks:
                for t in ts:
                    mm = te.transpose(ps[k][:, P * t:P * t + P], h2[:, t, P * k:P * k + P], g.ident[:, :])
                mm.then_inc(*pe(f"h{k}"))
            te.wait_ge(*act.at("h6"))
            te.wait_ge(*vec.at("h7"))
            for t in ts:
                for k in ks:
                    mm = te.matmul(ps[0][:, N_EXP * t:N_EXP * t + N_EXP], h2T[:, k, P * t:P * t + P], g.w_router[:, k, :], start=(k == 0), stop=(k == KD - 1))
            mm.then_inc(*pe("lg"))
            te.wait_ge(*vec.at("mask"))
            for t in ts:
                for s in range(t + 1):
                    mm = te.matmul(ps[1][0:N_EXP, P * t:P * t + P], mask[:, s, 0, :], g.later[:, :] if s == t else g.ones[:, :],
                                   start=(s == 0), stop=(s == t))
            mm.then_inc(*pe("rank"))
            te.wait_ge(*vec.at("mask2"))
            for t in ts:
                mm = te.matmul(ps[2][0:64, 0:64], mask[:, t, :, :].rearrange("p a e -> p (a e)"), g.ones[:, 0:64], start=(t == 0), stop=(t == NT - 1))
            mm.then_inc(*pe("count"))
            for t in ts:
                mm = te.transpose(ps[3][0:N_EXP, P * t:P * t + P], mask[:, t, 0, :], g.ident[:, :])
            mm.then_inc(*pe("maskT"))
            te.wait_ge(*vec.at("weight"))
            for t in ts:
                mm = te.transpose(ps[4][0:N_EXP, P * t:P * t + P], weight[:, t, :], g.ident[:, :])
            mm.then_inc(*pe("wT"))
            te.wait_ge(*vec.at("b3"))
            te.wait_ge(*vec.at("later2b"))
            te.matmul(ps[5][0:64, 0:64], twice[0:N_EXP, :], block_sum[0:N_EXP, :], start=True, stop=True).then_inc(*pe("js"))
            te.wait_ge(*vec.at("table"))
            te.matmul(ps[6][0:1, 0:64], g.iota_part[0:N_EXP, 0:1], g.job_of[0:N_EXP, :], start=True, stop=True).then_inc(*pe("table"))
            te.matmul(ps[7][0:1, 0:64], g.ones[0:N_EXP, 0:1], block_sum[0:N_EXP, :], start=True, stop=True).then_inc(*pe("total"))
            te.wait_ge(*vec.at("rf"))
            te.wait_ge(*vec.at("wT"))
            for x, src, banks in (("slot", rank, (0, 1, 2, 3)), ("weight", wT, (4, 5, 0, 1))):
                for t in ts:
                    if x == "weight" and t >= 2:
                        te.wait_ge(*vec.at(f"slot{t - 2}"))
                    te.matmul(ps[banks[t]][:, 0:64], src[:, P * t:P * t + P], g.job_of[0:N_EXP, :], start=True, stop=True).then_inc(*pe(f"{x}{t}"))

        @block.vector
        def _(ve):
            def then(ins, name):
                ins.then_inc(*vec(name))
                ve.wait_ge(*vec.at(name))

            ve.wait_ge(*act.at("std"))
            then(ve.reciprocal(rstd, rstd), "rstd")
            for t in ts:
                then(ve.scalar_tensor_tensor(h2[:, t, :], g.x[:, t, :], rstd[:, t:t + 1], g.mod[:, 2, :], ALU.mult, ALU.mult), f"g{t}")
                ve.tensor_tensor(h2[:, t, :], h2[:, t, :], g.mod[:, 1, :], ALU.add).then_inc(*vec(f"s{t}"))
            for k in ks[1::2]:
                ve.wait_ge(*pe.at(f"h{k}"))
                ve.tensor_copy(h2T[:, k, :], ps[k][:, :]).then_inc(*vec(f"h{k}"))
            ve.wait_ge(*pe.at("lg"))
            then(ve.tensor_tensor(logits, ps[0][:, 0:N_EXP * NT].rearrange("p (t e) -> p t e", t=NT),
                                  g.b_router[:, :].unsqueeze(1).broadcast_to([P, NT, N_EXP]), ALU.add), "lg")
            for t in ts:
                ve.max(top[:, t, :], logits[:, t, :]).then_inc(*vec(f"max{t}"))
            ve.wait_ge(*vec.at("max3"))
            for t in ts:
                ve.max_index(g.top_i[:, t, :], top[:, t, :], logits[:, t, :]).then_inc(*vec(f"mi{t}"))
            ve.wait_ge(*vec.at("mi3"))
            ve.tensor_copy(idx, g.top_i[:, :, 0:TOP_K]).then_inc(*vec("idx"))
            ve.tensor_scalar(neg, top[:, :, 0], -1.0, None, ALU.mult).then_inc(*vec("neg"))
            ve.wait_ge(*act.at("ex3"))
            then(ve.reciprocal(inv, total), "inv")
            then(ve.tensor_tensor(prob, ex, inv.unsqueeze(2).broadcast_to([P, NT, TOP_K]), ALU.mult), "prob")
            experts = g.iota_row[:, 0:N_EXP].unsqueeze(1).unsqueeze(1).broadcast_to([P, NT, TOP_K, N_EXP])
            wide = lambda x: x.unsqueeze(3).broadcast_to([P, NT, TOP_K, N_EXP])
            then(ve.tensor_tensor(choice, experts, wide(idx), ALU.is_equal), "choice")
            ve.tensor_tensor(chosen, choice, wide(prob), ALU.mult).then_inc(*vec("chosen"))
            then(ve.tensor_reduce(mask[:, :, 0, :], choice.rearrange("p t k e -> p t e k"), AX_X, ALU.add), "mask")
            ve.tensor_copy(mask[:, :, 1, :], mask[:, :, 0, :]).then_inc(*vec("mask2"))
            ve.tensor_reduce(weight, chosen.rearrange("p t k e -> p t e k"), AX_X, ALU.add).then_inc(*vec("weight"))
            ve.tensor_copy(twice[0:N_EXP, 0:N_EXP], g.later[0:N_EXP, 0:N_EXP]).then_inc(*vec("later2a"))
            ve.tensor_copy(twice[0:N_EXP, N_EXP:64], g.later[0:N_EXP, 0:N_EXP]).then_inc(*vec("later2b"))
            ve.wait_ge(*pe.at("count"))
            then(ve.tensor_copy(counts, ps[2][0:64, 0:64]), "counts")
            then(ve.tensor_scalar(block_sum, counts, 0.0, None, ALU.is_gt), "b0")
            for i in range(1, NT):
                then(ve.scalar_tensor_tensor(block_sum, counts, float(P * i), block_sum, ALU.is_gt, ALU.add), f"b{i}")
            ve.wait_ge(*pe.at("maskT"))
            ve.tensor_copy(maskT, ps[3][0:N_EXP, :]).then_inc(*vec("maskT"))
            ve.wait_ge(*pe.at("wT"))
            ve.tensor_copy(wT, ps[4][0:N_EXP, :]).then_inc(*vec("wT"))
            ve.wait_ge(*pe.at("js"))
            then(ve.tensor_copy(job_end, ps[5][0:64, 0:64]), "js")
            ve.wait_ge(*pe.at("rank"))
            ve.scalar_tensor_tensor(rank, job_end[0:N_EXP, 0:1].broadcast_to([N_EXP, SEQ]), float(P), ps[1][0:N_EXP, :], ALU.mult, ALU.add).then_inc(*vec("rank"))
            jobs = g.iota_row[0:64, 0:JOBS]
            then(ve.tensor_tensor(oh_lt, jobs, job_end, ALU.is_ge), "jg")
            then(ve.tensor_tensor(job_end, job_end, block_sum, ALU.add), "je")
            then(ve.tensor_tensor(job_end, jobs, job_end, ALU.is_lt), "lt")
            ve.tensor_tensor(g.job_of[:, :], oh_lt, job_end, ALU.mult).then_inc(*vec("table"))
            then(ve.scalar_tensor_tensor(rank, rank, FAR, maskT, ALU.add, ALU.mult), "rm")
            ve.tensor_scalar(rank, rank, -FAR, None, ALU.add).then_inc(*vec("rf"))
            ve.wait_ge(*pe.at("table"))
            ve.tensor_copy(g.table[0:1, 1:1 + JOBS], ps[6][0:1, 0:JOBS]).then_inc(*vec("tab"))
            ve.wait_ge(*pe.at("total"))
            ve.tensor_copy(g.table[0:1, 0:1], ps[7][0:1, 0:1]).then_inc(*vec("nb"))
            for t in ts:
                ve.wait_ge(*pe.at(f"slot{t}"))
                ve.scalar_tensor_tensor(g.slot_of[:, t, :], g.iota_row[:, 0:JOBS], -float(P), ps[t][:, 0:JOBS], ALU.mult, ALU.add).then_inc(*vec(f"slot{t}"))
            for t, b in zip(ts, (4, 5, 0, 1)):
                ve.wait_ge(*pe.at(f"weight{t}"))
                ve.tensor_copy(g.weight_of[:, t, 1:1 + JOBS], ps[b][:, 0:JOBS]).then_inc(*vec(f"weight{t}"))
            ve.memset(g.weight_of[:, :, 0:1], 0.0).then_inc(*vec("zero"))
            ve.wait_ge(bias_in, 16 * 4)
            then(ve.tensor_copy(g.bias[:, :], g.bias_raw[:, :]), "bias_hi")
            ve.tensor_tensor(g.bias[N_EXP:2 * N_EXP, :], g.bias_raw[N_EXP:2 * N_EXP, :], g.bias[N_EXP:2 * N_EXP, :].bitcast(F32), ALU.subtract).then_inc(*vec("bias_lo"))


N_CHUNK, RAW, PARTS = 12, 4, 3
GU, DOWN = 4, 2
MIN_JOBS, MAX_JOBS = SEQ * TOP_K // P, (SEQ * TOP_K + N_EXP * (P - 1)) // P
VEC_ROWS = 3


def phase_experts(nc, g):
    with ExitStack() as ctx:
        split = ([P, PARTS, 4, 512], F32R)
        pair = ([P, KD, P], F32R)
        (g.e_hi, g.e_lo, g.x_hi, g.x_lo, g.a_hi, g.a_lo, g.y_hi, g.y_lo, g.pick, g.pickT, g.bias_pick, g.ident_r) = g.sb(ctx, e_hi=split, e_lo=split, x_hi=pair, x_lo=pair, a_hi=pair, a_lo=pair, y_hi=([P, D], F32R), y_lo=([P, D], F32R),
             pick=([P, NT, P], F32R), pickT=([P, SEQ], F32R), bias_pick=([2 * N_EXP, P], F32R), ident_r=([P, P], F32R))
        ts = range(NT)
        act_out = g.mod[:, 0, :]
        x_slot = act_out
        gate_c, up_c, sig = (g.mod[:, 1 + i // 2, 512 * (i % 2):512 * (i % 2) + 512].rearrange("p (a n) -> p a n", a=2) for i in range(3))
        ps = g.ps
        pe = Turns(g.sem(ctx, "m_pe"), ["w0", "w1", "cb0", "cb1", "w2", "w3", "cb2", "cb3", "tr0", "w4", "w5", "cb4", "cb5", "tr1", "w6", "w7",
                                        "cb6", "cb7", "tr2", "w8", "st", "w9", "tr3", "ga0", "ga1", "w10", "xt0", "xt1", "w11"])
        act = Turns(g.sem(ctx, "m_act"), ["h2", "h3", "h4", "sg0", "h5", "h6", "th0", "sg1", "h7", "h8", "th1", "sg2", "h9", "h10", "th2", "sg3",
                                          "h11", "st", "th3", "h0", "gx0", "gx1", "y0", "xh0", "xh1", "h1", "y1"])
        vec = Turns(g.sem(ctx, "m_vec"), ["gc0", "uc0", "ad0", "ad1", "m0", "ac0", "gc1", "uc1", "ad2", "ad3", "tl0", "m1", "ac1",
                                          "gc2", "uc2", "ad4", "ad5", "tl1", "m2", "ac2", "gc3", "uc3", "ad6", "ad7", "tl2", "m3", "ac3",
                                          "pick0", "pick1", "pick2", "pick3", "bp", "tl3", "y0", "xl0", "xl1", "y1"])
        order = list(range(2, N_CHUNK)) + [0, 1]
        split_done = [g.sem(ctx, f"split_done{i}") for i in range(PARTS)]
        raw_in = [g.sem(ctx, f"raw_in{i}") for i in range(RAW)]
        first_pe = g.steps(ctx, "first_pe", ["ga0", "ga1", "xt0", "xt1"])
        first_act = g.steps(ctx, "first_act", ["gx0", "gx1", "xh0", "xh1", "h0"])
        first_vec = g.steps(ctx, "first_vec", names("pick{}", 4) + names("zero{}", 4) + ["ident", "bp", "xl0"])
        last_pe = g.steps(ctx, "last_pe", names("cb{}", 8))
        last_vec = g.steps(ctx, "last_vec", [x for t in ts for x in (f"ad{2 * t}", f"ad{2 * t + 1}", f"gate{t}")])
        last_pool = g.steps(ctx, "last_pool", names("out{}", NT))
        out_done = g.sem(ctx, "out_done")
        block = ctx.enter_context(nc.Block())

        def job_count(eng):
            return eng.value_load(g.table[0:1, 0:1], min_val=MIN_JOBS, max_val=MAX_JOBS)

        def raw(c):
            return g.w_raw[:, c % RAW, :].rearrange("p (k n) -> p k n", k=4)

        def loaded(c, turn):
            return raw_in[c % RAW], 48 * turn + 16 * (c // RAW + 1 + (3 if c < 2 else 0))

        def is_split(c, turn):
            return split_done[c % PARTS], 8 * turn + 2 * (c // PARTS + 1)

        def slot_left(c, turn):
            n = (c - PARTS) % N_CHUNK
            return pe.before(f"w{n}", turn) if c == 2 else pe.at(f"w{n}", turn)

        def lo_part(eng, c, rows):
            return eng.tensor_tensor(g.e_lo[:, c % PARTS, rows, :], raw(c)[:, rows, :], g.e_hi[:, c % PARTS, rows, :].bitcast(F32), ALU.subtract)

        @block.sync
        def _(sp):
            def load(c, e):
                if c < 2 * GU:
                    half, n, w = c % 2, c // 2, g.a["w_gate_up"]
                else:
                    half, n, w = (c - 2 * GU) // 2, c % 2, g.a["w_down"]
                src = w[0][bass.ds(e, 1), 512 * half:512 * half + 512, 512 * n:512 * n + 512]
                sp.dma_start(raw(c), src.rearrange("a (k p) n -> p (a k) n", p=P)).then_inc(raw_in[c % RAW], 16)

            jobs = job_count(sp)
            first = sp.value_load(g.table[0:1, 1:2], min_val=0, max_val=N_EXP - 1)
            for c in range(RAW):
                load(c, first)
            with sp.Fori(0, jobs) as turn:
                e = sp.value_load(g.table[0:1, bass.ds(turn + 1, 1)], min_val=0, max_val=N_EXP - 1)
                for c in list(range(RAW, N_CHUNK)) + list(range(RAW)):
                    if c == 0:
                        e = sp.value_load(g.table[0:1, bass.ds(turn + 2, 1)], min_val=0, max_val=N_EXP - 1)
                    sp.wait_ge(*is_split((c - RAW) % N_CHUNK, turn))
                    load(c, e)
            for c in (2, 3):
                sp.wait_ge(raw_in[c], 48 * jobs + 16)
            for t in ts:
                sp.wait_ge(*last_pool.at(f"out{t}"))
                sp.dma_start(g.out[0, P * t:P * t + P, :], g.acc[:, t, :]).then_inc(out_done, 16)
            sp.wait_ge(out_done, 16 * NT)

        @block.tensor
        def _(te):
            def gather(i):
                for t in ts:
                    for part in (g.h2_hi, g.h2_lo):
                        mm = te.matmul(ps[i][:, :], g.pick[:, t, :], part[:, t, 512 * i:512 * i + 512],
                                       start=(t == 0 and part is g.h2_hi), stop=(t == NT - 1 and part is g.h2_lo))
                return mm

            def features(i):
                for j in range(4):
                    mm = te.transpose(ps[i][:, P * j:P * j + P], x_slot[:, 512 * i + P * j:512 * i + P * j + P], g.ident[:, :])
                return mm

            def product(c, out, hi, lo, k0, bias, stop, turn):
                te.wait_ge(*is_split(c, turn))
                if bias is not None:
                    te.matmul(out, g.bias_pick[:, :], g.bias[:, bias:bias + 512], start=True, stop=False)
                for k in range(4):
                    w_hi, w_lo = g.e_hi[:, c % PARTS, k, :], g.e_lo[:, c % PARTS, k, :]
                    te.matmul(out, hi[:, k0 + k, :], w_hi, start=False, stop=False)
                    te.matmul(out, hi[:, k0 + k, :], w_lo, start=False, stop=False)
                    mm = te.matmul(out, lo[:, k0 + k, :], w_hi, start=False, stop=(stop and k == 3))
                mm.then_inc(*pe(f"w{c}"))

            def scatter(i):
                t, n = i // 2, i % 2
                te.matmul(ps[6 + n][:, :], g.pickT[:, P * t:P * t + P], g.y_hi[:, 512 * n:512 * n + 512], start=True, stop=False)
                return te.matmul(ps[6 + n][:, :], g.pickT[:, P * t:P * t + P], g.y_lo[:, 512 * n:512 * n + 512], start=False, stop=True)

            def turned(n, turn):
                te.wait_ge(*vec.at(f"ac{n}", turn))
                te.wait_ge(*(vec.at(f"tl{n - 2}", turn) if n >= 2 else vec.before(f"tl{n + 2}", turn)))
                for j in range(2):
                    mm = te.transpose(ps[2 + n % 2][:, P * j:P * j + P], act_out[:, 256 * n + P * j:256 * n + P * j + P], g.ident[:, :])
                mm.then_inc(*pe(f"tr{n}"))

            jobs = job_count(te)
            te.wait_ge(*first_vec.at("pick3"))
            for i in range(2):
                gather(i).then_inc(*first_pe(f"ga{i}"))
            for i in range(2):
                te.wait_ge(*first_act.at(f"gx{i}"))
                features(i).then_inc(*first_pe(f"xt{i}"))
            with te.Fori(0, jobs) as turn:
                te.wait_ge(*vec.before("xl1", turn))
                for n in range(GU):
                    out = ps[n % 2][:, :]
                    if n >= 2:
                        te.wait_ge(*vec.at(f"uc{n - 2}", turn))
                    product(2 * n, out, g.x_hi, g.x_lo, 0, 512 * n, False, turn)
                    product(2 * n + 1, out, g.x_hi, g.x_lo, 4, None, True, turn)
                    for i in (2 * n, 2 * n + 1):
                        if i == 0:
                            te.wait_ge(*vec.before("y1", turn))
                            te.wait_ge(*act.before("st", turn))
                        te.wait_ge(*(vec.at(f"ad{i - 2}", turn) if i >= 2 else vec.before(f"ad{i + 6}", turn)))
                        scatter(i).then_inc(*pe(f"cb{i}"))
                    if n:
                        turned(n - 1, turn)
                te.wait_ge(*vec.at("tl1", turn))
                product(8, ps[4][:, :], g.a_hi, g.a_lo, 0, 2 * D_FF, False, turn)
                te.wait_ge(*vec.at("ad6", turn))
                for t in ts:
                    mm = te.matmul(ps[6][:, P * t:P * t + P], g.pick[:, t, :], g.ident_r[:, :], start=True, stop=True)
                mm.then_inc(*pe("st"))
                product(9, ps[5][:, :], g.a_hi, g.a_lo, 0, 2 * D_FF + 512, False, turn)
                turned(3, turn)
                te.wait_ge(*vec.at("pick3", turn))
                for i in range(2):
                    te.wait_ge(*vec.at(f"uc{i + 2}", turn))
                    gather(i).then_inc(*pe(f"ga{i}"))
                te.wait_ge(*vec.at("tl3", turn))
                product(10, ps[4][:, :], g.a_hi, g.a_lo, 4, None, True, turn)
                for i in range(2):
                    te.wait_ge(*act.at(f"gx{i}", turn))
                    features(i).then_inc(*pe(f"xt{i}"))
                product(11, ps[5][:, :], g.a_hi, g.a_lo, 4, None, True, turn)
            te.wait_ge(*vec.before("y1", jobs))
            te.wait_ge(*act.before("st", jobs))
            for i in range(8):
                te.wait_ge(*(last_vec.at(f"ad{i - 2}") if i >= 2 else vec.before(f"ad{i + 6}", jobs)))
                scatter(i).then_inc(*last_pe(f"cb{i}"))

        @block.scalar
        def _(sc):
            def hi_part(c):
                return sc.copy(g.e_hi[:, c % PARTS, :, :], raw(c))

            def gathered(i):
                return sc.copy(x_slot[:, 512 * i:512 * i + 512], ps[i][:, :])

            def features_hi(i):
                return sc.copy(g.x_hi[:, 4 * i:4 * i + 4, :], ps[i][:, :].rearrange("p (k n) -> p k n", k=4))

            jobs = job_count(sc)
            for i in range(2):
                sc.wait_ge(*first_pe.at(f"ga{i}"))
                gathered(i).then_inc(*first_act(f"gx{i}"))
            for i in range(2):
                sc.wait_ge(*first_pe.at(f"xt{i}"))
                features_hi(i).then_inc(*first_act(f"xh{i}"))
            for c in range(2):
                sc.wait_ge(raw_in[c], 16)
                hi_part(c).then_inc(*(first_act("h0") if c == 0 else act.credit()))
            with sc.Fori(0, jobs) as turn:
                def hi(c):
                    sc.wait_ge(*loaded(c, turn))
                    sc.wait_ge(*slot_left(c, turn))
                    hi_part(c).then_inc(*act(f"h{c}"))

                def sigmoid(n):
                    sc.wait_ge(*vec.at(f"gc{n}", turn))
                    sc.activation(sig[:, n % 2, :], gate_c[:, n % 2, :], ACT.Sigmoid, scale=ALPHA).then_inc(*act(f"sg{n}"))

                def turned_hi(n):
                    sc.wait_ge(*pe.at(f"tr{n}", turn))
                    sc.copy(g.a_hi[:, 2 * n:2 * n + 2, :], ps[2 + n % 2][:, 0:2 * P].rearrange("p (k n) -> p k n", k=2)).then_inc(*act(f"th{n}"))

                def down(n):
                    sc.wait_ge(*pe.at(f"w{10 + n}", turn))
                    sc.copy(g.y_hi[:, 512 * n:512 * n + 512], ps[4 + n][:, :]).then_inc(*act(f"y{n}"))

                hi(2)
                hi(3)
                hi(4)
                sigmoid(0)
                hi(5)
                hi(6)
                turned_hi(0)
                sigmoid(1)
                hi(7)
                hi(8)
                turned_hi(1)
                sigmoid(2)
                hi(9)
                hi(10)
                turned_hi(2)
                sigmoid(3)
                hi(11)
                sc.wait_ge(*pe.at("st", turn))
                sc.copy(g.pickT[:, :], ps[6][:, :]).then_inc(*act("st"))
                turned_hi(3)
                hi(0)
                for i in range(2):
                    sc.wait_ge(*pe.at(f"ga{i}", turn))
                    gathered(i).then_inc(*act(f"gx{i}"))
                down(0)
                for i in range(2):
                    sc.wait_ge(*pe.at(f"xt{i}", turn))
                    features_hi(i).then_inc(*act(f"xh{i}"))
                hi(1)
                down(1)

        @block.gpsimd
        def _(po):
            jobs = job_count(po)
            for c in range(2):
                po.wait_ge(*(first_act.at("h0") if c == 0 else act.credit()))
                lo_part(po, c, slice(VEC_ROWS, 4)).then_inc(split_done[c % PARTS], 1)
            with po.Fori(0, jobs) as turn:
                for c in order:
                    po.wait_ge(*act.at(f"h{c}", turn))
                    lo_part(po, c, slice(VEC_ROWS, 4)).then_inc(split_done[c % PARTS], 1)
            for t in ts:
                po.wait_ge(*last_vec.at(f"gate{t}"))
                po.tensor_tensor(g.acc[:, t, :], g.acc[:, t, :], g.x[:, t, :], ALU.add).then_inc(*last_pool(f"out{t}"))

        @block.vector
        def _(ve):
            def pick(t, job):
                return ve.tensor_scalar(g.pick[:, t, :], g.iota_row[:, :], g.slot_of[:, t, job], None, ALU.is_equal)

            def bias_pick(job):
                return ve.tensor_scalar(g.bias_pick[:, :], g.ones[0:2 * N_EXP, :], g.job_of[:, job], None, ALU.mult)

            def add(i, column):
                t, n = i // 2, i % 2
                at = g.acc[:, t, 512 * n:512 * n + 512]
                return ve.scalar_tensor_tensor(at, ps[6 + n][:, :], g.weight_of[:, t, column], at, ALU.mult, ALU.add)

            def features_lo(i):
                at = slice(4 * i, 4 * i + 4)
                return ve.tensor_tensor(g.x_lo[:, at, :], ps[i][:, :].rearrange("p (k n) -> p k n", k=4), g.x_hi[:, at, :].bitcast(F32), ALU.subtract)

            jobs = job_count(ve)
            for t in ts:
                pick(t, slice(0, 1)).then_inc(*first_vec(f"pick{t}"))
            for i, buf in enumerate((g.acc[:, :, :], g.y_hi[:, :].bitcast(F32), g.y_lo[:, :].bitcast(F32), g.pickT[:, :].bitcast(F32))):
                ve.memset(buf, 0.0).then_inc(*first_vec(f"zero{i}"))
            ve.memset(g.unused[:, :], 0.0).then_inc(*pe.credit())
            ve.tensor_copy(g.ident_r[:, :], g.ident[:, :]).then_inc(*first_vec("ident"))
            bias_pick(slice(0, 1)).then_inc(*first_vec("bp"))
            for i in range(2):
                ve.wait_ge(*first_act.at(f"xh{i}"))
                features_lo(i).then_inc(*(first_vec("xl0") if i == 0 else vec.credit()))
            for c in range(2):
                ve.wait_ge(*(first_act.at("h0") if c == 0 else act.credit()))
                lo_part(ve, c, slice(0, VEC_ROWS)).then_inc(split_done[c % PARTS], 1)
            with ve.Fori(0, jobs) as turn:
                def lo(c):
                    ve.wait_ge(*act.at(f"h{c}", turn))
                    lo_part(ve, c, slice(0, VEC_ROWS)).then_inc(split_done[c % PARTS], 1)

                def clamp(n):
                    both = ps[n % 2][:, :].rearrange("p (n a) -> p n a", a=2)
                    ve.wait_ge(*pe.at(f"w{2 * n + 1}", turn))
                    ve.wait_ge(*(vec.at(f"ac{n - 2}", turn) if n >= 2 else vec.before(f"ac{n + 2}", turn)))
                    ve.tensor_scalar(gate_c[:, n % 2, :], both[:, :, 0], LIMIT, None, ALU.min).then_inc(*vec(f"gc{n}"))
                    ve.tensor_scalar(up_c[:, n % 2, :], both[:, :, 1], LIMIT, -LIMIT, ALU.min, ALU.max).then_inc(*vec(f"uc{n}"))

                def gated(n):
                    up = up_c[:, n % 2, :]
                    ve.wait_ge(*vec.at(f"uc{n}", turn))
                    ve.scalar_tensor_tensor(up, up, 1.0, gate_c[:, n % 2, :], ALU.add, ALU.mult).then_inc(*vec(f"m{n}"))
                    ve.wait_ge(*vec.at(f"m{n}", turn))
                    ve.wait_ge(*act.at(f"sg{n}", turn))
                    ve.tensor_tensor(act_out[:, 256 * n:256 * n + 256], up, sig[:, n % 2, :], ALU.mult).then_inc(*vec(f"ac{n}"))

                def turned_lo(n):
                    ve.wait_ge(*act.at(f"th{n}", turn))
                    at = slice(2 * n, 2 * n + 2)
                    ve.tensor_tensor(g.a_lo[:, at, :], ps[2 + n % 2][:, 0:2 * P].rearrange("p (k n) -> p k n", k=2),
                                     g.a_hi[:, at, :].bitcast(F32), ALU.subtract).then_inc(*vec(f"tl{n}"))

                def added(i):
                    ve.wait_ge(*pe.at(f"cb{i}", turn))
                    add(i, bass.ds(turn, 1)).then_inc(*vec(f"ad{i}"))

                def down(n):
                    ve.wait_ge(*act.at(f"y{n}", turn))
                    at = slice(512 * n, 512 * n + 512)
                    ve.tensor_tensor(g.y_lo[:, at], ps[4 + n][:, :], g.y_hi[:, at].bitcast(F32), ALU.subtract).then_inc(*vec(f"y{n}"))

                lo(2)
                lo(3)
                clamp(0)
                added(0)
                added(1)
                lo(4)
                gated(0)
                lo(5)
                clamp(1)
                added(2)
                added(3)
                lo(6)
                turned_lo(0)
                gated(1)
                lo(7)
                clamp(2)
                added(4)
                added(5)
                lo(8)
                turned_lo(1)
                gated(2)
                lo(9)
                clamp(3)
                added(6)
                added(7)
                lo(10)
                turned_lo(2)
                gated(3)
                ve.wait_ge(*pe.at("st", turn))
                for t in ts:
                    pick(t, bass.ds(turn + 1, 1)).then_inc(*vec(f"pick{t}"))
                lo(11)
                ve.wait_ge(*pe.at("w9", turn))
                bias_pick(bass.ds(turn + 1, 1)).then_inc(*vec("bp"))
                turned_lo(3)
                lo(0)
                down(0)
                for i in range(2):
                    ve.wait_ge(*act.at(f"xh{i}", turn))
                    features_lo(i).then_inc(*vec(f"xl{i}"))
                lo(1)
                down(1)
            ve.wait_ge(*vec.before("y1", jobs))
            for t in ts:
                for i in (2 * t, 2 * t + 1):
                    ve.wait_ge(*last_pe.at(f"cb{i}"))
                    add(i, bass.ds(jobs, 1)).then_inc(*last_vec(f"ad{i}"))
                ve.wait_ge(*last_vec.at(f"ad{2 * t + 1}"))
                ve.tensor_tensor(g.acc[:, t, :], g.acc[:, t, :], g.mod[:, 3, :], ALU.mult).then_inc(*last_vec(f"gate{t}"))


def decoder_layer(nc, a, out):
    with ExitStack() as ctx:
        g = Space(nc, ctx, a)
        g.out = out
        g.chunks = ring_chunks(a)
        (g.x, g.mod, g.cols, g.eps, g.ones, g.ident, g.head_ones, g.later, g.iota_row, g.iota_part, g.vec1, g.b_router,
         g.w_router) = g.sb(ctx, x=([P, NT, D], F32), mod=([P, 4, D], F32), cols=([P, N_ROWS], F32), eps=([P, 2], F32),
             ones=([P, P], F32), ident=([P, P], F32), head_ones=([P, P], F32), later=([P, P], F32),
             iota_row=([P, P], F32), iota_part=([P, 1], F32), vec1=([P, 1], F32), b_router=([P, N_EXP], F32),
             w_router=([P, KD, N_EXP], F32))
        g.ps = [ctx.enter_context(nc.psum_tensor(f"bank{i}", [P, 512], F32)) for i in range(8)]
        g.small_in, g.eps_ready = g.sem(ctx, "small_in"), g.sem(ctx, "eps_ready")
        g.mod_out = g.sem(ctx, "mod_out")
        g.mod_rows = nc.dram_tensor("mod_rows", (1, 4, D), F32, kind="Internal").ap()
        g.ring_in = [g.sem(ctx, f"ring_in{i}") for i in range(RING)]
        with ExitStack() as mixer:
            (g.ring, g.hT, g.eye64, g.gram_mask, g.causal, g.chunk_mask, g.level_mask, g.qk_w, g.freq, g.pos, g.w_lo, g.w_g) = g.sb(mixer, ring=([P, RING, 4096], F32), hT=([P, KD, SEQ], F32), eye64=([P, 64], F32), gram_mask=([P, 2, P], F32),
                 causal=([P, P], F32), chunk_mask=([P, SEQ], F32), level_mask=([P, 6, P], F32), qk_w=([P, 2, QK], F32),
                 freq=([P, HALF], F32), pos=([P, NT], I32), w_lo=([P, WIDTH], F32), w_g=([P, WIDTH], F32))
            phase_adaln(nc, g)
            (g.mla_in, g.yT) = g.sb(mixer, mla_in=([P, NT, MLA_IN], F32), yT=([P, FT, SEQ], F32))
            rwkv = mixer.enter_context(ExitStack())
            (g.AR, g.Bt, g.Kt, g.v, g.bv, g.gate, g.w_end) = g.sb(rwkv, AR=([P, FT, NT, 2, P], F32), Bt=([P, FT, SEQ], F32), Kt=([P, FT, SEQ], F32), v=([P, FT, SEQ], F32),
                 bv=([P, FT, SEQ], F32), gate=([P, FT, SEQ], F32), w_end=([P, FT, NCH], F32))
            phase_project(nc, g)

            phase_rwkv(nc, g)
            rwkv.close()
            (g.oT,) = g.sb(mixer, oT=([P, FT, SEQ], F32))
            phase_mla(nc, g)

            phase_output(nc, g)
        with ExitStack() as moe:
            (g.h2_hi, g.h2_lo, g.acc, g.w_raw, g.bias, g.job_of, g.table, g.slot_of, g.weight_of, g.unused) = g.sb(moe, h2_hi=([P, NT, D], F32R), h2_lo=([P, NT, D], F32R), acc=([P, NT, D], F32), w_raw=([P, RAW, 2048], F32),
                 bias=([2 * N_EXP, 2 * D_FF + D], F32R), job_of=([2 * N_EXP, JOBS], F32), table=([1, JOBS + 1], I32), slot_of=([P, NT, JOBS], F32), weight_of=([P, NT, JOBS + 1], F32), unused=([P, 1], F32))
            phase_route(nc, g)
            phase_experts(nc, g)


_INS = ["x", "c", "positions", "ada_w", "ada_b", "norm_mix_w", "norm_ffn_w", "w_in",
        "q_a_norm_w", "w_q_up", "kv_a_norm_w", "w_kv_up", "q_norm_w", "k_norm_w", "w_o_mla", "rwkv_mu",
        "rwkv_w0", "rwkv_w2", "rwkv_a0", "rwkv_a2", "rwkv_g2", "rwkv_k_k", "rwkv_k_a", "rwkv_r_k",
        "rwkv_ln_w", "rwkv_ln_b", "rwkv_w_o", "w_out", "w_router", "b_router", "w_gate_up", "b_gate_up",
        "w_down", "b_down"]


def kernel(**inputs):
    import numpy as _np
    import concourse.bacc as _bacc
    from concourse import mybir as _mybir
    from concourse.bass_utils import run_bass_kernel_spmd as _run

    nc = _bacc.Bacc("TRN2", target_bir_lowering=False, num_devices=1)
    given = {name: _np.ascontiguousarray(inputs[name]) for name in _INS}
    given["inv_freq"] = (_np.float32(10000.0) ** (-(_np.arange(HALF, dtype=_np.float32) / _np.float32(HALF))))[None, :]
    arrays = {f"in_{name}_dram": array for name, array in given.items()}
    args = {name: nc.dram_tensor(f"in_{name}_dram", array.shape, _mybir.dt.from_np(array.dtype), kind="ExternalInput").ap()
            for name, array in given.items()}
    out = nc.dram_tensor("out_0_dram", (1, SEQ, D), F32, kind="ExternalOutput").ap()
    decoder_layer(nc, args, out)
    return _run(nc, [arrays], core_ids=[0]).results[0]["out_0_dram"]
```

```python
from contextlib import ExitStack

import concourse.bass as bass
from concourse import mybir

F32 = mybir.dt.float32
F32R = mybir.dt.float32r
I32 = mybir.dt.int32
U32 = mybir.dt.uint32
ALU = mybir.AluOpType
ACT = mybir.ActivationFunctionType
AX_X = mybir.AxisListType.X

P = 128
SEQ, D = 512, 1024
NT, KD = SEQ // P, D // P
HEADS, NOPE, ROPE, DV = 8, 64, 32, 64
QK = NOPE + ROPE
HALF = ROPE // 2
Q_LORA, KV_LORA = 256, 128
WIDTH = 512
FT = WIDTH // P
MLA_IN = Q_LORA + KV_LORA + ROPE
SLAB = 3 * WIDTH + 256
GATES = MLA_IN + SLAB
NMU = SLAB // P
CH = 64
NCH = SEQ // CH
N_EXP, TOP_K, D_FF = 32, 4, 1024
NORM_EPS, GN_EPS = 1e-6, 64e-5
DECAY = -0.6065306597126334
LIMIT, ALPHA = 7.0, 1.702
TWO_PI, PI_BELOW, ROUND = 6.283185307179586, 3.1415925, 12582912.0
TURN_PARTS = (6.28125, 0.0019340515136718750, 6.283185307179586 - 6.28125 - 0.0019340515136718750)
JOBS = 64
RING = 3

ROWS = {}
_n = 0
for _name, _k in (("c", 8), ("norm_mix_w", 8), ("q_a_norm_w", 2), ("kv_a_norm_w", 1), ("mu", NMU), ("w0", 4),
                  ("a0", 4), ("k_k", 4), ("k_a", 4), ("r_k", 4), ("ln_w", 4), ("ln_b", 4)):
    ROWS[_name] = (_n, _k)
    _n += _k
N_ROWS = _n


class Steps:

    def __init__(self, sem, names):
        self.sem, self.value, self.count = sem, {n: i + 1 for i, n in enumerate(names)}, 0
        assert len(self.value) == len(names)

    def __call__(self, name):
        self.count += 1
        assert self.value[name] == self.count, (name, self.value[name], self.count)
        return self.sem, 1

    def at(self, name):
        return self.sem, self.value[name]


def names(fmt, n):
    return [fmt.format(i) for i in range(n)]


class Space:

    def __init__(self, nc, ctx, a):
        self.nc, self.ctx, self.a = nc, ctx, a

    def sb(self, ctx, **shapes):
        return [ctx.enter_context(self.nc.sbuf_tensor(f"sb_{name}", shape, dt)) for name, (shape, dt) in shapes.items()]

    def sem(self, ctx, name):
        return ctx.enter_context(self.nc.semaphore(name))

    def steps(self, ctx, name, order):
        return Steps(self.sem(ctx, name), order)

    def col(self, name, i=0):
        return self.cols[:, ROWS[name][0] + i:ROWS[name][0] + i + 1]


def ring_chunks(a):
    def rows(w, lo, hi):
        return w[0, :, lo:hi].rearrange("(k p) n -> p k n", p=P)

    slab = MLA_IN
    chunks = [rows(a["ada_w"], 512 * j, 512 * j + 512) for j in range(12)]
    chunks += [rows(a["w_in"], slab + 3 * WIDTH, slab + SLAB)]
    chunks += [rows(a["w_in"], slab + 512 * j, slab + 512 * j + 512) for j in range(3)]
    chunks += [rows(a["w_in"], 0, MLA_IN)]
    chunks += [rows(a["w_o_mla"], 0, D), rows(a["rwkv_w_o"], 0, D)]
    chunks += [rows(a["w_in"], GATES + 512 * j, GATES + 512 * j + 512) for j in range(4)]
    chunks += [rows(a["w_out"], 512 * j, 512 * j + 512) for j in range(2)]
    return chunks


ADA0, LO, RKV, MLA, OA, OB, GA, GB, WOUT, N_CHUNKS = 0, 12, 13, 16, 17, 18, 19, 21, 23, 25


def slot(g, i):
    k, n = g.chunks[i].shape[1:]
    return g.ring[:, i % RING, 0:k * n].rearrange("p (k n) -> p k n", k=k)


def load_chunk(g, eng, i):
    eng.dma_start(slot(g, i), g.chunks[i]).then_inc(g.ring_in[i % RING], 16)


def chunk_loaded(g, i):
    return g.ring_in[i % RING], 16 * (i // RING + 1)


def phase_adaln(nc, g):
    a = g.a
    with ExitStack() as ctx:
        part = ([P, 3, 4, 512], F32R)
        (g.stage, g.cond, g.sig, g.cond_hi, g.cond_lo, g.rep_hi, g.rep_lo, g.ada_b_rows, g.mod1, g.ffn_w_row, g.xn,
         g.ss, g.rstd, g.mod1_cols, g.gain, g.p_hi, g.p_lo) = g.sb(
            ctx, stage=([N_ROWS, P], F32), cond=([P, KD], F32), sig=([P, KD], F32), cond_hi=([P, KD], F32R), cond_lo=([P, KD], F32),
            rep_hi=([P, KD, P], F32R), rep_lo=([P, KD, P], F32R), ada_b_rows=([1, 4, 512], F32), mod1=([P, 4, 512], F32),
            ffn_w_row=([P, D], F32), xn=([P, NT, D], F32), ss=([P, NT], F32), rstd=([P, NT], F32),
            mod1_cols=([P, 2 * KD], F32), gain=([P, KD], F32), p_hi=part, p_lo=part)
        rows_in, x_in = (g.sem(ctx, n) for n in ("rows_in", "x_in"))
        row_in = [g.sem(ctx, f"ada_row_in{i}") for i in range(4)]
        pool_s = g.steps(ctx, "a_consts", names("c{}", N_CONSTS))
        vec = g.steps(ctx, "a_vec", ["cols", "cond", "cond_hi", "cond_lo"] + [f"{x}{k}" for k in range(KD) for x in ("rh", "rl")]
                      + names("p{}", 12) + names("mcol{}", 4) + ["gain", "p12", "rstd", "xn0", "xn1", "p13", "xn2", "xn3", "p14", "p15"]
                      + names("h{}", KD) + names("p{}", 24)[16:] + ["g2"])
        turns = [[f"p{2 * j + 2}", f"p{2 * j + 3}"] * (j < 11) + [f"mod{j}"] for j in range(12)]
        act = g.steps(ctx, "a_act", ["sig", "p0", "p1"] + turns[0] + [x for t in range(NT) for x in turns[t + 1] + [f"sq{t}"]] + ["std"]
                      + [x for t in turns[NT + 1:] for x in t])
        pe = g.steps(ctx, "a_pe", ["rows"] + names("p{}", 10) + names("mcol{}", 4) + names("p{}", 14)[10:] + names("h{}", KD) + names("p{}", 24)[14:])
        ps = g.ps
        block = ctx.enter_context(nc.Block())

        unused = g.hT[:, 0:2, :].rearrange("p a n -> p (a n)")

        def piece(q):
            return slot(g, q // 2)[:, 4 * (q % 2):4 * (q % 2) + 4, :]

        @block.sync
        def _(sp):
            flat = {"c": a["c"], "mu": a["rwkv_mu"], "r_k": a["rwkv_r_k"][0].rearrange("h n -> (h n)").unsqueeze(0)}
            for name, (at, k) in ROWS.items():
                src = flat.get(name)
                if src is None:
                    src = a[name if name in a else "rwkv_" + name]
                sp.dma_start(g.stage[at:at + k, :], src.rearrange("a (k p) -> (a k) p", p=P)).then_inc(rows_in, 16)
            load_chunk(g, sp, 0)

            def load_row(j):
                sp.dma_start(g.ada_b_rows[:, j % 4, :], a["ada_b"][:, 512 * j:512 * j + 512]).then_inc(row_in[j % 4], 16)

            for j in range(4):
                load_row(j)
            load_chunk(g, sp, 1)
            sp.dma_start(g.x[:, :, :], a["x"][0].rearrange("(t p) d -> p t d", p=P)).then_inc(x_in, 16)
            load_chunk(g, sp, 2)
            for i in range(RING, 12 + RING):
                sp.wait_ge(*vec.at(f"p{2 * (i - RING) + 1}"))
                load_chunk(g, sp, i)
                if 4 <= i < 12:
                    sp.wait_ge(*pe.at(f"p{2 * (i - 4) + 1}"))
                    load_row(i)

            sp.wait_ge(*vec.at("g2"))
            sp.dma_start(g.mod_rows, g.mod[0:1, :, :]).then_inc(g.mod_out, 16)

        @block.gpsimd
        def _(pool):
            make_constants(nc, g, pool, pool_s)

        @block.scalar
        def _(sc):
            def small(dst, src):
                sc.dma_start(dst, src).then_inc(g.small_in, 16)
                g.n_small += 16

            g.n_small = 0
            small(g.ffn_w_row[:, :], a["norm_ffn_w"].partition_broadcast(P).rearrange("p a n -> p (a n)"))
            for i, n in enumerate(("q_norm_w", "k_norm_w")):
                small(g.qk_w[:, i, :], a[n].partition_broadcast(P).rearrange("p a n -> p (a n)"))
            small(g.b_router[:, :], a["b_router"].partition_broadcast(P).rearrange("p a n -> p (a n)"))
            small(g.freq[:, :], a["inv_freq"].partition_broadcast(P).rearrange("p a n -> p (a n)"))
            sc.dma_start(g.pos[:, :], a["positions"][0].rearrange("(t p) -> p t", p=P), allow_slow_non_contiguous=True).then_inc(g.small_in, 16)
            small(g.w_lo[0:64, :], a["rwkv_w2"][0])
            small(g.w_lo[64:128, :], a["rwkv_a2"][0])
            small(g.w_g[:, :], a["rwkv_g2"][0])
            small(g.w_router[:, :, :], a["w_router"][0].rearrange("(k p) n -> p k n", p=P))
            sc.wait_ge(*vec.at("cols"))
            sc.activation(g.sig[:, :], g.cols[:, 0:KD], ACT.Sigmoid).then_inc(*act("sig"))

            def evacuate(j):
                sc.wait_ge(*pe.at(f"p{2 * j + 1}"))
                dst = g.mod1[:, j, :] if j < 4 else g.mod[:, (j - 4) // 2, (j % 2) * 512:(j % 2) * 512 + 512]
                sc.copy(dst, ps[1 + j % 3][:, :]).then_inc(*act(f"mod{j}"))

            def hi_part(q):
                if q % 2 == 0:
                    sc.wait_ge(*chunk_loaded(g, q // 2))
                if q >= 3:
                    sc.wait_ge(*pe.at(f"p{q - 3}"))
                sc.copy(g.p_hi[:, q % 3, :, :], piece(q)).then_inc(*act(f"p{q}"))

            hi_part(0)
            hi_part(1)
            for j in range(12):
                if j < 11:
                    hi_part(2 * j + 2)
                    hi_part(2 * j + 3)
                evacuate(j)
                if 1 <= j <= NT:
                    t = j - 1
                    if t == 0:
                        sc.wait_ge(x_in, 16)
                    else:
                        sc.wait_ge(*act.at(f"sq{t - 1}"))
                    sc.activation(unused, g.x[:, t, :], ACT.Square, accum_out=g.ss[:, t:t + 1]).then_inc(*act(f"sq{t}"))
                if j == NT:
                    sc.wait_ge(*act.at(f"sq{NT - 1}"))
                    sc.wait_ge(g.eps_ready, 1)
                    sc.activation(g.rstd[:, :], g.ss[:, :], ACT.Sqrt, bias=g.eps[:, 0:1], scale=1.0 / D).then_inc(*act("std"))

        @block.vector
        def _(ve):
            ve.memset(g.eps[:, 0:1], NORM_EPS)
            ve.memset(g.eps[:, 1:2], GN_EPS).then_inc(g.eps_ready, 1)
            ve.wait_ge(*pe.at("rows"))
            ve.tensor_copy(g.cols[:, :], ps[0][:, 0:N_ROWS]).then_inc(*vec("cols"))
            ve.wait_ge(*act.at("sig"))
            ve.wait_ge(*vec.at("cols"))
            ve.tensor_tensor(g.cond[:, :], g.cols[:, 0:KD], g.sig[:, :], ALU.mult).then_inc(*vec("cond"))
            ve.wait_ge(*pool_s.at("c2"))
            ve.wait_ge(*vec.at("cond"))
            ve.tensor_copy(g.cond_hi[:, :], g.cond[:, :]).then_inc(*vec("cond_hi"))
            ve.wait_ge(*vec.at("cond_hi"))
            ve.tensor_tensor(g.cond_lo[:, :], g.cond[:, :], g.cond_hi[:, :].bitcast(F32), ALU.subtract).then_inc(*vec("cond_lo"))
            ve.wait_ge(*vec.at("cond_lo"))
            for k in range(KD):
                for x, rep, col in (("rh", g.rep_hi, g.cond_hi[:, k:k + 1].bitcast(F32)), ("rl", g.rep_lo, g.cond_lo[:, k:k + 1])):
                    ve.tensor_scalar(rep[:, k, :], g.ones[:, :], col, None, ALU.mult).then_inc(*vec(f"{x}{k}"))

            def lo_part(q):
                ve.wait_ge(*act.at(f"p{q}"))
                ve.tensor_tensor(g.p_lo[:, q % 3, :, :], piece(q), g.p_hi[:, q % 3, :, :].bitcast(F32), ALU.subtract).then_inc(*vec(f"p{q}"))

            for q in range(12):
                lo_part(q)
            for q in range(4):
                ve.wait_ge(*pe.at(f"mcol{q}"))
                src = ps[4 + q][:, :].rearrange("p (b n) -> p b n", b=4)[:, :, 0]
                ve.tensor_copy(g.mod1_cols[:, 4 * q:4 * q + 4], src).then_inc(*vec(f"mcol{q}"))
            ve.wait_ge(*vec.at("mcol3"))
            at = ROWS["norm_mix_w"][0]
            ve.scalar_tensor_tensor(g.gain[:, :], g.mod1_cols[:, KD:2 * KD], 1.0, g.cols[:, at:at + KD], ALU.add, ALU.mult).then_inc(*vec("gain"))
            lo_part(12)
            ve.wait_ge(*act.at("std"))
            ve.reciprocal(g.rstd[:, :], g.rstd[:, :]).then_inc(*vec("rstd"))
            ve.wait_ge(*vec.at("rstd"))
            for t in range(NT):
                ve.tensor_scalar(g.xn[:, t, :], g.x[:, t, :], g.rstd[:, t:t + 1], None, ALU.mult).then_inc(*vec(f"xn{t}"))
                if t == 1:
                    lo_part(13)
            lo_part(14)
            lo_part(15)
            ve.wait_ge(*vec.at("gain"))
            for k in range(KD):
                ve.wait_ge(*pe.at(f"h{k}"))
                ve.tensor_scalar(g.hT[:, k, :], ps[4 + k % 4][:, :], g.gain[:, k:k + 1], g.mod1_cols[:, k:k + 1],
                                 ALU.mult, ALU.add).then_inc(*vec(f"h{k}"))
            for q in range(16, 24):
                lo_part(q)
            ve.wait_ge(g.small_in, 16 * 10)
            ve.wait_ge(*act.at("mod11"))
            ve.scalar_tensor_tensor(g.mod[:, 2, :], g.mod[:, 2, :], 1.0, g.ffn_w_row[:, :], ALU.add, ALU.mult).then_inc(*vec("g2"))

        @block.tensor
        def _(te):
            te.wait_ge(rows_in, 16 * len(ROWS))
            te.wait_ge(*pool_s.at("c2"))
            te.transpose(ps[0][:, 0:N_ROWS], g.stage[:, :], g.ident[0:N_ROWS, 0:N_ROWS]).then_inc(*pe("rows"))
            te.wait_ge(*vec.at(f"rl{KD - 1}"))

            def ada(j):
                te.wait_ge(row_in[j % 4], 16 * (j // 4 + 1))
                if j >= 3:
                    te.wait_ge(*act.at(f"mod{j - 3}"))
                out = ps[1 + j % 3][:, :]
                te.matmul(out, g.ones[0:1, :], g.ada_b_rows[:, j % 4, :], start=True, stop=False)
                for q in (2 * j, 2 * j + 1):
                    te.wait_ge(*vec.at(f"p{q}"))
                    for i in range(4):
                        k, hi, lo = 4 * (q % 2) + i, g.p_hi[:, q % 3, i, :], g.p_lo[:, q % 3, i, :]
                        te.matmul(out, g.rep_hi[:, k, :], hi, start=False, stop=False)
                        te.matmul(out, g.rep_hi[:, k, :], lo, start=False, stop=False)
                        mm = te.matmul(out, g.rep_lo[:, k, :], hi, start=False, stop=(k == KD - 1))
                    mm.then_inc(*pe(f"p{q}"))

            for j in range(5):
                ada(j)
            for q in range(4):
                te.wait_ge(*act.at(f"mod{q}"))
                for b in range(4):
                    mm = te.transpose(ps[4 + q][:, 128 * b:128 * b + 128], g.mod1[:, q, 128 * b:128 * b + 128], g.ident[:, :])
                mm.then_inc(*pe(f"mcol{q}"))
            ada(5)
            ada(6)
            te.wait_ge(*vec.at(f"xn{NT - 1}"))
            for k in range(KD):
                te.wait_ge(*vec.at(f"h{k - 4}" if k >= 4 else f"mcol{k}"))
                for t in range(NT):
                    mm = te.transpose(ps[4 + k % 4][:, P * t:P * t + P], g.xn[:, t, P * k:P * k + P], g.ident[:, :])
                mm.then_inc(*pe(f"h{k}"))
            for j in range(7, 12):
                ada(j)


N_CONSTS = 68


def make_constants(nc, g, pool, s):
    def step(ins):
        ins.then_inc(*s(f"c{s.count}"))
        pool.wait_ge(s.sem, s.count)

    def select(dst, pattern, op, fill, base, cm):
        step(pool.affine_select(out=dst, in_=dst, pattern=pattern, compare_op=op, fill=fill, base=base, channel_multiplier=cm))

    def fill(dst, value):
        step(pool.memset(dst, value))

    fill(g.ones[:, :], 1.0)
    fill(g.ident[:, :], 0.0)
    select(g.ident[:, :], [[-1, P]], ALU.not_equal, 1.0, 0, 1)
    fill(g.eye64[:, :], 0.0)
    for base in (0, -64):
        select(g.eye64[:, :], [[-1, 64]], ALU.not_equal, 1.0, base, 1)
    fill(g.gram_mask[:, :, :], 1.0)
    select(g.gram_mask[:, 0, :], [[1, P]], ALU.is_gt, 0.0, 0, -1)
    select(g.gram_mask[:, 1, :], [[1, P]], ALU.is_ge, 0.0, 0, -1)
    fill(g.gram_mask[0:64, :, 64:P], 0.0)
    fill(g.causal[:, :], 0.0)
    select(g.causal[:, :], [[-1, P]], ALU.is_ge, -1e30, 0, 1)
    fill(g.chunk_mask[:, :], 1.0)
    fill(g.chunk_mask[:, :].rearrange("p (c n) -> p c n", n=CH)[:, :, 0], 0.0)
    for l in range(6):
        b = 1 << l
        half = g.level_mask[:, l, :].rearrange("p (j h b) -> p j h b", h=2, b=b)
        fill(g.level_mask[:, l, :], 0.0)
        fill(half[:, :, 1, :], 1.0)
        select(half[:, :, 1, :], [[-2 * b, P // (2 * b)], [0, b]], ALU.is_ge, 0.0, 0, 1)
        select(half[:, :, 1, :], [[2 * b, P // (2 * b)], [0, b]], ALU.is_ge, 0.0, b - 1, -1)
    fill(g.by_head[:, :, :], 0.0)
    for f in range(FT):
        fill(g.by_head[0:64, f, 2 * f:2 * f + 1], 1.0)
        fill(g.by_head[64:P, f, 2 * f + 1:2 * f + 2], 1.0)
    fill(g.from_head[:, :, :], 0.0)
    select(g.from_head[:, :, :].rearrange("p f (h n) -> p f h n", h=2), [[-2, FT], [-1, 2], [0, 64]], ALU.not_equal, 1.0, 0, 1)
    fill(g.head_ones[:, :], 0.0)
    fill(g.head_ones[0:64, 0:64], 1.0)
    fill(g.head_ones[64:P, 64:P], 1.0)
    fill(g.later[:, :], 1.0)
    select(g.later[:, :], [[1, P]], ALU.is_gt, 0.0, 0, -1)
    for dst, n, cm in ((g.iota_row, P, 0), (g.iota_part, 1, 1)):
        step(pool.iota(dst[:, :], [[1, n]], base=0, channel_multiplier=cm, allow_small_or_imprecise_dtypes=True))
    fill(g.vec1[:, :], 1.0)
    assert s.count <= N_CONSTS, s.count


def phase_project(nc, g):
    with ExitStack() as ctx:
        tile = ([P, SEQ], F32)
        (g.raw, g.lerp, g.wa, g.sg, g.not_mu, g.ka, g.rn) = g.sb(ctx, raw=([P, 4, SEQ + 1], F32), lerp=([P, 2, SEQ], F32), wa=tile, sg=tile, not_mu=([P, NMU], F32), ka=tile, rn=tile)
        quarter = lambda buf, i: buf[:, 2 * i:2 * i + 2, :].rearrange("p a (b n) -> p (a b) n", n=SEQ)
        sw, al, rk = quarter(g.x, 0), quarter(g.x, 1), quarter(g.mod, 0)
        csum, ew = quarter(g.mod, 1)[:, 0:2, :], quarter(g.mod, 1)[:, 2:4, :]
        flat = g.AR[:, :, :, :, :].rearrange("p i t x n -> p i (t x n)")
        squares, norms = flat[:, :, 0:SEQ], flat[:, :, SEQ:2 * SEQ]
        f4 = range(FT)
        outs = ["l0", "l1"] + [f"r{i}" for i in f4] + [f"k{i}" for i in f4] + [f"{x}{i}" for i in f4 for x in ("zw", "za")]
        outs += [f"{x}{i}" for x in ("g", "ss", "v", "m", "bo") for i in f4]
        pe = g.steps(ctx, "b_pe", outs)
        exps = [[f"{x}{i}" for x in ("ew", "ep", "ei")] for i in f4]
        act = g.steps(ctx, "b_act", outs[:6] + ["tanh", "sigg"] + outs[6:18] + names("sq{}", 4) + outs[18:26] + exps[0] + exps[1]
                      + ["v0", "v1"] + exps[2] + ["v2", "v3"] + exps[3] + names("m{}", 4))
        lerps = outs[:10] + names("v{}", 4)

        def forms(i):
            return [f"{x}{i}" for x in ("ld", "L", "Lp", "nm", "rn", "kk", "ka", "k2", "rk", "R", "A", "kb", "B", "K", "wc")]

        vec = g.steps(ctx, "b_vec", ["not_mu", "zero"] + [x for n in lerps[:10] for x in (f"t_{n}", n)] + names("kk0{}", 4)
                      + [x for i in f4 for x in forms(i) + ({1: ["t_v0", "v0", "t_v1", "v1"], 2: ["t_v2", "v2", "t_v3", "v3"]}.get(i, []))]
                      + names("bv{}", 4))
        block = ctx.enter_context(nc.Block())
        bank = {n: g.ps[j % 8] for j, n in enumerate(outs)}

        @block.sync
        def _(sp):
            for i, last in ((LO, "l1"), (LO + 1, "r3"), (LO + 2, "k3"), (LO + 3, "v3"), (MLA, "m3")):
                if i + RING <= MLA:
                    sp.wait_ge(*pe.at(last))
                    load_chunk(g, sp, i + RING)

        @block.tensor
        def _(te):
            def product(name, pairs, cols=SEQ):
                j = outs.index(name)
                if j >= 8:
                    te.wait_ge(*act.at(outs[j - 8]))
                for n, (lhsT, rhs) in enumerate(pairs):
                    mm = te.matmul(bank[name][:, 0:cols], lhsT, rhs, start=(n == 0), stop=(n == len(pairs) - 1))
                mm.then_inc(*pe(name))

            def feature(name, chunk, i):
                te.wait_ge(*chunk_loaded(g, chunk))
                w = slot(g, chunk)
                product(name, [(w[:, k, P * i:P * i + P], g.hT[:, k, :]) for k in range(KD)])

            for i in range(2):
                feature(f"l{i}", LO, i)
            for i in f4:
                feature(f"r{i}", RKV, i)
            for i in f4:
                feature(f"k{i}", RKV + 1, i)
            te.wait_ge(*act.at("tanh"))
            for i in f4:
                at = slice(P * i, P * i + P)
                product(f"zw{i}", [(g.w_lo[0:64, at], g.wa[0:64, :])])
                product(f"za{i}", [(g.w_lo[64:P, at], g.wa[64:P, :])])
            te.wait_ge(*act.at("sigg"))
            for i in f4:
                product(f"g{i}", [(g.w_g[:, P * i:P * i + P], g.sg[:, :])])
            for i in f4:
                te.wait_ge(*act.at(f"sq{i}"))
                product(f"ss{i}", [(g.head_ones[:, :], squares[:, i, :])])
            for i in f4:
                feature(f"v{i}", RKV + 2, i)
            te.wait_ge(*chunk_loaded(g, MLA))
            for t in range(NT):
                product(f"m{t}", [(g.hT[:, k, P * t:P * t + P], slot(g, MLA)[:, k, :]) for k in range(KD)], MLA_IN)
            for i in f4:
                te.wait_ge(*vec.at(f"rk{i}"))
                product(f"bo{i}", [(g.head_ones[:, :], rk[:, i, :])])

        @block.scalar
        def _(sc):
            def raw(name):
                m = lerps.index(name)
                sc.wait_ge(*pe.at(name))
                sc.wait_ge(*(vec.at(lerps[m - 4]) if m >= 4 else vec.at("zero")))
                sc.copy(g.raw[:, m % 4, 1:SEQ + 1], bank[name][:, :]).then_inc(*act(name))

            for n in lerps[:6]:
                raw(n)
            sc.wait_ge(*vec.at("l0"))
            sc.activation(g.wa[0:64, :], g.wa[0:64, :], ACT.Tanh).then_inc(*act("tanh"))
            sc.wait_ge(*vec.at("l1"))
            sc.activation(g.sg[:, :], g.sg[:, :], ACT.Sigmoid).then_inc(*act("sigg"))
            for n in lerps[6:10]:
                raw(n)
            for i in f4:
                sc.wait_ge(*pe.at(f"zw{i}"))
                sc.activation(sw[:, i, :], bank[f"zw{i}"][:, :], ACT.Sigmoid, bias=g.col("w0", i)).then_inc(*act(f"zw{i}"))
                sc.wait_ge(*pe.at(f"za{i}"))
                sc.activation(al[:, i, :], bank[f"za{i}"][:, :], ACT.Sigmoid, bias=g.col("a0", i)).then_inc(*act(f"za{i}"))
            for i in f4:
                sc.wait_ge(*vec.at(f"kk0{i}"))
                sc.activation(squares[:, i, :], g.Bt[:, i, :], ACT.Square).then_inc(*act(f"sq{i}"))
            for i in f4:
                sc.wait_ge(*pe.at(f"g{i}"))
                sc.copy(g.gate[:, i, :], bank[f"g{i}"][:, :]).then_inc(*act(f"g{i}"))
            for i in f4:
                sc.wait_ge(*pe.at(f"ss{i}"))
                sc.activation(norms[:, i, :], bank[f"ss{i}"][:, :], ACT.Sqrt).then_inc(*act(f"ss{i}"))

            def exponentials(i):
                j = i % 2
                sc.wait_ge(*vec.at(f"L{i}"))
                sc.activation(ew[:, j, :], csum[:, j, :], ACT.Exp).then_inc(*act(f"ew{i}"))
                sc.wait_ge(*vec.at(f"Lp{i}"))
                sc.activation(sw[:, i, :], sw[:, i, :], ACT.Exp).then_inc(*act(f"ep{i}"))
                sc.activation(csum[:, j, :], csum[:, j, :], ACT.Exp, scale=-1.0).then_inc(*act(f"ei{i}"))

            exponentials(0)
            exponentials(1)
            raw("v0")
            raw("v1")
            exponentials(2)
            raw("v2")
            raw("v3")
            exponentials(3)
            for t in range(NT):
                sc.wait_ge(*pe.at(f"m{t}"))
                sc.copy(g.mla_in[:, t, :], bank[f"m{t}"][:, 0:MLA_IN]).then_inc(*act(f"m{t}"))

        @block.vector
        def _(ve):
            at = ROWS["mu"][0]
            ve.tensor_scalar(g.not_mu[:, :], g.cols[:, at:at + NMU], -1.0, 1.0, ALU.mult, ALU.add).then_inc(*vec("not_mu"))
            ve.memset(g.raw[:, :, 0:1], 0.0).then_inc(*vec("zero"))
            ve.wait_ge(*vec.at("zero"))

            def shift(name, dst, mu):
                m = lerps.index(name)
                ve.wait_ge(*act.at(name))
                ve.tensor_scalar(g.lerp[:, m % 2, :], g.raw[:, m % 4, 0:SEQ], g.col("mu", mu), None, ALU.mult).then_inc(*vec(f"t_{name}"))
                ve.wait_ge(*vec.at(f"t_{name}"))
                ve.scalar_tensor_tensor(dst, g.raw[:, m % 4, 1:SEQ + 1], g.not_mu[:, mu:mu + 1], g.lerp[:, m % 2, :],
                                        ALU.mult, ALU.add).then_inc(*vec(name))

            shift("l0", g.wa[:, :], 12)
            shift("l1", g.sg[:, :], 13)
            for i in f4:
                shift(f"r{i}", g.bv[:, i, :], i)
            for i in f4:
                shift(f"k{i}", g.Kt[:, i, :], 4 + i)
            for i in f4:
                ve.wait_ge(*vec.at(f"k{i}"))
                ve.tensor_scalar(g.Bt[:, i, :], g.Kt[:, i, :], g.col("k_k", i), None, ALU.mult).then_inc(*vec(f"kk0{i}"))
            ve.wait_ge(g.mod_out, 16)
            for i in f4:
                if i >= 2:
                    for n in (2 * i - 4, 2 * i - 3):
                        shift(f"v{n}", g.v[:, n, :], 8 + n)
                j = i % 2
                k, r, b = g.Kt[:, i, :], g.bv[:, i, :], g.Bt[:, i, :]
                ve.wait_ge(*act.at(f"zw{i}"))
                ve.tensor_scalar(sw[:, i, :], sw[:, i, :], DECAY, None, ALU.mult).then_inc(*vec(f"ld{i}"))
                ve.wait_ge(*vec.at(f"ld{i}"))
                ve.tensor_tensor_scan(csum[:, j, :], g.chunk_mask[:, :], sw[:, i, :], 0.0, ALU.mult, ALU.add).then_inc(*vec(f"L{i}"))
                ve.wait_ge(*vec.at(f"L{i}"))
                ve.tensor_tensor(sw[:, i, :], csum[:, j, :], sw[:, i, :], ALU.subtract).then_inc(*vec(f"Lp{i}"))
                ve.wait_ge(*act.at(f"ss{i}"))
                ve.tensor_scalar(g.rn[:, :], norms[:, i, :], 1e-12, None, ALU.max).then_inc(*vec(f"nm{i}"))
                ve.wait_ge(*vec.at(f"nm{i}"))
                ve.reciprocal(g.rn[:, :], g.rn[:, :]).then_inc(*vec(f"rn{i}"))
                ve.wait_ge(*vec.at(f"rn{i}"))
                ve.tensor_tensor(b, b, g.rn[:, :], ALU.mult).then_inc(*vec(f"kk{i}"))
                ve.wait_ge(*act.at(f"za{i}"))
                ve.tensor_scalar(g.ka[:, :], al[:, i, :], -1.0, g.col("k_a", i), ALU.add, ALU.mult).then_inc(*vec(f"ka{i}"))
                ve.wait_ge(*vec.at(f"ka{i}"))
                ve.scalar_tensor_tensor(k, g.ka[:, :], 1.0, k, ALU.add, ALU.mult).then_inc(*vec(f"k2{i}"))
                ve.wait_ge(*vec.at(f"k2{i}"))
                ve.scalar_tensor_tensor(rk[:, i, :], r, g.col("r_k", i), k, ALU.mult, ALU.mult).then_inc(*vec(f"rk{i}"))
                split = lambda x: x.rearrange("p (t n) -> p t n", t=NT)
                ve.wait_ge(*act.at(f"ew{i}"))
                ve.tensor_tensor(g.AR[:, i, :, 1, :], split(r), split(ew[:, j, :]), ALU.mult).then_inc(*vec(f"R{i}"))
                ve.wait_ge(*act.at(f"ep{i}"))
                ve.scalar_tensor_tensor(g.AR[:, i, :, 0, :], split(b), -1.0, split(sw[:, i, :]), ALU.mult, ALU.mult).then_inc(*vec(f"A{i}"))
                ve.wait_ge(*vec.at(f"A{i}"))
                ve.tensor_tensor(b, b, al[:, i, :], ALU.mult).then_inc(*vec(f"kb{i}"))
                ve.wait_ge(*vec.at(f"kb{i}"))
                ve.wait_ge(*act.at(f"ei{i}"))
                ve.tensor_tensor(b, b, csum[:, j, :], ALU.mult).then_inc(*vec(f"B{i}"))
                ve.tensor_tensor(k, k, csum[:, j, :], ALU.mult).then_inc(*vec(f"K{i}"))
                ve.tensor_copy(g.w_end[:, i, :], ew[:, j, :].rearrange("p (c n) -> p c n", n=CH)[:, :, CH - 1]).then_inc(*vec(f"wc{i}"))
            for i in f4:
                ve.wait_ge(*pe.at(f"bo{i}"))
                ve.tensor_tensor(g.bv[:, i, :], bank[f"bo{i}"][:, :], g.v[:, i, :], ALU.mult).then_inc(*vec(f"bv{i}"))


def phase_rwkv(nc, g):
    with ExitStack() as ctx:
        ring = g.ring[:, :, :]
        gm_buf = [ring[:, j, :].rearrange("p (u n) -> p u n", u=8) for j in range(2)]
        scratch = [ring[:, 2, :], g.x[:, :, :].rearrange("p a b -> p (a b)"), g.mod[:, :, :].rearrange("p a b -> p (a b)")]
        take = [0]

        def quad():
            i = take[0]
            take[0] += 1
            return scratch[i // 8][:, 512 * (i % 8):512 * (i % 8) + 512].rearrange("p (u n) -> p u n", u=4)

        X = [quad() for _ in range(2)]
        T = [quad() for _ in range(2)]
        TT = [quad() for _ in range(2)]
        off = [[quad() for _ in range(2)] for _ in range(2)]
        X0 = [quad() for _ in range(2)]
        Y1 = [quad() for _ in range(2)]
        (g.inv_dev,) = g.sb(ctx, inv_dev=([HEADS, SEQ], F32))
        g.squares_used = g.sem(ctx, "squares_used")
        (g.tok, g.square) = g.sb(ctx, tok=([P, 2, NT, 4, P], F32), square=([P, 2, SEQ], F32))
        ysq = g.square
        fts, halves = range(FT), range(2)
        fh = [(f, h) for f in fts for h in halves]

        def pre_names(f):
            return [f"tm{f}{t}" for t in range(NT)] + [f"gm{f}{u}" for u in range(8)]

        def level_names(f, l):
            out = [f"xx{f}{l}{h}" for h in halves]
            for h in halves:
                out += [f"tt{f}{l}{h}"] + ([f"t{f}{l}{h}"] if l < 5 else [])
            return out

        def post_names(f):
            return [f"{x}{f}{h}" for x in ("x0", "y1", "ry", "eg") for h in halves]

        order = pre_names(0)
        for f in fts:
            order += [f"tr{f}{h}" for h in halves]
            nxt = pre_names(f + 1) if f + 1 < FT else []
            for l in range(1, 6):
                order += level_names(f, l)
                order += nxt[3 * (l - 1):3 * l]
            order += post_names(f)
        chain = []
        for c in range(NCH):
            chain += [f"y{c}"] + ([f"s{c}"] if c < NCH - 1 else [])
        tail = [f"mean{f}" for f in fts] + ["var"] + [f"rs{f}" for f in fts]
        pe = g.steps(ctx, "c_pe", order + chain + tail)
        pool_names = []
        for f in fts:
            pool_names += [f"off{f}0{h}" for h in halves] + [f"i{f}{h}" for h in halves] + [f"off{f}{l}{h}" for l in range(1, 6) for h in halves]
        pool = g.steps(ctx, "c_pool", pool_names + [f"yT{f}" for f in fts])
        act_names, vec_names = [], []
        for n in order:
            if n[0:2] in ("tm", "tr", "x0", "y1"):
                act_names.append(n)
            elif n[0:2] in ("gm", "tt"):
                vec_names.append(n)
            elif n[0] == "x":
                act_names.append(n)
            elif n[0:2] == "ry":
                vec_names.append("r" + n[2:])
                act_names.append("y0_" + n[2:])
            elif n[0:2] == "eg":
                vec_names += [f"{x}{n[2:]}{c}" for c in range(2) for x in "eg"]
            else:
                vec_names.append(n)
        vec_names += ["s_first"]
        for c in range(NCH - 1):
            vec_names += [f"s{c}_{f}" for f in fts] + ([f"lb{c}"] if c < FT else [])
        vec_names += [f"y{f}" for f in fts] + [f"mean{f}" for f in fts]
        vec_names += ["rs"] + [f"{x}{f}" for f in fts for x in ("yn", "ya")]
        act_names += [f"ysq{f}" for f in fts] + ["std"]
        act = g.steps(ctx, "c_act", act_names)
        vec = g.steps(ctx, "c_vec", vec_names)
        block = ctx.enter_context(nc.Block())
        ps = g.ps
        pre_bank = {}
        for f in fts:
            for j, n in enumerate(pre_names(f)):
                pre_bank[n] = ps[j % 4]

        def gm(f, u):
            return gm_buf[f % 2][:, u, :]

        def rows(hh):
            return slice(64 * hh, 64 * hh + 64)

        def unit(u):
            return u // 4, u % 4, u // 2, u % 2

        def as_units(ap):
            return ap.rearrange("p (u n) -> p u n", u=4)

        def yc_of(f):
            return g.Bt[:, f, :]

        @block.tensor
        def _(te):
            def group(out, pairs):
                for n, (lhsT, rhs) in enumerate(pairs):
                    mm = te.matmul(out, lhsT, rhs, start=(n == 0), stop=(n == len(pairs) - 1))
                return mm

            def pre(f, n):
                names_ = pre_names(f)
                j = names_.index(n)
                prev = names_[j - 4] if j >= 4 else (pre_names(f - 1)[j + 8] if f else None)
                if prev:
                    te.wait_ge(*(act.at(prev) if prev.startswith("tm") else vec.at(prev)))
                if j in (2, 3) and f >= 2:
                    te.wait_ge(*vec.at(f"g{f - 2}{j - 2}1"))
                bank = pre_bank[n]
                if j < NT:
                    cols = slice(P * j, P * j + P)
                    for i, src in enumerate((g.v[:, f, cols], g.Bt[:, f, cols], g.Kt[:, f, cols], g.AR[:, f, j, 0, :])):
                        mm = te.transpose(bank[:, P * i:P * i + P], src, g.ident[:, :])
                else:
                    _, _, t, hh = unit(j - NT)
                    for i, src in enumerate((g.Bt, g.Kt)):
                        mm = te.matmul(bank[:, 256 * i:256 * i + 256], src[rows(hh), f, P * t:P * t + P],
                                       g.AR[rows(hh), f, t, :, :].rearrange("p a n -> p (a n)"), start=True, stop=True)
                mm.then_inc(*pe(n))

            for n in pre_names(0):
                pre(0, n)
            for f in fts:
                tok = g.tok[:, f % 2, :, :, :]
                for h in halves:
                    te.wait_ge(*pool.at(f"i{f}{h}"))
                    if f:
                        te.wait_ge(*act.at(f"y0_{f - 1}{h}"))
                        te.wait_ge(*vec.at(f"r{f - 1}{h}"))
                    for u in range(4):
                        mm = te.transpose(ps[4 + 2 * h][:, P * u:P * u + P], TT[h][:, u, :], g.ident[:, :])
                    mm.then_inc(*pe(f"tr{f}{h}"))
                nxt = pre_names(f + 1) if f + 1 < FT else []
                for l in range(1, 6):
                    for h in halves:
                        te.wait_ge(*pool.at(f"off{f}{l}{h}"))
                        te.wait_ge(*(act.at(f"tr{f}{h}") if l == 1 else vec.at(f"t{f}{l - 1}{h}")))
                        for u in range(4):
                            mm = te.matmul(ps[4 + 2 * h][:, P * u:P * u + P], off[l % 2][h][:, u, :], T[h][:, u, :], start=True, stop=True)
                        mm.then_inc(*pe(f"xx{f}{l}{h}"))
                    for h in halves:
                        te.wait_ge(*act.at(f"xx{f}{l}{h}"))
                        if l > 1:
                            te.wait_ge(*vec.at(f"tt{f}{l - 1}{h}"))
                        elif f:
                            te.wait_ge(*vec.at(f"g{f - 1}{h}1"))
                        for u in range(4):
                            mm = te.matmul(ps[5 + 2 * h][:, P * u:P * u + P], X[h][:, u, :], TT[h][:, u, :], start=True, stop=True)
                        mm.then_inc(*pe(f"tt{f}{l}{h}"))
                        if l < 5:
                            for u in range(4):
                                mm = te.matmul(ps[4 + 2 * h][:, P * u:P * u + P], TT[h][:, u, :], X[h][:, u, :], start=True, stop=True)
                            mm.then_inc(*pe(f"t{f}{l}{h}"))
                    for n in nxt[3 * (l - 1):3 * l]:
                        pre(f + 1, n)
                for h in halves:
                    te.wait_ge(*act.at(f"xx{f}5{h}"))
                    te.wait_ge(*act.at(f"tm{f}{2 * h + 1}"))
                    for u in range(4):
                        _, _, t, hh = unit(4 * h + u)
                        mm = te.matmul(ps[4 + 2 * h][:, 64 * u:64 * u + 64], gm(f, 4 * h + u)[:, 256:384], tok[:, t, 0, 64 * hh:64 * hh + 64],
                                       start=True, stop=True)
                    mm.then_inc(*pe(f"x0{f}{h}"))
                for h in halves:
                    te.wait_ge(*act.at(f"x0{f}{h}"))
                    te.wait_ge(*vec.at(f"tt{f}5{h}"))
                    for u in range(4):
                        _, _, t, hh = unit(4 * h + u)
                        for at, rhs in ((0, tok[:, t, 3, 64 * hh:64 * hh + 64]), (64, X0[h][:, u, 0:64])):
                            mm = te.matmul(ps[5 + 2 * h][:, P * u + at:P * u + at + 64], TT[h][:, u, :], rhs, start=True, stop=True)
                    mm.then_inc(*pe(f"y1{f}{h}"))
                for h in halves:
                    te.wait_ge(*act.at(f"y1{f}{h}"))
                    for u in range(4):
                        _, _, t, hh = unit(4 * h + u)
                        m, at = gm(f, 4 * h + u), 256 * (u // 2)
                        te.matmul(ps[4 + 2 * h][rows(hh), at:at + P], Y1[h][:, u, 0:64], m[:, 128:256], start=True, stop=True)
                        mm = group(ps[4 + 2 * h][rows(hh), at + P:at + 2 * P],
                                   [(Y1[h][:, u, 64:P], m[:, 128:256]), (tok[:, t, 0, 64 * hh:64 * hh + 64], m[:, 384:512])])
                    mm.then_inc(*pe(f"ry{f}{h}"))
                for h in halves:
                    te.wait_ge(*vec.at(f"gm{min(f + 1, FT - 1)}{6 + h}"))
                    te.wait_ge(*act.at(f"y1{f}{h}"))
                    for u in range(4):
                        _, _, t, hh = unit(4 * h + u)
                        cols = slice(64 * hh, 64 * hh + 64)
                        for c in range(2):
                            bank, at = (ps[5 + 2 * h], ps[2 + h])[c], P * (u // 2)
                            te.matmul(bank[rows(hh), at:at + 64], Y1[h][rows(c), u, 0:64], tok[rows(c), t, 1, cols], start=True, stop=True)
                            mm = group(bank[rows(hh), at + 64:at + P],
                                       [(tok[rows(c), t, 1, cols], Y1[h][rows(c), u, 64:P]), (tok[rows(c), t, 2, cols], tok[rows(c), t, 0, cols])])
                    mm.then_inc(*pe(f"eg{f}{h}"))
            te.wait_ge(*vec.at("s_first"))
            te.wait_ge(*act.at("y0_31"))
            for c in range(NCH):
                if c:
                    te.wait_ge(*vec.at(f"s{c - 1}_3"))
                for f in fts:
                    for hh in range(2):
                        state = g.AR[rows(hh), f, c // 2, 0, 64 * (c % 2):64 * (c % 2) + 64]
                        mm = te.matmul(ps[4 + f][rows(hh), 64 * c:64 * c + 64], state,
                                       g.AR[rows(hh), f, c // 2, 1, 64 * (c % 2):64 * (c % 2) + 64], start=True, stop=True)
                mm.then_inc(*pe(f"y{c}"))
                if c == NCH - 1:
                    continue
                for f in fts:
                    for hh in range(2):
                        state = g.AR[rows(hh), f, c // 2, 0, 64 * (c % 2):64 * (c % 2) + 64]
                        mm = te.matmul(ps[c % 2][rows(hh), 64 * f:64 * f + 64], g.Bt[rows(hh), f, 64 * c:64 * c + 64], state, start=True, stop=True)
                mm.then_inc(*pe(f"s{c}"))
            for f in fts:
                te.wait_ge(*vec.at(f"y{f}"))
                te.matmul(ps[f][:, :], g.head_ones[:, :], g.v[:, f, :], start=True, stop=True).then_inc(*pe(f"mean{f}"))
            for f in fts:
                te.wait_ge(*act.at(f"ysq{f}"))
                mm = te.matmul(ps[4][0:HEADS, :], g.by_head[:, f, :], ysq[:, f % 2, :], start=(f == 0), stop=(f == FT - 1))
                if f < 2:
                    mm.then_inc(g.squares_used, 1)
            mm.then_inc(*pe("var"))
            te.wait_ge(*vec.at("rs"))
            for f in fts:
                te.matmul(ps[4 + f][:, :], g.from_head[:, f, :], g.inv_dev[:, :], start=True, stop=True).then_inc(*pe(f"rs{f}"))

        @block.gpsimd
        def _(po):
            for f in fts:
                def masked(l, h):
                    src = gm_buf[f % 2][:, 4 * h:4 * h + 4, 0:P]
                    mask = g.level_mask[:, l:l + 1, :].broadcast_to([P, 4, P])
                    po.tensor_tensor(off[l % 2][h], src, mask, ALU.mult).then_inc(*pool(f"off{f}{l}{h}"))

                for h in halves:
                    po.wait_ge(*vec.at(f"gm{f}{4 * h + 3}"))
                    if f:
                        po.wait_ge(*pe.at(f"y1{f - 1}{h}"))
                    masked(0, h)
                for h in halves:
                    po.wait_ge(*pool.at(f"off{f}0{h}"))
                    eye = g.ident[:, :].unsqueeze(1).broadcast_to([P, 4, P])
                    po.tensor_tensor(TT[h], off[0][h], eye, ALU.add).then_inc(*pool(f"i{f}{h}"))
                for l in range(1, 6):
                    for h in halves:
                        if l >= 2:
                            po.wait_ge(*(pool.at(f"i{f}{h}") if l == 2 else pe.at(f"xx{f}{l - 2}{h}")))
                        masked(l, h)
            for f in fts:
                po.wait_ge(*vec.at(f"ya{f}"))
                po.tensor_tensor(g.yT[:, f, :], yc_of(f), g.gate[:, f, :], ALU.mult).then_inc(*pool(f"yT{f}"))

        @block.scalar
        def _(sc):
            for n in order:
                k = n[0:2]
                if k == "tm":
                    f, t = int(n[2]), int(n[3])
                    if f >= 2:
                        sc.wait_ge(*pe.at(f"eg{f - 2}1"))
                    sc.wait_ge(*pe.at(n))
                    sc.copy(g.tok[:, f % 2, t, :, :].rearrange("p a n -> p (a n)"), pre_bank[n][:, :]).then_inc(*act(n))
                elif k in ("tr", "x0", "y1"):
                    f, h = int(n[2]), int(n[3])
                    sc.wait_ge(*pe.at(n))
                    dst = {"tr": T, "x0": X0, "y1": Y1}[k][h]
                    n_cols = 64 if k == "x0" else P
                    src = ps[(5 if k == "y1" else 4) + 2 * h][:, 0:4 * n_cols]
                    sc.copy(dst[:, :, 0:n_cols], as_units(src)).then_inc(*act(n))
                elif n[0] == "x":
                    h = int(n[4])
                    sc.wait_ge(*pe.at(n))
                    sc.copy(X[h], as_units(ps[4 + 2 * h][:, :])).then_inc(*act(n))
                elif k == "ry":
                    f, h = int(n[2]), int(n[3])
                    sc.wait_ge(*vec.at(f"r{f}{h}"))
                    src = ps[4 + 2 * h][:, :].rearrange("p (t x n) -> p t x n", t=2, x=2)[:, :, 1, :]
                    sc.copy(g.v[:, f, 256 * h:256 * h + 256].rearrange("p (t n) -> p t n", t=2), src).then_inc(*act(f"y0_{f}{h}"))
            for f in fts:
                sc.wait_ge(*vec.at(f"mean{f}"))
                if f >= 2:
                    sc.wait_ge(g.squares_used, f - 1)
                sc.activation(ysq[:, f % 2, :], yc_of(f), ACT.Square).then_inc(*act(f"ysq{f}"))
            sc.wait_ge(*pe.at("var"))
            sc.activation(g.inv_dev[:, :], ps[4][0:HEADS, :], ACT.Sqrt, bias=g.eps[0:HEADS, 1:2], scale=1.0 / DV).then_inc(*act("std"))

        @block.vector
        def _(ve):
            for n in order:
                if n[0:2] == "gm":
                    f, u = int(n[2]), int(n[3])
                    ve.wait_ge(*pe.at(n))
                    if f >= 2:
                        ve.wait_ge(*pe.at(f"ry{f - 2}1"))
                    mask = g.gram_mask[:, :, :].rearrange("p a n -> p (a n)").unsqueeze(1).broadcast_to([P, 2, 256])
                    ve.tensor_tensor(gm(f, u).rearrange("p (x n) -> p x n", x=2), pre_bank[n][:, :].rearrange("p (x n) -> p x n", x=2),
                                     mask, ALU.mult).then_inc(*vec(n))
                elif n[0:2] == "tt" or (n[0] == "t" and n[1].isdigit()):
                    h = int(n[-1])
                    ve.wait_ge(*pe.at(n))
                    dst, b = (TT, 5) if n[0:2] == "tt" else (T, 4)
                    if n[0:2] == "tt" and f"t{n[2:]}" in pe.value:
                        ve.wait_ge(*pe.at(f"t{n[2:]}"))
                    ve.tensor_tensor(dst[h], as_units(ps[b + 2 * h][:, :]), dst[h], ALU.add).then_inc(*vec(n))
                elif n[0:2] == "ry":
                    f, h = int(n[2]), int(n[3])
                    ve.wait_ge(*pe.at(n))
                    src = ps[4 + 2 * h][:, :].rearrange("p (t x n) -> p t x n", t=2, x=2)[:, :, 0, :]
                    dst = g.AR[:, f, 2 * h:2 * h + 2, 1, :]
                    ve.tensor_tensor(dst, src, dst, ALU.add).then_inc(*vec(f"r{f}{h}"))
                elif n[0:2] == "eg":
                    f, h = int(n[2]), int(n[3])
                    ve.wait_ge(*pe.at(n))
                    for c in range(2):
                        src = (ps[5 + 2 * h], ps[2 + h])[c][:, 0:2 * P].rearrange("p (t x n) -> p t x n", t=2, x=2)
                        part = lambda buf: buf[:, f, 256 * h:256 * h + 256].rearrange("p (t c n) -> p t c n", t=2, c=2)[:, :, c, :]
                        eye = g.eye64[:, :].unsqueeze(1).broadcast_to([P, 2, 64])
                        w = g.w_end[:, f, 4 * h:4 * h + 4].rearrange("p (t c) -> p t c", t=2)[:, :, c:c + 1].broadcast_to([P, 2, 64])
                        ve.tensor_tensor(part(g.Bt), src[:, :, 0, :], eye, ALU.add).then_inc(*vec(f"e{f}{h}{c}"))
                        ve.tensor_tensor(part(g.Kt), src[:, :, 1, :], w, ALU.mult).then_inc(*vec(f"g{f}{h}{c}"))
            ve.wait_ge(*pe.at("eg31"))
            ve.memset(g.AR[:, :, 0, 0, 0:64], 0.0).then_inc(*vec("s_first"))
            for c in range(NCH - 1):
                ve.wait_ge(*pe.at(f"s{c}"))
                for f in fts:
                    at = c + 1
                    dst = g.AR[:, f, at // 2, 0, 64 * (at % 2):64 * (at % 2) + 64]
                    ve.scalar_tensor_tensor(dst, ps[c % 2][:, 64 * f:64 * f + 64], g.w_end[:, f, c:c + 1], g.Kt[:, f, 64 * c:64 * c + 64],
                                            ALU.mult, ALU.add).then_inc(*vec(f"s{c}_{f}"))
                if c < FT:
                    ve.tensor_scalar(g.bv[:, c, :], g.bv[:, c, :], g.col("ln_b", c), None, ALU.add).then_inc(*vec(f"lb{c}"))
            for f in fts:
                ve.wait_ge(*pe.at(f"y{NCH - 1}"))
                ve.wait_ge(*act.at(f"y0_{f}1"))
                ve.tensor_tensor(g.v[:, f, :], ps[4 + f][:, :], g.v[:, f, :], ALU.add).then_inc(*vec(f"y{f}"))
            for f in fts:
                ve.wait_ge(*pe.at(f"mean{f}"))
                ve.wait_ge(*vec.at(f"y{f}"))
                ve.scalar_tensor_tensor(yc_of(f), ps[f][:, :], -1.0 / DV, g.v[:, f, :], ALU.mult, ALU.add).then_inc(*vec(f"mean{f}"))
            ve.wait_ge(*act.at("std"))
            ve.reciprocal(g.inv_dev[:, :], g.inv_dev[:, :]).then_inc(*vec("rs"))
            for f in fts:
                ve.wait_ge(*pe.at(f"rs{f}"))
                ve.tensor_tensor(yc_of(f), ps[4 + f][:, :], yc_of(f), ALU.mult).then_inc(*vec(f"yn{f}"))
                ve.wait_ge(*vec.at(f"yn{f}"))
                ve.scalar_tensor_tensor(yc_of(f), yc_of(f), g.col("ln_w", f), g.bv[:, f, :], ALU.mult, ALU.add).then_inc(*vec(f"ya{f}"))


def phase_mla(nc, g):
    with ExitStack() as ctx:
        (g.w_q, g.w_kv, g.cn, g.cT, g.qk, g.sqk, g.rope, g.v_tok, g.probT, g.o_tok, g.ss2, g.ssn, g.stat, g.trig, g.ang, g.turns,
         g.posf, g.junk2) = g.sb(ctx, w_q=([P, 2, HEADS * QK], F32), w_kv=([P, HEADS * (NOPE + DV)], F32), cn=([P, NT, Q_LORA + KV_LORA], F32),
             cT=([P, 3, SEQ], F32), qk=([P, 2, 2 * HEADS, QK], F32), sqk=([P, 2 * HEADS, QK], F32), rope=([P, 2, 4, 2 * HEADS, HALF], F32),
             v_tok=([P, NT, HEADS * DV], F32), probT=([P, 2, SEQ], F32), o_tok=([P, NT, HEADS * DV], F32),
             ss2=([P, NT, 2], F32), ssn=([P, NT, 2 * HEADS], F32), stat=([P, 4, NT * HEADS], F32), trig=([P, 2, NT, HALF], F32),
             ang=([P, NT, HALF], F32), turns=([P, 2, NT, HALF], F32), posf=([P, NT], F32), junk2=([P, Q_LORA], F32))
        qkT = [buf[0:QK, :, :].rearrange("p a (b n) -> p (a b) n", n=SEQ) for buf in (g.x, g.mod)]
        prob = g.qk[:, 0, :, :].rearrange("p h n -> p (h n)").rearrange("p (a n) -> p a n", n=SEQ)
        w_in = g.sem(ctx, "mla_weights_in")
        ts, units = range(NT), range(NT * HEADS)
        SCALE = float(QK) ** -0.5
        maxs, negs, sums, rsums = (g.stat[:, i, :] for i in range(4))
        act = g.steps(ctx, "d_act", [f"{x}{t}" for t in ts for x in ("sqq", "sqk")] + ["stq", "stk"] + names("ct{}", 3) + ["sin"]
                      + [n for t in ts for n in [f"{x}{t}" for x in ("q0_", "q1_", "kn0_", "vv0_", "kn1_", "vv1_", "kr", "sq", "sn")]
                         + ([f"tq{t - 1}{j}" for j in range(4)] if t else [])] + names("tq3{}", 4) + [x for u in units for x in [f"ex{u}"] + ([f"pc{u - 1}"] if u else [])]
                      + [f"pc{len(units) - 1}"] + names("ot{}", 4))
        vec = g.steps(ctx, "d_vec", ["rc"] + [f"{x}{t}" for t in ts for x in ("cq", "ck")] + ["posf"] + names("ang{}", NT)
                      + ["n0", "n1", "n2", "n3"] + [f"r{j}{i}" for j in range(2) for i in range(3)] + ["shift", "cl0", "cl1"]
                      + [f"{x}{t}" for t in ts for x in ("red", "rn", "nq", "c1_", "s2_", "c2_", "s1_", "o1_", "o2_")]
                      + [x for u in units for x in ([f"ov{u - 3}"] if u >= 3 else []) + [f"mx{u}", f"ng{u}"] + ([f"rs{u - 1}"] if u else [])] + [f"rs{len(units) - 1}", f"ov{len(units) - 3}", f"ov{len(units) - 2}", f"ov{len(units) - 1}"])
        pool = g.steps(ctx, "d_pool", names("nw{}", NT))
        outs = [f"{x}{t}" for t in ts for x in ("q0_", "q1_", "kv0_", "kv1_")]
        tqs = [f"tq{t}{j}" for t in ts for j in range(4)]
        pe_names = names("ct{}", 3) + outs[0:4]
        for t in ts:
            pe_names += outs[4 * (t + 1):4 * (t + 2)] + tqs[4 * t:4 * t + 4]
        pe_names += ["s0", "s1"]
        for u in units:
            pe_names += ([f"s{u + 2}"] if u + 2 < len(units) else []) + [f"pt{u}"] + ([f"o{u - 1}"] if u else [])
        pe_names += [f"o{len(units) - 1}"] + names("ot{}", 4)
        pe = g.steps(ctx, "d_pe", pe_names)
        block = ctx.enter_context(nc.Block())
        ps = g.ps
        last = len(units) - 1

        @block.sync
        def _(sp):
            sp.dma_start(g.w_q[:, :, :], g.a["w_q_up"][0].rearrange("(k p) n -> p k n", p=P)).then_inc(w_in, 16)
            sp.dma_start(g.w_kv[:, :], g.a["w_kv_up"][0]).then_inc(w_in, 16)
            for i in range(OA, OA + RING):
                load_chunk(g, sp, i)

        @block.tensor
        def _(te):
            for j in range(3):
                te.wait_ge(*vec.at("ck3" if j == 2 else "cq3"))
                for t in ts:
                    mm = te.transpose(ps[j][:, P * t:P * t + P], g.cn[:, t, P * j:P * j + P], g.ident[:, :])
                mm.then_inc(*pe(f"ct{j}"))

            def up(t):
                at = slice(P * t, P * t + P)
                for i in range(2):
                    if t:
                        te.wait_ge(*act.at(f"q{i}_{t - 1}"))
                    else:
                        te.wait_ge(*act.at("ct2"))
                    for k in range(2):
                        mm = te.matmul(ps[i][:, 0:384], g.cT[:, k, at], g.w_q[:, k, 384 * i:384 * i + 384], start=(k == 0), stop=(k == 1))
                    mm.then_inc(*pe(f"q{i}_{t}"))
                for i in range(2):
                    if t:
                        te.wait_ge(*act.at(f"vv{i}_{t - 1}"))
                    te.matmul(ps[2 + i][:, :], g.cT[:, 2, at], g.w_kv[:, 512 * i:512 * i + 512], start=True, stop=True).then_inc(*pe(f"kv{i}_{t}"))

            te.wait_ge(w_in, 32)
            up(0)
            for t in ts:
                if t + 1 < NT:
                    up(t + 1)
                te.wait_ge(*vec.at(f"o2_{t}"))
                for j in range(4):
                    if t:
                        te.wait_ge(*act.at(f"tq{t - 1}{j}"))
                    for h in range(4):
                        mm = te.transpose(ps[4 + j][0:QK, P * h:P * h + P], g.qk[:, t % 2, 4 * j + h, :], g.ident[:, :])
                    mm.then_inc(*pe(f"tq{t}{j}"))

            def scores(u):
                qt, h = u // HEADS, u % HEADS
                if u >= 3:
                    te.wait_ge(*act.at(f"ex{u - 3}"))
                bank, n = ps[u % 3], P * (qt + 1)
                te.matmul(bank[:, 0:n], qkT[0][:, h, P * qt:n], qkT[1][:, h, 0:n], start=True, stop=False)
                te.matmul(bank[:, n - P:n], g.ident[:, :], g.causal[:, :], start=False, stop=True).then_inc(*pe(f"s{u}"))

            def turn(u):
                qt = u // HEADS
                te.wait_ge(*act.at(f"ex{u}"))
                if u >= 2:
                    te.wait_ge(*act.at(f"pc{u - 2}"))
                for kt in range(qt + 1):
                    mm = te.transpose(ps[3 + u % 2][:, P * kt:P * kt + P], prob[:, u % 3, P * kt:P * kt + P], g.ident[:, :])
                mm.then_inc(*pe(f"pt{u}"))

            def values(u):
                qt, h = u // HEADS, u % HEADS
                te.wait_ge(*act.at(f"pc{u}"))
                if u >= 2:
                    te.wait_ge(*vec.at(f"ov{u - 2}"))
                for kt in range(qt + 1):
                    mm = te.matmul(ps[5 + u % 2][:, 0:DV], g.probT[:, u % 2, P * kt:P * kt + P], g.v_tok[:, kt, DV * h:DV * h + DV],
                                   start=(kt == 0), stop=(kt == qt))
                mm.then_inc(*pe(f"o{u}"))

            te.wait_ge(*act.at("tq33"))
            scores(0)
            scores(1)
            for u in units:
                if u + 2 <= last:
                    scores(u + 2)
                turn(u)
                if u:
                    values(u - 1)
            values(last)
            te.wait_ge(*vec.at(f"ov{last}"))
            for j in range(4):
                for t in ts:
                    mm = te.transpose(ps[j][:, P * t:P * t + P], g.o_tok[:, t, P * j:P * j + P], g.ident[:, :])
                mm.then_inc(*pe(f"ot{j}"))

        @block.gpsimd
        def _(po):
            for t in ts:
                po.wait_ge(*vec.at(f"nq{t}"))
                x = g.qk[:, t % 2, :, :].rearrange("p (a h) n -> p a h n", a=2)
                for i in range(1):
                    w = g.qk_w[:, :, :].unsqueeze(2).broadcast_to([P, 2, HEADS, QK])
                    po.tensor_tensor(x, x, w, ALU.mult).then_inc(*pool(f"nw{t}"))

        @block.scalar
        def _(sc):
            for t in ts:
                for n, lo, hi, i in (("sqq", 0, Q_LORA, 0), ("sqk", Q_LORA, Q_LORA + KV_LORA, 1)):
                    if t or i:
                        sc.wait_ge(*act.at(f"sqq{t}" if i else f"sqk{t - 1}"))
                    sc.activation(g.junk2[:, 0:hi - lo], g.mla_in[:, t, lo:hi], ACT.Square, accum_out=g.ss2[:, t, i:i + 1]).then_inc(*act(f"{n}{t}"))
            sc.wait_ge(*act.at("sqk3"))
            for i, n, k in ((0, "stq", Q_LORA), (1, "stk", KV_LORA)):
                sc.activation(g.ss2[:, :, i], g.ss2[:, :, i], ACT.Sqrt, bias=g.eps[:, 0:1], scale=1.0 / k).then_inc(*act(n))
            for j in range(3):
                sc.wait_ge(*pe.at(f"ct{j}"))
                w = g.col("q_a_norm_w", j) if j < 2 else g.col("kv_a_norm_w")
                sc.activation(g.cT[:, j, :], ps[j][:, :], ACT.Copy, scale=w).then_inc(*act(f"ct{j}"))
            sc.wait_ge(*vec.at("cl1"))
            sc.activation(g.trig[:, :, :, :], g.turns[:, :, :, :], ACT.Sin).then_inc(*act("sin"))

            def turned(t):
                for j in range(4):
                    sc.wait_ge(*pe.at(f"tq{t}{j}"))
                    dst = qkT[j // 2][:, 4 * (j % 2):4 * (j % 2) + 4, P * t:P * t + P]
                    sc.copy(dst, ps[4 + j][0:QK, :].rearrange("p (h n) -> p h n", h=4)).then_inc(*act(f"tq{t}{j}"))

            for t in ts:
                x = g.qk[:, t % 2, :, :]
                if t >= 2:
                    sc.wait_ge(*pe.at(f"tq{t - 2}3"))
                for i in range(2):
                    sc.wait_ge(*pe.at(f"q{i}_{t}"))
                    sc.copy(x[:, 4 * i:4 * i + 4, :], ps[i][:, 0:384].rearrange("p (h n) -> p h n", h=4)).then_inc(*act(f"q{i}_{t}"))
                for i in range(2):
                    kv = ps[2 + i][:, :].rearrange("p (h n) -> p h n", h=4)
                    sc.wait_ge(*pe.at(f"kv{i}_{t}"))
                    sc.copy(x[:, 8 + 4 * i:12 + 4 * i, 0:NOPE], kv[:, :, 0:NOPE]).then_inc(*act(f"kn{i}_{t}"))
                    sc.copy(g.v_tok[:, t, 256 * i:256 * i + 256].rearrange("p (h n) -> p h n", h=4), kv[:, :, NOPE:]).then_inc(*act(f"vv{i}_{t}"))
                kr = g.mla_in[:, t:t + 1, Q_LORA + KV_LORA:].broadcast_to([P, HEADS, ROPE])
                sc.copy(x[:, 8:16, NOPE:QK], kr).then_inc(*act(f"kr{t}"))
                sc.wait_ge(*act.at(f"kr{t}"))
                if t:
                    sc.wait_ge(*vec.at(f"red{t - 1}"))
                sc.activation(g.sqk[:, :, :], x, ACT.Square).then_inc(*act(f"sq{t}"))
                sc.wait_ge(*vec.at(f"red{t}"))
                sc.activation(g.ssn[:, t, :], g.ssn[:, t, :], ACT.Sqrt, bias=g.eps[:, 0:1], scale=1.0 / QK).then_inc(*act(f"sn{t}"))
                if t:
                    turned(t - 1)
            turned(NT - 1)

            def probs_copy(u):
                n = P * (u // HEADS + 1)
                sc.wait_ge(*pe.at(f"pt{u}"))
                if u >= 2:
                    sc.wait_ge(*pe.at(f"o{u - 2}"))
                sc.copy(g.probT[:, u % 2, 0:n], ps[3 + u % 2][:, 0:n]).then_inc(*act(f"pc{u}"))

            for u in units:
                n = P * (u // HEADS + 1)
                sc.wait_ge(*vec.at(f"ng{u}"))
                sc.activation(prob[:, u % 3, 0:n], ps[u % 3][:, 0:n], ACT.Exp, bias=negs[:, u:u + 1], scale=SCALE,
                              accum_out=sums[:, u:u + 1]).then_inc(*act(f"ex{u}"))
                if u:
                    probs_copy(u - 1)
            probs_copy(last)
            for j in range(4):
                sc.wait_ge(*pe.at(f"ot{j}"))
                sc.copy(g.oT[:, j, :], ps[j][:, :]).then_inc(*act(f"ot{j}"))

        @block.vector
        def _(ve):
            ve.wait_ge(*act.at("stk"))
            ve.reciprocal(g.ss2[:, :, :], g.ss2[:, :, :]).then_inc(*vec("rc"))
            ve.wait_ge(*vec.at("rc"))
            for t in ts:
                for n, lo, hi, i in (("cq", 0, Q_LORA, 0), ("ck", Q_LORA, Q_LORA + KV_LORA, 1)):
                    ve.tensor_scalar(g.cn[:, t, lo:hi], g.mla_in[:, t, lo:hi], g.ss2[:, t, i:i + 1], None, ALU.mult).then_inc(*vec(f"{n}{t}"))
            ve.tensor_copy(g.posf[:, :], g.pos[:, :]).then_inc(*vec("posf"))
            ve.wait_ge(*vec.at("posf"))
            for t in ts:
                ve.tensor_scalar(g.ang[:, t, :], g.freq[:, :], g.posf[:, t:t + 1], None, ALU.mult).then_inc(*vec(f"ang{t}"))
            ve.wait_ge(*vec.at("ang3"))
            ve.tensor_scalar(g.turns[:, 0, :, :], g.ang[:, :, :], 1.0 / TWO_PI, 0.25, ALU.mult, ALU.add).then_inc(*vec("n0"))
            ve.tensor_scalar(g.turns[:, 1, :, :], g.ang[:, :, :], 1.0 / TWO_PI, None, ALU.mult).then_inc(*vec("n1"))
            ve.wait_ge(*vec.at("n1"))
            ve.tensor_scalar(g.turns[:, :, :, :], g.turns[:, :, :, :], ROUND, None, ALU.add).then_inc(*vec("n2"))
            ve.wait_ge(*vec.at("n2"))
            ve.tensor_scalar(g.turns[:, :, :, :], g.turns[:, :, :, :], -ROUND, None, ALU.add).then_inc(*vec("n3"))
            ve.wait_ge(*vec.at("n3"))
            for j in range(2):
                rest = g.ang[:, :, :]
                for i, part in enumerate(TURN_PARTS):
                    dst = g.trig[:, j, :, :]
                    ve.scalar_tensor_tensor(dst, g.turns[:, j, :, :], -part, rest, ALU.mult, ALU.add).then_inc(*vec(f"r{j}{i}"))
                    ve.wait_ge(*vec.at(f"r{j}{i}"))
                    rest = dst
            ve.tensor_scalar(g.trig[:, 0, :, :], g.trig[:, 0, :, :], TWO_PI / 4, None, ALU.add).then_inc(*vec("shift"))
            ve.wait_ge(*vec.at("shift"))
            ve.tensor_scalar(g.turns[:, :, :, :], g.trig[:, :, :, :], PI_BELOW, None, ALU.min).then_inc(*vec("cl0"))
            ve.wait_ge(*vec.at("cl0"))
            ve.tensor_scalar(g.turns[:, :, :, :], g.turns[:, :, :, :], -PI_BELOW, None, ALU.max).then_inc(*vec("cl1"))
            for t in ts:
                x = g.qk[:, t % 2, :, :]
                ve.wait_ge(*act.at(f"sq{t}"))
                ve.tensor_reduce(g.ssn[:, t, :], g.sqk[:, :, :], AX_X, ALU.add).then_inc(*vec(f"red{t}"))
                ve.wait_ge(*act.at(f"sn{t}"))
                ve.reciprocal(g.ssn[:, t, :], g.ssn[:, t, :]).then_inc(*vec(f"rn{t}"))
                ve.wait_ge(*vec.at(f"rn{t}"))
                ve.tensor_tensor(x, x, g.ssn[:, t, :].unsqueeze(2).broadcast_to([P, 2 * HEADS, QK]), ALU.mult).then_inc(*vec(f"nq{t}"))
                ve.wait_ge(*pool.at(f"nw{t}"))
                ve.wait_ge(*act.at("sin"))
                x1, x2 = x[:, :, NOPE:NOPE + HALF], x[:, :, NOPE + HALF:QK]
                cos, sin = (g.trig[:, i, t:t + 1, :].broadcast_to([P, 2 * HEADS, HALF]) for i in range(2))
                tmp = [g.rope[:, t % 2, i, :, :] for i in range(4)]
                for i, (n, xx, f) in enumerate((("c1_", x1, cos), ("s2_", x2, sin), ("c2_", x2, cos), ("s1_", x1, sin))):
                    ve.tensor_tensor(tmp[i], xx, f, ALU.mult).then_inc(*vec(f"{n}{t}"))
                ve.wait_ge(*vec.at(f"s1_{t}"))
                ve.tensor_tensor(x1, tmp[0], tmp[1], ALU.subtract).then_inc(*vec(f"o1_{t}"))
                ve.tensor_tensor(x2, tmp[2], tmp[3], ALU.add).then_inc(*vec(f"o2_{t}"))

            def output(u):
                qt, h = u // HEADS, u % HEADS
                ve.wait_ge(*pe.at(f"o{u}"))
                ve.wait_ge(*vec.at(f"rs{u}"))
                ve.tensor_scalar(g.o_tok[:, qt, DV * h:DV * h + DV], ps[5 + u % 2][:, 0:DV], rsums[:, u:u + 1], None, ALU.mult).then_inc(*vec(f"ov{u}"))

            def inverse(u):
                ve.wait_ge(*act.at(f"ex{u}"))
                ve.reciprocal(rsums[:, u:u + 1], sums[:, u:u + 1]).then_inc(*vec(f"rs{u}"))

            for u in units:
                if u >= 3:
                    output(u - 3)
                ve.wait_ge(*pe.at(f"s{u}"))
                ve.tensor_reduce(maxs[:, u:u + 1], ps[u % 3][:, 0:P * (u // HEADS + 1)], AX_X, ALU.max).then_inc(*vec(f"mx{u}"))
                ve.wait_ge(*vec.at(f"mx{u}"))
                ve.tensor_scalar(negs[:, u:u + 1], maxs[:, u:u + 1], -SCALE, None, ALU.mult).then_inc(*vec(f"ng{u}"))
                if u:
                    inverse(u - 1)
            inverse(last)
            output(last - 2)
            output(last - 1)
            output(last)


def phase_output(nc, g):
    with ExitStack() as ctx:
        piece = ([P, 2, KD, 256], F32R)
        whole = ([P, KD, SEQ], F32R)
        (g.g_hi, g.g_lo, g.l_hi, g.l_lo, g.gated) = g.sb(ctx, g_hi=piece, g_lo=piece, l_hi=whole, l_lo=whole, gated=([P, 2, 512], F32))
        merged, sig_b = (buf[:, :, :].rearrange("p a (b n) -> p (a b) n", n=SEQ) for buf in (g.x, g.mod))
        ks, ts = range(KD), range(NT)
        rows_in = g.sem(ctx, "rows_back")
        tiles = [f"{x}{i}" for x in ("oa", "ob", "ga", "gb") for i in ks] + [f"w{t}{n}" for n in range(4) for t in ts]
        pieces = [(GA + i // 2, i % 2) for i in range(4)] + [(GB + i // 2, i % 2) for i in range(4)] + [(WOUT + i // 2, i % 2) for i in range(4)]
        through = [f"g{x}{2 * i + 1}" for x in "ab" for i in range(4)] + [f"w3{n}" for n in range(4)]
        pe = g.steps(ctx, "e_pe", tiles)
        act = g.steps(ctx, "e_act", names("hT{}", 2) + names("oa{}", 4) + ["p0"] + names("oa{}", 8)[4:] + ["p1"]
                      + [x for i in range(4) for x in (f"ga{2 * i}", f"ga{2 * i + 1}", f"p{i + 2}")]
                      + [x for i in range(4) for x in (f"gb{2 * i}", f"gb{2 * i + 1}", f"p{i + 6}")]
                      + names("m{}", 8) + ["p10", "p11"])
        both = [x for i in ks for x in ((f"gb{i}", f"m{i}") + ((f"p{6 + i // 2}",) if i % 2 else ()))]
        evens = [x for n in range(4) for t in ts for x in ([f"w{t}{n}", f"x_w{t}{n}"] + ([f"p{n + 9}"] if t == 0 and n in (1, 2) else []))]
        vec = g.steps(ctx, "e_vec", names("hT{}", 2) + names("ob{}", 4) + ["p0"] + names("ob{}", 8)[4:] + ["p1"]
                      + [x for i in range(4) for x in (f"ga{2 * i}", f"ga{2 * i + 1}", f"p{i + 2}")] + both + names("s{}", 8) + evens)
        block = ctx.enter_context(nc.Block())
        bank = {n: g.ps[j % 8] for j, n in enumerate(tiles)}
        reader = {n: (act if n[0] == "g" or n[:2] == "oa" else vec) for n in tiles}

        @block.sync
        def _(sp):
            for i, s, last in ((OA, pe, "oa7"), (OB, pe, "ob7"), (GA, vec, "p1"), (GA + 1, vec, "p3"), (GB, vec, "p5")):
                sp.wait_ge(*s.at(last))
                load_chunk(g, sp, i + RING)
            sp.wait_ge(*vec.at("s7"))
            sp.dma_start(g.x[:, :, :], g.a["x"][0].rearrange("(t p) d -> p t d", p=P)).then_inc(rows_in, 16)
            sp.wait_ge(g.mod_out, 16)
            sp.dma_start(g.mod[:, :, :], g.mod_rows.partition_broadcast(P).rearrange("p a r n -> p (a r) n")).then_inc(rows_in, 16)

        @block.tensor
        def _(te):
            def product(name, pairs, cols=SEQ, first=False):
                j = tiles.index(name)
                if j >= 8:
                    te.wait_ge(*reader[tiles[j - 8]].at(tiles[j - 8]))
                for n, (lhsT, rhs) in enumerate(pairs):
                    if first and n % 3 == 0:
                        te.wait_ge(*vec.at(f"s{n // 3}"))
                    mm = te.matmul(bank[name][:, 0:cols], lhsT, rhs, start=(n == 0), stop=(n == len(pairs) - 1))
                mm.then_inc(*pe(name))

            for x, o, src in (("a", OA, g.oT), ("b", OB, g.yT)):
                te.wait_ge(*chunk_loaded(g, o))
                for i in ks:
                    product(f"o{x}{i}", [(slot(g, o)[:, k, P * i:P * i + P], src[:, k, :]) for k in range(FT)])
            for x in "ab":
                for i in ks:
                    n = 4 * (x == "b") + i // 2
                    te.wait_ge(*vec.at(f"p{n}"))
                    at = slice(P * (i % 2), P * (i % 2) + P)
                    w_hi, w_lo = g.g_hi[:, n % 2, :, at], g.g_lo[:, n % 2, :, at]
                    product(f"g{x}{i}", [y for k in ks for y in ((w_hi[:, k, :], g.l_hi[:, k, :]), (w_hi[:, k, :], g.l_lo[:, k, :]),
                                                                 (w_lo[:, k, :], g.l_hi[:, k, :]))])
            for n in range(4):
                te.wait_ge(*vec.at(f"p{8 + n}"))
                w_hi, w_lo = g.g_hi[:, n % 2, :, :], g.g_lo[:, n % 2, :, :]
                for t in ts:
                    at = slice(P * t, P * t + P)
                    product(f"w{t}{n}", [y for k in ks for y in ((g.l_hi[:, k, at], w_hi[:, k, :]), (g.l_hi[:, k, at], w_lo[:, k, :]),
                                                                 (g.l_lo[:, k, at], w_hi[:, k, :]))], 256, n == 0 and t == 0)

        def piece_of(n):
            chunk, half = pieces[n]
            return slot(g, chunk)[:, :, 256 * half:256 * half + 256]

        @block.scalar
        def _(sc):
            def split_hi(n):
                sc.wait_ge(*chunk_loaded(g, pieces[n][0]))
                if n >= 2:
                    sc.wait_ge(*pe.at(through[n - 2]))
                sc.copy(g.g_hi[:, n % 2, :, :], piece_of(n)).then_inc(*act(f"p{n}"))

            def sigmoid(x, i):
                sc.wait_ge(*pe.at(f"{x}{i}"))
                if i >= 2:
                    sc.wait_ge(*vec.at(f"{x}{i - 2}"))
                elif x == "gb":
                    sc.wait_ge(*vec.at(f"ga{i + 6}"))
                sc.activation(g.gated[:, i % 2, :], bank[f"{x}{i}"][:, :], ACT.Sigmoid).then_inc(*act(f"{x}{i}"))

            def branch(i):
                sc.wait_ge(*pe.at(f"oa{i}"))
                sc.copy(merged[:, i, :], bank[f"oa{i}"][:, :]).then_inc(*act(f"oa{i}"))

            def merged_hi(i):
                sc.wait_ge(*vec.at(f"m{i}"))
                if i == 0:
                    sc.wait_ge(*pe.at("gb7"))
                sc.copy(g.l_hi[:, i, :], merged[:, i, :]).then_inc(*act(f"m{i}"))

            for i in range(2):
                sc.copy(g.l_hi[:, 4 * i:4 * i + 4, :], g.hT[:, 4 * i:4 * i + 4, :]).then_inc(*act(f"hT{i}"))
            for i in range(4):
                branch(i)
            split_hi(0)
            for i in range(4, 8):
                branch(i)
            split_hi(1)
            for i in range(4):
                sigmoid("ga", 2 * i)
                sigmoid("ga", 2 * i + 1)
                split_hi(i + 2)
            for i in range(4):
                sigmoid("gb", 2 * i)
                sigmoid("gb", 2 * i + 1)
                split_hi(i + 6)
            for i in ks:
                merged_hi(i)
            split_hi(10)
            split_hi(11)

        @block.vector
        def _(ve):
            def split_lo(n):
                ve.wait_ge(*act.at(f"p{n}"))
                ve.tensor_tensor(g.g_lo[:, n % 2, :, :], piece_of(n), g.g_hi[:, n % 2, :, :].bitcast(F32), ALU.subtract).then_inc(*vec(f"p{n}"))

            for i in range(2):
                at = slice(4 * i, 4 * i + 4)
                ve.wait_ge(*act.at(f"hT{i}"))
                ve.tensor_tensor(g.l_lo[:, at, :], g.hT[:, at, :], g.l_hi[:, at, :].bitcast(F32), ALU.subtract).then_inc(*vec(f"hT{i}"))
            def branch(i):
                ve.wait_ge(*pe.at(f"ob{i}"))
                ve.tensor_copy(sig_b[:, i, :], bank[f"ob{i}"][:, :]).then_inc(*vec(f"ob{i}"))

            def gate(x, dst, i):
                ve.wait_ge(*act.at(f"{x}{i}"))
                ve.wait_ge(*(vec.at(f"ob{i}") if x == "gb" else act.at(f"oa{i}")))
                ve.tensor_tensor(dst[:, i, :], g.gated[:, i % 2, :], dst[:, i, :], ALU.mult).then_inc(*vec(f"{x}{i}"))

            def merged_lo(i):
                ve.wait_ge(*act.at(f"m{i}"))
                ve.tensor_tensor(g.l_lo[:, i, :], merged[:, i, :], g.l_hi[:, i, :].bitcast(F32), ALU.subtract).then_inc(*vec(f"s{i}"))

            for i in range(4):
                branch(i)
            split_lo(0)
            for i in range(4, 8):
                branch(i)
            split_lo(1)
            for i in range(4):
                gate("ga", merged, 2 * i)
                gate("ga", merged, 2 * i + 1)
                split_lo(i + 2)
            for i in ks:
                gate("gb", sig_b, i)
                ve.wait_ge(*vec.at(f"gb{i}"))
                ve.tensor_tensor(merged[:, i, :], merged[:, i, :], sig_b[:, i, :], ALU.add).then_inc(*vec(f"m{i}"))
                if i % 2:
                    split_lo(6 + i // 2)
            for i in ks:
                merged_lo(i)
            ve.wait_ge(rows_in, 32)
            for n in range(4):
                for t in ts:
                    name, at = f"w{t}{n}", slice(256 * n, 256 * n + 256)
                    ve.wait_ge(*pe.at(name))
                    if n or t:
                        ve.wait_ge(*vec.at(f"x_w{t - 1}{n}" if t else f"x_w3{n - 1}"))
                    ve.tensor_tensor(g.gated[:, 0, 0:256], bank[name][:, 0:256], g.mod[:, 0, at], ALU.mult).then_inc(*vec(name))
                    ve.wait_ge(*vec.at(name))
                    ve.tensor_tensor(g.x[:, t, at], g.x[:, t, at], g.gated[:, 0, 0:256], ALU.add).then_inc(*vec(f"x_{name}"))
                    if t == 0 and n in (1, 2):
                        split_lo(n + 9)


class Turns:

    def __init__(self, sem, order):
        self.sem, self.place, self.n, self.done = sem, {s: i + 1 for i, s in enumerate(order)}, len(order), 0
        assert len(self.place) == self.n

    def __call__(self, name):
        self.done += 1
        assert self.place[name] == self.done, (name, self.place[name], self.done)
        return self.sem, 1

    def credit(self):
        return self.sem, self.n

    def at(self, name, turn):
        return self.sem, self.n * turn + (self.n + self.place[name])

    def before(self, name, turn):
        return self.sem, self.n * turn + self.place[name]


N_CHUNK, RAW, PARTS = 12, 4, 3
GU, DOWN = 4, 2


def raw_slot(g, c):
    return g.w_raw[:, c % RAW, :].rearrange("p (k n) -> p k n", k=4)


def load_weights(g, sp, c, e):
    if c < 2 * GU:
        half, n, w = c % 2, c // 2, g.a["w_gate_up"]
    else:
        half, n, w = (c - 2 * GU) // 2, c % 2, g.a["w_down"]
    src = w[0][bass.ds(e, 1), 512 * half:512 * half + 512, 512 * n:512 * n + 512]
    sp.dma_start(raw_slot(g, c), src.rearrange("a (k p) n -> p (a k) n", p=P)).then_inc(g.raw_in[c % RAW], 16)


FAR = 100000.0


def phase_route(nc, g):
    with ExitStack() as ctx:
        area = g.w_raw[:, :, :].rearrange("p a n -> p (a n)")
        h2 = area[:, 0:NT * D].rearrange("p (t d) -> p t d", t=NT)
        h2T = area[:, NT * D:2 * NT * D].rearrange("p (k n) -> p k n", k=KD)
        rows = g.acc[:, :, :].rearrange("p a n -> p (a n)")
        rank, maskT, wT = (rows[0:N_EXP, 512 * i:512 * i + 512] for i in range(3))
        block_sum, job_end, oh_lt, twice = (rows[0:64, 1536 + 64 * i:1600 + 64 * i] for i in range(4))
        counts = rows[0:64, 1792:1856]
        choice = rows[:, 2048:2560].rearrange("p (t k e) -> p t k e", t=NT, k=TOP_K)
        chosen = rows[:, 2560:3072].rearrange("p (t k e) -> p t k e", t=NT, k=TOP_K)
        mask = rows[:, 3072:3328].rearrange("p (t a e) -> p t a e", t=NT, a=2)
        weight = rows[:, 3328:3456].rearrange("p (t e) -> p t e", t=NT)
        logits = rows[:, 3456:3584].rearrange("p (t e) -> p t e", t=NT)
        ss, rstd = rows[:, 3584:3588], rows[:, 3588:3592]
        top = rows[:, 3592:3624].rearrange("p (t k) -> p t k", t=NT)
        idx = rows[:, 3624:3640].rearrange("p (t k) -> p t k", t=NT)
        neg, total, inv = rows[:, 3640:3644], rows[:, 3644:3648], rows[:, 3648:3652]
        ex = rows[:, 3652:3668].rearrange("p (t k) -> p t k", t=NT)
        prob = rows[:, 3668:3684].rearrange("p (t k) -> p t k", t=NT)
        square = g.mod[:, 0, :]
        (g.top_i, g.bias_raw) = g.sb(ctx, top_i=([P, NT, 8], U32), bias_raw=([2 * N_EXP, 2 * D_FF + D], F32))
        ts, ks = range(NT), range(KD)
        pe = g.steps(ctx, "f_pe", names("h{}", KD) + ["lg", "rank", "count", "maskT", "wT", "js", "table", "total"]
                     + names("slot{}", NT) + names("weight{}", NT))
        act = g.steps(ctx, "f_act", names("sq{}", NT) + ["std"] + [f"hi{t}" for t in ts] + names("h{}", KD)[0::2] + names("ex{}", NT))
        vec = g.steps(ctx, "f_vec", ["rstd"] + [x for t in ts for x in (f"g{t}", f"s{t}")] + names("h{}", KD)[1::2] + ["zero", "bias_hi", "bias_lo", "lg"]
                      + names("max{}", NT) + names("mi{}", NT) + ["idx", "neg", "inv", "prob", "choice", "chosen", "mask", "mask2", "weight"]
                      + ["later2a", "later2b", "counts", "b0", "b1", "b2", "b3", "maskT", "wT", "js", "rank", "jg", "je", "lt", "table",
                         "rm", "rf", "tab", "nb"] + names("slot{}", NT) + names("weight{}", NT))
        pool = g.steps(ctx, "f_pool", names("lo{}", NT))
        bias_in = g.sem(ctx, "bias_in")
        block = ctx.enter_context(nc.Block())
        ps = g.ps

        @block.sync
        def _(sp):
            for i in range(2):
                at = slice(N_EXP * i, N_EXP * i + N_EXP)
                sp.dma_start(g.bias_raw[at, 0:2 * D_FF], g.a["b_gate_up"][0]).then_inc(bias_in, 16)
                sp.dma_start(g.bias_raw[at, 2 * D_FF:], g.a["b_down"][0]).then_inc(bias_in, 16)
            sp.wait_ge(*vec.at("tab"))
            sp.wait_ge(*pe.at("lg"))
            sp.wait_ge(*pool.at("lo3"))
            first = sp.value_load(g.table[0:1, 1:2], min_val=0, max_val=N_EXP - 1)
            for c in range(RAW):
                load_weights(g, sp, c, first)

        @block.gpsimd
        def _(po):
            for t in ts:
                po.wait_ge(*act.at(f"hi{t}"))
                po.tensor_tensor(g.h2_lo[:, t, :], h2[:, t, :], g.h2_hi[:, t, :].bitcast(F32), ALU.subtract).then_inc(*pool(f"lo{t}"))

        @block.scalar
        def _(sc):
            for t in ts:
                if t:
                    sc.wait_ge(*act.at(f"sq{t - 1}"))
                sc.activation(square, g.x[:, t, :], ACT.Square, accum_out=ss[:, t:t + 1]).then_inc(*act(f"sq{t}"))
            sc.wait_ge(*act.at("sq3"))
            sc.activation(rstd, ss, ACT.Sqrt, bias=g.eps[:, 0:1], scale=1.0 / D).then_inc(*act("std"))
            for t in ts:
                sc.wait_ge(*vec.at(f"s{t}"))
                sc.copy(g.h2_hi[:, t, :], h2[:, t, :]).then_inc(*act(f"hi{t}"))
            for k in ks[0::2]:
                sc.wait_ge(*pe.at(f"h{k}"))
                sc.copy(h2T[:, k, :], ps[k][:, :]).then_inc(*act(f"h{k}"))
            sc.wait_ge(*vec.at("neg"))
            for t in ts:
                sc.activation(ex[:, t, :], top[:, t, 0:TOP_K], ACT.Exp, bias=neg[:, t:t + 1], accum_out=total[:, t:t + 1]).then_inc(*act(f"ex{t}"))

        @block.tensor
        def _(te):
            for t in ts:
                te.wait_ge(*vec.at(f"s{t}"))
                for k in ks:
                    mm = te.transpose(ps[k][:, P * t:P * t + P], h2[:, t, P * k:P * k + P], g.ident[:, :])
                    if t == NT - 1:
                        mm.then_inc(*pe(f"h{k}"))
            te.wait_ge(*act.at("h6"))
            te.wait_ge(*vec.at("h7"))
            for t in ts:
                for k in ks:
                    mm = te.matmul(ps[0][:, N_EXP * t:N_EXP * t + N_EXP], h2T[:, k, P * t:P * t + P], g.w_router[:, k, :], start=(k == 0), stop=(k == KD - 1))
            mm.then_inc(*pe("lg"))
            te.wait_ge(*vec.at("mask"))
            for t in ts:
                for s in range(t + 1):
                    mm = te.matmul(ps[1][0:N_EXP, P * t:P * t + P], mask[:, s, 0, :], g.later[:, :] if s == t else g.ones[:, :],
                                   start=(s == 0), stop=(s == t))
            mm.then_inc(*pe("rank"))
            te.wait_ge(*vec.at("mask2"))
            for t in ts:
                mm = te.matmul(ps[2][0:64, 0:64], mask[:, t, :, :].rearrange("p a e -> p (a e)"), g.ones[:, 0:64], start=(t == 0), stop=(t == NT - 1))
            mm.then_inc(*pe("count"))
            for t in ts:
                mm = te.transpose(ps[3][0:N_EXP, P * t:P * t + P], mask[:, t, 0, :], g.ident[:, :])
            mm.then_inc(*pe("maskT"))
            te.wait_ge(*vec.at("weight"))
            for t in ts:
                mm = te.transpose(ps[4][0:N_EXP, P * t:P * t + P], weight[:, t, :], g.ident[:, :])
            mm.then_inc(*pe("wT"))
            te.wait_ge(*vec.at("b3"))
            te.wait_ge(*vec.at("later2b"))
            te.matmul(ps[5][0:64, 0:64], twice[0:N_EXP, :], block_sum[0:N_EXP, :], start=True, stop=True).then_inc(*pe("js"))
            te.wait_ge(*vec.at("table"))
            te.matmul(ps[6][0:1, 0:64], g.iota_part[0:N_EXP, 0:1], g.job_of[0:N_EXP, :], start=True, stop=True).then_inc(*pe("table"))
            te.matmul(ps[7][0:1, 0:64], g.ones[0:N_EXP, 0:1], block_sum[0:N_EXP, :], start=True, stop=True).then_inc(*pe("total"))
            te.wait_ge(*vec.at("rf"))
            te.wait_ge(*vec.at("wT"))
            for x, src, banks in (("slot", rank, (0, 1, 2, 3)), ("weight", wT, (4, 5, 0, 1))):
                for t in ts:
                    if x == "weight" and t >= 2:
                        te.wait_ge(*vec.at(f"slot{t - 2}"))
                    te.matmul(ps[banks[t]][:, 0:64], src[:, P * t:P * t + P], g.job_of[0:N_EXP, :], start=True, stop=True).then_inc(*pe(f"{x}{t}"))

        @block.vector
        def _(ve):
            def then(ins, name):
                ins.then_inc(*vec(name))
                ve.wait_ge(*vec.at(name))

            ve.wait_ge(*act.at("std"))
            then(ve.reciprocal(rstd, rstd), "rstd")
            for t in ts:
                then(ve.scalar_tensor_tensor(h2[:, t, :], g.x[:, t, :], rstd[:, t:t + 1], g.mod[:, 2, :], ALU.mult, ALU.mult), f"g{t}")
                ve.tensor_tensor(h2[:, t, :], h2[:, t, :], g.mod[:, 1, :], ALU.add).then_inc(*vec(f"s{t}"))
            for k in ks[1::2]:
                ve.wait_ge(*pe.at(f"h{k}"))
                ve.tensor_copy(h2T[:, k, :], ps[k][:, :]).then_inc(*vec(f"h{k}"))
            ve.memset(g.weight_of[:, :, 0:1], 0.0).then_inc(*vec("zero"))
            ve.wait_ge(bias_in, 16 * 4)
            then(ve.tensor_copy(g.bias[:, :], g.bias_raw[:, :]), "bias_hi")
            ve.tensor_tensor(g.bias[N_EXP:2 * N_EXP, :], g.bias_raw[N_EXP:2 * N_EXP, :], g.bias[N_EXP:2 * N_EXP, :].bitcast(F32), ALU.subtract).then_inc(*vec("bias_lo"))
            ve.wait_ge(*pe.at("lg"))
            then(ve.tensor_tensor(logits, ps[0][:, 0:N_EXP * NT].rearrange("p (t e) -> p t e", t=NT),
                                  g.b_router[:, :].unsqueeze(1).broadcast_to([P, NT, N_EXP]), ALU.add), "lg")
            for t in ts:
                ve.max(top[:, t, :], logits[:, t, :]).then_inc(*vec(f"max{t}"))
            ve.wait_ge(*vec.at("max3"))
            for t in ts:
                ve.max_index(g.top_i[:, t, :], top[:, t, :], logits[:, t, :]).then_inc(*vec(f"mi{t}"))
            ve.wait_ge(*vec.at("mi3"))
            ve.tensor_copy(idx, g.top_i[:, :, 0:TOP_K]).then_inc(*vec("idx"))
            ve.tensor_scalar(neg, top[:, :, 0], -1.0, None, ALU.mult).then_inc(*vec("neg"))
            ve.wait_ge(*act.at("ex3"))
            then(ve.reciprocal(inv, total), "inv")
            then(ve.tensor_tensor(prob, ex, inv.unsqueeze(2).broadcast_to([P, NT, TOP_K]), ALU.mult), "prob")
            experts = g.iota_row[:, 0:N_EXP].unsqueeze(1).unsqueeze(1).broadcast_to([P, NT, TOP_K, N_EXP])
            wide = lambda x: x.unsqueeze(3).broadcast_to([P, NT, TOP_K, N_EXP])
            then(ve.tensor_tensor(choice, experts, wide(idx), ALU.is_equal), "choice")
            ve.tensor_tensor(chosen, choice, wide(prob), ALU.mult).then_inc(*vec("chosen"))
            then(ve.tensor_reduce(mask[:, :, 0, :], choice.rearrange("p t k e -> p t e k"), AX_X, ALU.add), "mask")
            ve.tensor_copy(mask[:, :, 1, :], mask[:, :, 0, :]).then_inc(*vec("mask2"))
            ve.tensor_reduce(weight, chosen.rearrange("p t k e -> p t e k"), AX_X, ALU.add).then_inc(*vec("weight"))
            ve.tensor_copy(twice[0:N_EXP, 0:N_EXP], g.later[0:N_EXP, 0:N_EXP]).then_inc(*vec("later2a"))
            ve.tensor_copy(twice[0:N_EXP, N_EXP:64], g.later[0:N_EXP, 0:N_EXP]).then_inc(*vec("later2b"))
            ve.wait_ge(*pe.at("count"))
            then(ve.tensor_copy(counts, ps[2][0:64, 0:64]), "counts")
            then(ve.tensor_scalar(block_sum, counts, 0.0, None, ALU.is_gt), "b0")
            for i in range(1, NT):
                then(ve.scalar_tensor_tensor(block_sum, counts, float(P * i), block_sum, ALU.is_gt, ALU.add), f"b{i}")
            ve.wait_ge(*pe.at("maskT"))
            ve.tensor_copy(maskT, ps[3][0:N_EXP, :]).then_inc(*vec("maskT"))
            ve.wait_ge(*pe.at("wT"))
            ve.tensor_copy(wT, ps[4][0:N_EXP, :]).then_inc(*vec("wT"))
            ve.wait_ge(*pe.at("js"))
            then(ve.tensor_copy(job_end, ps[5][0:64, 0:64]), "js")
            ve.wait_ge(*pe.at("rank"))
            ve.scalar_tensor_tensor(rank, job_end[0:N_EXP, 0:1].broadcast_to([N_EXP, SEQ]), float(P), ps[1][0:N_EXP, :], ALU.mult, ALU.add).then_inc(*vec("rank"))
            jobs = g.iota_row[0:64, 0:JOBS]
            then(ve.tensor_tensor(oh_lt, jobs, job_end, ALU.is_ge), "jg")
            then(ve.tensor_tensor(job_end, job_end, block_sum, ALU.add), "je")
            then(ve.tensor_tensor(job_end, jobs, job_end, ALU.is_lt), "lt")
            ve.tensor_tensor(g.job_of[:, :], oh_lt, job_end, ALU.mult).then_inc(*vec("table"))
            then(ve.scalar_tensor_tensor(rank, rank, FAR, maskT, ALU.add, ALU.mult), "rm")
            ve.tensor_scalar(rank, rank, -FAR, None, ALU.add).then_inc(*vec("rf"))
            ve.wait_ge(*pe.at("table"))
            ve.tensor_copy(g.table[0:1, 1:1 + JOBS], ps[6][0:1, 0:JOBS]).then_inc(*vec("tab"))
            ve.wait_ge(*pe.at("total"))
            ve.tensor_copy(g.table[0:1, 0:1], ps[7][0:1, 0:1]).then_inc(*vec("nb"))
            for t in ts:
                ve.wait_ge(*pe.at(f"slot{t}"))
                ve.scalar_tensor_tensor(g.slot_of[:, t, :], g.iota_row[:, 0:JOBS], -float(P), ps[t][:, 0:JOBS], ALU.mult, ALU.add).then_inc(*vec(f"slot{t}"))
            for t, b in zip(ts, (4, 5, 0, 1)):
                ve.wait_ge(*pe.at(f"weight{t}"))
                ve.tensor_copy(g.weight_of[:, t, 1:1 + JOBS], ps[b][:, 0:JOBS]).then_inc(*vec(f"weight{t}"))


MIN_JOBS, MAX_JOBS = SEQ * TOP_K // P, (SEQ * TOP_K + N_EXP * (P - 1)) // P
VEC_ROWS = 3


def phase_experts(nc, g):
    with ExitStack() as ctx:
        split = ([P, PARTS, 4, 512], F32R)
        pair = ([P, KD, P], F32R)
        (g.e_hi, g.e_lo, g.x_hi, g.x_lo, g.a_hi, g.a_lo, g.y_hi, g.y_lo, g.pick, g.pickT, g.bias_pick, g.ident_r) = g.sb(ctx, e_hi=split, e_lo=split, x_hi=pair, x_lo=pair, a_hi=pair, a_lo=pair, y_hi=([P, D], F32R), y_lo=([P, D], F32R),
             pick=([P, NT, P], F32R), pickT=([P, SEQ], F32R), bias_pick=([2 * N_EXP, P], F32R), ident_r=([P, P], F32R))
        ts = range(NT)
        act_out = g.mod[:, 0, :]
        x_slot = act_out
        gate_c, up_c, sig = (g.mod[:, 1 + i // 2, 512 * (i % 2):512 * (i % 2) + 512].rearrange("p (a n) -> p a n", a=2) for i in range(3))
        ps = g.ps
        pe = Turns(g.sem(ctx, "m_pe"), ["w0", "w1", "cb0", "cb1", "w2", "w3", "cb2", "cb3", "tr0", "w4", "w5", "cb4", "cb5", "tr1", "w6", "w7",
                                        "cb6", "cb7", "tr2", "w8", "st", "w9", "tr3", "ga0", "ga1", "w10", "xt0", "xt1", "w11"])
        act = Turns(g.sem(ctx, "m_act"), ["h2", "h3", "h4", "sg0", "h5", "h6", "th0", "sg1", "h7", "h8", "th1", "sg2", "h9", "h10", "th2", "sg3",
                                          "h11", "st", "th3", "h0", "gx0", "gx1", "y0", "xh0", "xh1", "h1", "y1"])
        vec = Turns(g.sem(ctx, "m_vec"), ["gc0", "uc0", "ad0", "ad1", "m0", "ac0", "gc1", "uc1", "ad2", "ad3", "tl0", "m1", "ac1",
                                          "gc2", "uc2", "ad4", "ad5", "tl1", "m2", "ac2", "gc3", "uc3", "ad6", "ad7", "tl2", "m3", "ac3",
                                          "pick0", "pick1", "pick2", "pick3", "bp", "tl3", "y0", "xl0", "xl1", "y1"])
        order = list(range(2, N_CHUNK)) + [0, 1]
        split_done = [g.sem(ctx, f"split_done{i}") for i in range(PARTS)]
        raw_in = g.raw_in
        first_pe = g.steps(ctx, "first_pe", ["ga0", "ga1", "xt0", "xt1"])
        first_act = g.steps(ctx, "first_act", ["h0", "h1", "gx0", "gx1", "xh0"])
        first_vec = g.steps(ctx, "first_vec", names("pick{}", 4) + ["ident", "bp", "xl0"])
        first_pool = g.steps(ctx, "first_pool", names("zero{}", 4))
        last_pe = g.steps(ctx, "last_pe", names("cb{}", 8))
        last_vec = g.steps(ctx, "last_vec", [x for t in ts for x in (f"ad{2 * t}", f"ad{2 * t + 1}", f"gate{t}")])
        last_pool = g.steps(ctx, "last_pool", names("out{}", NT))
        out_done = g.sem(ctx, "out_done")
        block = ctx.enter_context(nc.Block())

        def job_count(eng):
            return eng.value_load(g.table[0:1, 0:1], min_val=MIN_JOBS, max_val=MAX_JOBS)

        def raw(c):
            return raw_slot(g, c)

        def loaded(c, turn):
            return raw_in[c % RAW], 48 * turn + 16 * (c // RAW + 1 + (3 if c < 2 else 0))

        def is_split(c, turn):
            return split_done[c % PARTS], 8 * turn + 2 * (c // PARTS + 1)

        def slot_left(c, turn):
            n = (c - PARTS) % N_CHUNK
            return pe.before(f"w{n}", turn) if c == 2 else pe.at(f"w{n}", turn)

        def lo_part(eng, c, rows):
            return eng.tensor_tensor(g.e_lo[:, c % PARTS, rows, :], raw(c)[:, rows, :], g.e_hi[:, c % PARTS, rows, :].bitcast(F32), ALU.subtract)

        @block.sync
        def _(sp):
            jobs = job_count(sp)
            with sp.Fori(0, jobs) as turn:
                e = sp.value_load(g.table[0:1, bass.ds(turn + 1, 1)], min_val=0, max_val=N_EXP - 1)
                for c in list(range(RAW, N_CHUNK)) + list(range(RAW)):
                    if c == 0:
                        e = sp.value_load(g.table[0:1, bass.ds(turn + 2, 1)], min_val=0, max_val=N_EXP - 1)
                    sp.wait_ge(*is_split((c - RAW) % N_CHUNK, turn))
                    load_weights(g, sp, c, e)
            for c in (2, 3):
                sp.wait_ge(raw_in[c], 48 * jobs + 16)
            for t in ts:
                sp.wait_ge(*last_pool.at(f"out{t}"))
                sp.dma_start(g.out[0, P * t:P * t + P, :], g.acc[:, t, :]).then_inc(out_done, 16)
            sp.wait_ge(out_done, 16 * NT)

        @block.tensor
        def _(te):
            def gather(i):
                for t in ts:
                    for part in (g.h2_hi, g.h2_lo):
                        mm = te.matmul(ps[i][:, :], g.pick[:, t, :], part[:, t, 512 * i:512 * i + 512],
                                       start=(t == 0 and part is g.h2_hi), stop=(t == NT - 1 and part is g.h2_lo))
                return mm

            def features(i):
                for j in range(4):
                    mm = te.transpose(ps[i][:, P * j:P * j + P], x_slot[:, 512 * i + P * j:512 * i + P * j + P], g.ident[:, :])
                return mm

            def product(c, out, hi, lo, k0, bias, stop, turn):
                te.wait_ge(*is_split(c, turn))
                if bias is not None:
                    te.matmul(out, g.bias_pick[:, :], g.bias[:, bias:bias + 512], start=True, stop=False)
                for k in range(4):
                    w_hi, w_lo = g.e_hi[:, c % PARTS, k, :], g.e_lo[:, c % PARTS, k, :]
                    te.matmul(out, hi[:, k0 + k, :], w_hi, start=False, stop=False)
                    te.matmul(out, hi[:, k0 + k, :], w_lo, start=False, stop=False)
                    mm = te.matmul(out, lo[:, k0 + k, :], w_hi, start=False, stop=(stop and k == 3))
                mm.then_inc(*pe(f"w{c}"))

            def scatter(i):
                t, n = i // 2, i % 2
                te.matmul(ps[6 + n][:, :], g.pickT[:, P * t:P * t + P], g.y_hi[:, 512 * n:512 * n + 512], start=True, stop=False)
                return te.matmul(ps[6 + n][:, :], g.pickT[:, P * t:P * t + P], g.y_lo[:, 512 * n:512 * n + 512], start=False, stop=True)

            def turned(n, turn):
                te.wait_ge(*vec.at(f"ac{n}", turn))
                te.wait_ge(*(vec.at(f"tl{n - 2}", turn) if n >= 2 else vec.before(f"tl{n + 2}", turn)))
                for j in range(2):
                    mm = te.transpose(ps[2 + n % 2][:, P * j:P * j + P], act_out[:, 256 * n + P * j:256 * n + P * j + P], g.ident[:, :])
                mm.then_inc(*pe(f"tr{n}"))

            jobs = job_count(te)
            te.wait_ge(*first_vec.at("pick3"))
            for i in range(2):
                gather(i).then_inc(*first_pe(f"ga{i}"))
            for i in range(2):
                te.wait_ge(*first_act.at(f"gx{i}"))
                features(i).then_inc(*first_pe(f"xt{i}"))
            with te.Fori(0, jobs) as turn:
                te.wait_ge(*vec.before("xl1", turn))
                for n in range(GU):
                    out = ps[n % 2][:, :]
                    if n >= 2:
                        te.wait_ge(*vec.at(f"uc{n - 2}", turn))
                    product(2 * n, out, g.x_hi, g.x_lo, 0, 512 * n, False, turn)
                    product(2 * n + 1, out, g.x_hi, g.x_lo, 4, None, True, turn)
                    for i in (2 * n, 2 * n + 1):
                        if i == 0:
                            te.wait_ge(*vec.before("y1", turn))
                            te.wait_ge(*act.before("st", turn))
                        te.wait_ge(*(vec.at(f"ad{i - 2}", turn) if i >= 2 else vec.before(f"ad{i + 6}", turn)))
                        scatter(i).then_inc(*pe(f"cb{i}"))
                    if n:
                        turned(n - 1, turn)
                te.wait_ge(*vec.at("tl1", turn))
                product(8, ps[4][:, :], g.a_hi, g.a_lo, 0, 2 * D_FF, False, turn)
                te.wait_ge(*vec.at("ad6", turn))
                for t in ts:
                    mm = te.matmul(ps[6][:, P * t:P * t + P], g.pick[:, t, :], g.ident_r[:, :], start=True, stop=True)
                mm.then_inc(*pe("st"))
                product(9, ps[5][:, :], g.a_hi, g.a_lo, 0, 2 * D_FF + 512, False, turn)
                turned(3, turn)
                te.wait_ge(*vec.at("pick3", turn))
                for i in range(2):
                    te.wait_ge(*vec.at(f"uc{i + 2}", turn))
                    gather(i).then_inc(*pe(f"ga{i}"))
                te.wait_ge(*vec.at("tl3", turn))
                product(10, ps[4][:, :], g.a_hi, g.a_lo, 4, None, True, turn)
                for i in range(2):
                    te.wait_ge(*act.at(f"gx{i}", turn))
                    features(i).then_inc(*pe(f"xt{i}"))
                product(11, ps[5][:, :], g.a_hi, g.a_lo, 4, None, True, turn)
            te.wait_ge(*vec.before("y1", jobs))
            te.wait_ge(*act.before("st", jobs))
            for i in range(8):
                te.wait_ge(*(last_vec.at(f"ad{i - 2}") if i >= 2 else vec.before(f"ad{i + 6}", jobs)))
                scatter(i).then_inc(*last_pe(f"cb{i}"))

        @block.scalar
        def _(sc):
            def hi_part(c):
                return sc.copy(g.e_hi[:, c % PARTS, :, :], raw(c))

            def gathered(i):
                return sc.copy(x_slot[:, 512 * i:512 * i + 512], ps[i][:, :])

            def features_hi(i):
                return sc.copy(g.x_hi[:, 4 * i:4 * i + 4, :], ps[i][:, :].rearrange("p (k n) -> p k n", k=4))

            jobs = job_count(sc)
            for c in range(2):
                sc.wait_ge(raw_in[c], 16)
                hi_part(c).then_inc(*first_act(f"h{c}"))
            for i in range(2):
                sc.wait_ge(*first_pe.at(f"ga{i}"))
                gathered(i).then_inc(*first_act(f"gx{i}"))
            for i in range(2):
                sc.wait_ge(*first_pe.at(f"xt{i}"))
                features_hi(i).then_inc(*(first_act("xh0") if i == 0 else act.credit()))
            with sc.Fori(0, jobs) as turn:
                def hi(c):
                    sc.wait_ge(*loaded(c, turn))
                    sc.wait_ge(*slot_left(c, turn))
                    hi_part(c).then_inc(*act(f"h{c}"))

                def sigmoid(n):
                    sc.wait_ge(*vec.at(f"gc{n}", turn))
                    sc.activation(sig[:, n % 2, :], gate_c[:, n % 2, :], ACT.Sigmoid, scale=ALPHA).then_inc(*act(f"sg{n}"))

                def turned_hi(n):
                    sc.wait_ge(*pe.at(f"tr{n}", turn))
                    sc.copy(g.a_hi[:, 2 * n:2 * n + 2, :], ps[2 + n % 2][:, 0:2 * P].rearrange("p (k n) -> p k n", k=2)).then_inc(*act(f"th{n}"))

                def down(n):
                    sc.wait_ge(*pe.at(f"w{10 + n}", turn))
                    sc.copy(g.y_hi[:, 512 * n:512 * n + 512], ps[4 + n][:, :]).then_inc(*act(f"y{n}"))

                hi(2)
                hi(3)
                hi(4)
                sigmoid(0)
                hi(5)
                hi(6)
                turned_hi(0)
                sigmoid(1)
                hi(7)
                hi(8)
                turned_hi(1)
                sigmoid(2)
                hi(9)
                hi(10)
                turned_hi(2)
                sigmoid(3)
                hi(11)
                sc.wait_ge(*pe.at("st", turn))
                sc.copy(g.pickT[:, :], ps[6][:, :]).then_inc(*act("st"))
                turned_hi(3)
                hi(0)
                for i in range(2):
                    sc.wait_ge(*pe.at(f"ga{i}", turn))
                    gathered(i).then_inc(*act(f"gx{i}"))
                down(0)
                for i in range(2):
                    sc.wait_ge(*pe.at(f"xt{i}", turn))
                    features_hi(i).then_inc(*act(f"xh{i}"))
                hi(1)
                down(1)

        @block.gpsimd
        def _(po):
            jobs = job_count(po)
            for i, buf in enumerate((g.y_hi[:, :].bitcast(F32), g.y_lo[:, :].bitcast(F32), g.pickT[:, :].bitcast(F32), g.acc[:, :, :])):
                po.memset(buf, 0.0).then_inc(*first_pool(f"zero{i}"))
            for c in range(2):
                po.wait_ge(*first_act.at(f"h{c}"))
                lo_part(po, c, slice(VEC_ROWS, 4)).then_inc(split_done[c % PARTS], 1)
            with po.Fori(0, jobs) as turn:
                for c in order:
                    po.wait_ge(*act.at(f"h{c}", turn))
                    lo_part(po, c, slice(VEC_ROWS, 4)).then_inc(split_done[c % PARTS], 1)
            for t in ts:
                po.wait_ge(*last_vec.at(f"gate{t}"))
                po.tensor_tensor(g.acc[:, t, :], g.acc[:, t, :], g.x[:, t, :], ALU.add).then_inc(*last_pool(f"out{t}"))

        @block.vector
        def _(ve):
            def pick(t, job):
                return ve.tensor_scalar(g.pick[:, t, :], g.iota_row[:, :], g.slot_of[:, t, job], None, ALU.is_equal)

            def bias_pick(job):
                return ve.tensor_scalar(g.bias_pick[:, :], g.ones[0:2 * N_EXP, :], g.job_of[:, job], None, ALU.mult)

            def add(i, column):
                t, n = i // 2, i % 2
                at = g.acc[:, t, 512 * n:512 * n + 512]
                return ve.scalar_tensor_tensor(at, ps[6 + n][:, :], g.weight_of[:, t, column], at, ALU.mult, ALU.add)

            def features_lo(i):
                at = slice(4 * i, 4 * i + 4)
                return ve.tensor_tensor(g.x_lo[:, at, :], ps[i][:, :].rearrange("p (k n) -> p k n", k=4), g.x_hi[:, at, :].bitcast(F32), ALU.subtract)

            jobs = job_count(ve)
            for t in ts:
                pick(t, slice(0, 1)).then_inc(*first_vec(f"pick{t}"))
            ve.memset(g.unused[:, :], 0.0).then_inc(*pe.credit())
            ve.tensor_copy(g.ident_r[:, :], g.ident[:, :]).then_inc(*first_vec("ident"))
            bias_pick(slice(0, 1)).then_inc(*first_vec("bp"))
            for c in range(2):
                ve.wait_ge(*first_act.at(f"h{c}"))
                lo_part(ve, c, slice(0, VEC_ROWS)).then_inc(split_done[c % PARTS], 1)
            for i in range(2):
                ve.wait_ge(*(first_act.at("xh0") if i == 0 else act.credit()))
                if i:
                    ve.wait_ge(*first_pool.at("zero3"))
                features_lo(i).then_inc(*(first_vec("xl0") if i == 0 else vec.credit()))
            with ve.Fori(0, jobs) as turn:
                def lo(c):
                    ve.wait_ge(*act.at(f"h{c}", turn))
                    lo_part(ve, c, slice(0, VEC_ROWS)).then_inc(split_done[c % PARTS], 1)

                def clamp(n):
                    both = ps[n % 2][:, :].rearrange("p (n a) -> p n a", a=2)
                    ve.wait_ge(*pe.at(f"w{2 * n + 1}", turn))
                    ve.wait_ge(*(vec.at(f"ac{n - 2}", turn) if n >= 2 else vec.before(f"ac{n + 2}", turn)))
                    ve.tensor_scalar(gate_c[:, n % 2, :], both[:, :, 0], LIMIT, None, ALU.min).then_inc(*vec(f"gc{n}"))
                    ve.tensor_scalar(up_c[:, n % 2, :], both[:, :, 1], LIMIT, -LIMIT, ALU.min, ALU.max).then_inc(*vec(f"uc{n}"))

                def gated(n):
                    up = up_c[:, n % 2, :]
                    ve.wait_ge(*vec.at(f"uc{n}", turn))
                    ve.scalar_tensor_tensor(up, up, 1.0, gate_c[:, n % 2, :], ALU.add, ALU.mult).then_inc(*vec(f"m{n}"))
                    ve.wait_ge(*vec.at(f"m{n}", turn))
                    ve.wait_ge(*act.at(f"sg{n}", turn))
                    ve.tensor_tensor(act_out[:, 256 * n:256 * n + 256], up, sig[:, n % 2, :], ALU.mult).then_inc(*vec(f"ac{n}"))

                def turned_lo(n):
                    ve.wait_ge(*act.at(f"th{n}", turn))
                    at = slice(2 * n, 2 * n + 2)
                    ve.tensor_tensor(g.a_lo[:, at, :], ps[2 + n % 2][:, 0:2 * P].rearrange("p (k n) -> p k n", k=2),
                                     g.a_hi[:, at, :].bitcast(F32), ALU.subtract).then_inc(*vec(f"tl{n}"))

                def added(i):
                    ve.wait_ge(*pe.at(f"cb{i}", turn))
                    add(i, bass.ds(turn, 1)).then_inc(*vec(f"ad{i}"))

                def down(n):
                    ve.wait_ge(*act.at(f"y{n}", turn))
                    at = slice(512 * n, 512 * n + 512)
                    ve.tensor_tensor(g.y_lo[:, at], ps[4 + n][:, :], g.y_hi[:, at].bitcast(F32), ALU.subtract).then_inc(*vec(f"y{n}"))

                lo(2)
                lo(3)
                clamp(0)
                added(0)
                added(1)
                lo(4)
                gated(0)
                lo(5)
                clamp(1)
                added(2)
                added(3)
                lo(6)
                turned_lo(0)
                gated(1)
                lo(7)
                clamp(2)
                added(4)
                added(5)
                lo(8)
                turned_lo(1)
                gated(2)
                lo(9)
                clamp(3)
                added(6)
                added(7)
                lo(10)
                turned_lo(2)
                gated(3)
                ve.wait_ge(*pe.at("st", turn))
                for t in ts:
                    pick(t, bass.ds(turn + 1, 1)).then_inc(*vec(f"pick{t}"))
                lo(11)
                ve.wait_ge(*pe.at("w9", turn))
                bias_pick(bass.ds(turn + 1, 1)).then_inc(*vec("bp"))
                turned_lo(3)
                lo(0)
                down(0)
                for i in range(2):
                    ve.wait_ge(*act.at(f"xh{i}", turn))
                    features_lo(i).then_inc(*vec(f"xl{i}"))
                lo(1)
                down(1)
            ve.wait_ge(*vec.before("y1", jobs))
            for t in ts:
                for i in (2 * t, 2 * t + 1):
                    ve.wait_ge(*last_pe.at(f"cb{i}"))
                    add(i, bass.ds(jobs, 1)).then_inc(*last_vec(f"ad{i}"))
                ve.wait_ge(*last_vec.at(f"ad{2 * t + 1}"))
                ve.tensor_tensor(g.acc[:, t, :], g.acc[:, t, :], g.mod[:, 3, :], ALU.mult).then_inc(*last_vec(f"gate{t}"))


def decoder_layer(nc, a, out):
    with ExitStack() as ctx:
        g = Space(nc, ctx, a)
        g.out = out
        g.chunks = ring_chunks(a)
        (g.x, g.mod, g.cols, g.eps, g.ones, g.ident, g.head_ones, g.later, g.iota_row, g.iota_part, g.vec1, g.b_router,
         g.w_router) = g.sb(ctx, x=([P, NT, D], F32), mod=([P, 4, D], F32), cols=([P, N_ROWS], F32), eps=([P, 2], F32),
             ones=([P, P], F32), ident=([P, P], F32), head_ones=([P, P], F32), later=([P, P], F32),
             iota_row=([P, P], F32), iota_part=([P, 1], F32), vec1=([P, 1], F32), b_router=([P, N_EXP], F32),
             w_router=([P, KD, N_EXP], F32))
        g.ps = [ctx.enter_context(nc.psum_tensor(f"bank{i}", [P, 512], F32)) for i in range(8)]
        g.small_in, g.eps_ready = g.sem(ctx, "small_in"), g.sem(ctx, "eps_ready")
        g.mod_out = g.sem(ctx, "mod_out")
        g.mod_rows = nc.dram_tensor("mod_rows", (1, 4, D), F32, kind="Internal").ap()
        g.ring_in = [g.sem(ctx, f"ring_in{i}") for i in range(RING)]
        with ExitStack() as mixer:
            (g.ring, g.hT, g.eye64, g.gram_mask, g.causal, g.chunk_mask, g.level_mask, g.by_head, g.from_head, g.qk_w, g.freq, g.pos,
             g.w_lo, g.w_g) = g.sb(
                mixer, ring=([P, RING, 4096], F32), hT=([P, KD, SEQ], F32), eye64=([P, 64], F32), gram_mask=([P, 2, P], F32),
                causal=([P, P], F32), chunk_mask=([P, SEQ], F32), level_mask=([P, 6, P], F32), by_head=([P, FT, HEADS], F32),
                from_head=([HEADS, FT, P], F32), qk_w=([P, 2, QK], F32), freq=([P, HALF], F32), pos=([P, NT], I32),
                w_lo=([P, WIDTH], F32), w_g=([P, WIDTH], F32))
            phase_adaln(nc, g)
            (g.mla_in, g.yT) = g.sb(mixer, mla_in=([P, NT, MLA_IN], F32), yT=([P, FT, SEQ], F32))
            rwkv = mixer.enter_context(ExitStack())
            (g.AR, g.Bt, g.Kt, g.v, g.bv, g.gate, g.w_end) = g.sb(rwkv, AR=([P, FT, NT, 2, P], F32), Bt=([P, FT, SEQ], F32), Kt=([P, FT, SEQ], F32), v=([P, FT, SEQ], F32),
                 bv=([P, FT, SEQ], F32), gate=([P, FT, SEQ], F32), w_end=([P, FT, NCH], F32))
            phase_project(nc, g)

            phase_rwkv(nc, g)
            rwkv.close()
            (g.oT,) = g.sb(mixer, oT=([P, FT, SEQ], F32))
            phase_mla(nc, g)

            phase_output(nc, g)
        with ExitStack() as moe:
            (g.h2_hi, g.h2_lo, g.acc, g.w_raw, g.bias, g.job_of, g.table, g.slot_of, g.weight_of, g.unused) = g.sb(moe, h2_hi=([P, NT, D], F32R), h2_lo=([P, NT, D], F32R), acc=([P, NT, D], F32), w_raw=([P, RAW, 2048], F32),
                 bias=([2 * N_EXP, 2 * D_FF + D], F32R), job_of=([2 * N_EXP, JOBS], F32), table=([1, JOBS + 1], I32), slot_of=([P, NT, JOBS], F32), weight_of=([P, NT, JOBS + 1], F32), unused=([P, 1], F32))
            g.raw_in = [g.sem(moe, f"raw_in{i}") for i in range(RAW)]
            phase_route(nc, g)
            phase_experts(nc, g)


_INS = ["x", "c", "positions", "ada_w", "ada_b", "norm_mix_w", "norm_ffn_w", "w_in",
        "q_a_norm_w", "w_q_up", "kv_a_norm_w", "w_kv_up", "q_norm_w", "k_norm_w", "w_o_mla", "rwkv_mu",
        "rwkv_w0", "rwkv_w2", "rwkv_a0", "rwkv_a2", "rwkv_g2", "rwkv_k_k", "rwkv_k_a", "rwkv_r_k",
        "rwkv_ln_w", "rwkv_ln_b", "rwkv_w_o", "w_out", "w_router", "b_router", "w_gate_up", "b_gate_up",
        "w_down", "b_down"]


def kernel(**inputs):
    import numpy as _np
    import concourse.bacc as _bacc
    from concourse import mybir as _mybir
    from concourse.bass_utils import run_bass_kernel_spmd as _run

    nc = _bacc.Bacc("TRN2", target_bir_lowering=False, num_devices=1)
    given = {name: _np.ascontiguousarray(inputs[name]) for name in _INS}
    given["inv_freq"] = (_np.float32(10000.0) ** (-(_np.arange(HALF, dtype=_np.float32) / _np.float32(HALF))))[None, :]
    arrays = {f"in_{name}_dram": array for name, array in given.items()}
    args = {name: nc.dram_tensor(f"in_{name}_dram", array.shape, _mybir.dt.from_np(array.dtype), kind="ExternalInput").ap()
            for name, array in given.items()}
    out = nc.dram_tensor("out_0_dram", (1, SEQ, D), F32, kind="ExternalOutput").ap()
    decoder_layer(nc, args, out)
    return _run(nc, [arrays], core_ids=[0]).results[0]["out_0_dram"]
```
